# Optimizing a Trainium2 kernel written in Bass

```python
import math
import jax, jax.numpy as jnp
from jax import lax
import numpy as np

D_MODEL = 1024
BATCH = 1
SEQ = 512
DEPTH = 4

CHUNK = 64
Q_BLOCK = 128
N_MIXERS = 3
N_A = (DEPTH + 2) // 3
N_B = (DEPTH + 1) // 3
N_C = DEPTH // 3
DEEPNORM_ALPHA = (2.0 * DEPTH) ** 0.25
DEEPNORM_BETA = (8.0 * DEPTH) ** -0.25
LN_EPS = 1e-5
RMS_EPS = 1e-6
ROPE_BASE = 10000.0

LRU_WIDTH = D_MODEL
LRU_BLOCKS = 4
LRU_BLOCK_W = LRU_WIDTH // LRU_BLOCKS
LRU_CONV_W = 4
LRU_C = 8.0

MLA_HEADS = 16
QK_NOPE = 64
QK_ROPE = 32
V_HEAD = 64
KV_LORA = 256
Q_LORA = 768

RET_HEADS = 4
RET_QK = D_MODEL // RET_HEADS
RET_V = 2 * D_MODEL // RET_HEADS

D_FF = 2816
FFN_CONV_W = 3

kernel_name = "hybrid_rglru_mla_retention_deepnorm"

def layer_norm(x, g, b):
    xf = x.astype(jnp.float32)
    mu = jnp.mean(xf, axis=-1, keepdims=True)
    var = jnp.mean(jnp.square(xf - mu), axis=-1, keepdims=True)
    return (xf - mu) * lax.rsqrt(var + LN_EPS) * g + b

def rms_norm(x, g):
    xf = x.astype(jnp.float32)
    return (xf * lax.rsqrt(jnp.mean(xf * xf, axis=-1, keepdims=True) + RMS_EPS) * g).astype(x.dtype)

def rope(x, positions):
    d = x.shape[-1]
    inv_freq = ROPE_BASE ** (-jnp.arange(0, d, 2, dtype=jnp.float32) / d)
    ang = positions.astype(jnp.float32)[:, :, None, None] * inv_freq
    cos, sin = jnp.cos(ang), jnp.sin(ang)
    xf = x.astype(jnp.float32)
    x1, x2 = xf[..., : d // 2], xf[..., d // 2:]
    return jnp.concatenate([x1 * cos - x2 * sin, x1 * sin + x2 * cos], axis=-1)

def causal_dwconv(x, w, b):
    k_w, c = w.shape
    y = lax.conv_general_dilated(
        x, w.astype(x.dtype)[:, None, :], window_strides=(1,), padding=[(k_w - 1, 0)],
        dimension_numbers=("NWC", "WIO", "NWC"), feature_group_count=c)
    return y + b.astype(x.dtype)

def rglru_mixer(x, w_in, conv_w, conv_b, w_a, b_a, w_x, b_x, lam, w_out):
    bsz, s, _ = x.shape
    proj = x @ w_in
    gate_branch, rnn_in = jnp.split(proj, 2, axis=-1)
    u = causal_dwconv(rnn_in, conv_w, conv_b)
    ub = u.reshape(bsz, s, LRU_BLOCKS, LRU_BLOCK_W)
    r = jax.nn.sigmoid(jnp.einsum("bsgi,gij->bsgj", ub, w_a) + b_a).reshape(bsz, s, LRU_WIDTH)
    i = jax.nn.sigmoid(jnp.einsum("bsgi,gij->bsgj", ub, w_x) + b_x).reshape(bsz, s, LRU_WIDTH)
    log_a = -LRU_C * r.astype(jnp.float32) * jax.nn.softplus(-lam.astype(jnp.float32))
    a = jnp.exp(log_a)
    mult = jnp.sqrt(-jnp.expm1(2.0 * log_a))
    bvals = mult * (i * u).astype(jnp.float32)

    def combine(c1, c2):
        a1, b1 = c1
        a2, b2 = c2
        return a1 * a2, a2 * b1 + b2

    _, h = lax.associative_scan(combine, (a, bvals), axis=1)
    y = jax.nn.gelu(gate_branch) * h.astype(x.dtype)
    return y @ w_out

def chunk_causal_attention(q_nope, q_pe, k_nope, k_pe, v):
    s_len = q_nope.shape[1]
    scale = (QK_NOPE + QK_ROPE) ** -0.5
    outs = []
    for j in range(s_len // Q_BLOCK):
        q0 = j * Q_BLOCK
        kv_len = q0 + Q_BLOCK
        sc = (jnp.einsum("bqhd,bkhd->bhqk", q_nope[:, q0:kv_len], k_nope[:, :kv_len])
              + jnp.einsum("bqhd,bkd->bhqk", q_pe[:, q0:kv_len], k_pe[:, :kv_len]))
        sc = sc.astype(jnp.float32) * scale
        q_chunk = (q0 + jnp.arange(Q_BLOCK)) // CHUNK
        k_chunk = jnp.arange(kv_len) // CHUNK
        mask = k_chunk[None, :] <= q_chunk[:, None]
        sc = jnp.where(mask, sc, -jnp.inf)
        p = jax.nn.softmax(sc, axis=-1).astype(v.dtype)
        outs.append(jnp.einsum("bhqk,bkhd->bqhd", p, v[:, :kv_len]))
    return jnp.concatenate(outs, axis=1)

def mla_mixer(x, positions, w_in, q_norm_g, kv_norm_g, w_uq, w_ukv, w_out):
    bsz, s, _ = x.shape
    proj = x @ w_in
    c_q = proj[..., :Q_LORA]
    c_kv = proj[..., Q_LORA:Q_LORA + KV_LORA]
    k_pe = proj[..., Q_LORA + KV_LORA:]
    q = (rms_norm(c_q, q_norm_g) @ w_uq).reshape(bsz, s, MLA_HEADS, QK_NOPE + QK_ROPE)
    q_nope, q_pe = q[..., :QK_NOPE], q[..., QK_NOPE:]
    q_pe = rope(q_pe, positions).astype(x.dtype)
    k_pe = rope(k_pe[:, :, None, :], positions)[:, :, 0, :].astype(x.dtype)
    kv = (rms_norm(c_kv, kv_norm_g) @ w_ukv).reshape(bsz, s, MLA_HEADS, QK_NOPE + V_HEAD)
    k_nope, v = kv[..., :QK_NOPE], kv[..., QK_NOPE:]
    o = chunk_causal_attention(q_nope, q_pe, k_nope, k_pe, v)
    return o.reshape(bsz, s, MLA_HEADS * V_HEAD) @ w_out

def retention_mixer(x, positions, w_in, gn_g, w_out):
    bsz, s, _ = x.shape
    n_c = s // CHUNK
    hq, hv = RET_HEADS * RET_QK, RET_HEADS * RET_V
    proj = x @ w_in
    q = rope(proj[..., :hq].reshape(bsz, s, RET_HEADS, RET_QK), positions)
    k = rope(proj[..., hq:2 * hq].reshape(bsz, s, RET_HEADS, RET_QK), positions) * (RET_QK ** -0.5)
    v = proj[..., 2 * hq:2 * hq + hv].reshape(bsz, s, RET_HEADS, RET_V).astype(jnp.float32)
    g = proj[..., 2 * hq + hv:]
    qc = q.reshape(bsz, n_c, CHUNK, RET_HEADS, RET_QK)
    kc = k.reshape(bsz, n_c, CHUNK, RET_HEADS, RET_QK)
    vc = v.reshape(bsz, n_c, CHUNK, RET_HEADS, RET_V)
    log_gamma = jnp.log1p(-jnp.exp2(-5.0 - jnp.arange(RET_HEADS, dtype=jnp.float32)))
    idx = jnp.arange(CHUNK, dtype=jnp.float32)
    rel = jnp.abs(idx[:, None] - idx[None, :])
    d_intra = jnp.exp(log_gamma[:, None, None] * rel)
    sc = jnp.einsum("bnqhd,bnkhd->bnhqk", qc, kc) * d_intra
    y_intra = jnp.einsum("bnhqk,bnkhe->bnqhe", sc, vc)
    xi = jnp.exp(log_gamma[None, :] * (idx + 1.0)[:, None])
    zeta = jnp.exp(log_gamma[None, :] * (CHUNK - 1.0 - idx)[:, None])
    chunk_decay = jnp.exp(log_gamma * CHUNK)

    def step(state, inp):
        qn, kn, vn = inp
        y = jnp.einsum("bqhd,bhde->bqhe", qn, state) * xi[None, :, :, None]
        state = state * chunk_decay[None, :, None, None] + jnp.einsum(
            "bkhd,bkhe->bhde", kn * zeta[None, :, :, None], vn)
        return state, y

    state0 = jnp.zeros((bsz, RET_HEADS, RET_QK, RET_V), jnp.float32)
    _, y_inter = lax.scan(step, state0, (jnp.swapaxes(qc, 0, 1), jnp.swapaxes(kc, 0, 1),
                                         jnp.swapaxes(vc, 0, 1)))
    y = (y_intra + jnp.swapaxes(y_inter, 0, 1)).reshape(bsz, s, RET_HEADS, RET_V)
    mu = jnp.mean(y, axis=-1, keepdims=True)
    var = jnp.mean(jnp.square(y - mu), axis=-1, keepdims=True)
    y = ((y - mu) * lax.rsqrt(var + LN_EPS)).reshape(bsz, s, hv) * gn_g
    return (jax.nn.silu(g.astype(jnp.float32)) * y).astype(x.dtype) @ w_out

def conv_gated_ffn(x, w_up, conv_w, conv_b, w_down):
    h = causal_dwconv(x @ w_up, conv_w, conv_b)
    gate, up = jnp.split(h, 2, axis=-1)
    return (jax.nn.gelu(gate) * up) @ w_down

def setup_inputs(seed: int = 0) -> dict:
    key = jax.random.key(seed)
    ks = iter(jax.random.split(key, 64))
    f32 = jnp.float32

    def nrm(shape, scale):
        return scale * jax.random.normal(next(ks), shape, f32)

    def gain(shape):
        return 1.0 + nrm(shape, 0.02)

    W, F, D = LRU_WIDTH, D_FF, D_MODEL
    x = jax.random.normal(next(ks), (BATCH, SEQ, D), f32)
    positions = jnp.broadcast_to(jnp.arange(SEQ, dtype=jnp.int32), (BATCH, SEQ))
    a0 = jax.random.uniform(next(ks), (N_A, W), f32, 0.9, 0.999)
    s0 = a0 ** (1.0 / LRU_C)
    return {
        "x": x,
        "positions": positions,
        "ln1_g": gain((DEPTH, D)), "ln1_b": nrm((DEPTH, D), 0.01),
        "ln2_g": gain((DEPTH, D)), "ln2_b": nrm((DEPTH, D), 0.01),
        "ffn_w_up": nrm((DEPTH, D, 2 * F), D ** -0.5),
        "ffn_conv_w": nrm((DEPTH, FFN_CONV_W, 2 * F), FFN_CONV_W ** -0.5),
        "ffn_conv_b": nrm((DEPTH, 2 * F), 0.01),
        "ffn_w_down": nrm((DEPTH, F, D), DEEPNORM_BETA * F ** -0.5),
        "lru_w_in": nrm((N_A, D, 2 * W), D ** -0.5),
        "lru_conv_w": nrm((N_A, LRU_CONV_W, W), LRU_CONV_W ** -0.5),
        "lru_conv_b": nrm((N_A, W), 0.01),
        "lru_w_a": nrm((N_A, LRU_BLOCKS, LRU_BLOCK_W, LRU_BLOCK_W), LRU_BLOCK_W ** -0.5),
        "lru_b_a": nrm((N_A, LRU_BLOCKS, LRU_BLOCK_W), 0.01),
        "lru_w_x": nrm((N_A, LRU_BLOCKS, LRU_BLOCK_W, LRU_BLOCK_W), LRU_BLOCK_W ** -0.5),
        "lru_b_x": nrm((N_A, LRU_BLOCKS, LRU_BLOCK_W), 0.01),
        "lru_lambda": jnp.log(s0) - jnp.log1p(-s0),
        "lru_w_out": nrm((N_A, W, D), DEEPNORM_BETA * W ** -0.5),
        "mla_w_in": nrm((N_B, D, Q_LORA + KV_LORA + QK_ROPE), D ** -0.5),
        "mla_q_norm": gain((N_B, Q_LORA)),
        "mla_kv_norm": gain((N_B, KV_LORA)),
        "mla_w_uq": nrm((N_B, Q_LORA, MLA_HEADS * (QK_NOPE + QK_ROPE)), Q_LORA ** -0.5),
        "mla_w_ukv": nrm((N_B, KV_LORA, MLA_HEADS * (QK_NOPE + V_HEAD)), KV_LORA ** -0.5),
        "mla_w_out": nrm((N_B, MLA_HEADS * V_HEAD, D), DEEPNORM_BETA * (MLA_HEADS * V_HEAD) ** -0.5),
        "ret_w_in": nrm((N_C, D, 2 * RET_HEADS * RET_QK + 2 * RET_HEADS * RET_V), D ** -0.5),
        "ret_gn_g": gain((N_C, RET_HEADS * RET_V)),
        "ret_w_out": nrm((N_C, RET_HEADS * RET_V, D), DEEPNORM_BETA * (RET_HEADS * RET_V) ** -0.5),
    }

def reference(x, positions, ln1_g, ln1_b, ln2_g, ln2_b, ffn_w_up, ffn_conv_w, ffn_conv_b, ffn_w_down,
              lru_w_in, lru_conv_w, lru_conv_b, lru_w_a, lru_b_a, lru_w_x, lru_b_x, lru_lambda, lru_w_out,
              mla_w_in, mla_q_norm, mla_kv_norm, mla_w_uq, mla_w_ukv, mla_w_out,
              ret_w_in, ret_gn_g, ret_w_out):
    for i in range(DEPTH):
        kind, j = i % N_MIXERS, i // N_MIXERS
        if kind == 0:
            mix = rglru_mixer(x, lru_w_in[j], lru_conv_w[j], lru_conv_b[j], lru_w_a[j], lru_b_a[j],
                              lru_w_x[j], lru_b_x[j], lru_lambda[j], lru_w_out[j])
        elif kind == 1:
            mix = mla_mixer(x, positions, mla_w_in[j], mla_q_norm[j], mla_kv_norm[j],
                            mla_w_uq[j], mla_w_ukv[j], mla_w_out[j])
        else:
            mix = retention_mixer(x, positions, ret_w_in[j], ret_gn_g[j], ret_w_out[j])
        x = layer_norm(DEEPNORM_ALPHA * x + mix.astype(x.dtype), ln1_g[i], ln1_b[i]).astype(x.dtype)
        f = conv_gated_ffn(x, ffn_w_up[i], ffn_conv_w[i], ffn_conv_b[i], ffn_w_down[i])
        x = layer_norm(DEEPNORM_ALPHA * x + f.astype(x.dtype), ln2_g[i], ln2_b[i]).astype(x.dtype)
    return x


_drawn_inputs = setup_inputs


def setup_inputs(seed=0):
    import zlib

    import numpy as np

    out = dict(_drawn_inputs(seed))
    spreads = {}
    factors = {'ffn_conv_b': 8.0,
     'lru_conv_b': 5.145,
     'lru_b_a': 8.0,
     'lru_b_x': 8.0,
     'mla_q_norm': 8.0,
     'mla_kv_norm': 8.0,
     'ret_gn_g': 74.115}
    for name, (base, spread) in spreads.items():
        noise = np.random.default_rng([zlib.crc32(name.encode()), seed]).standard_normal(out[name].shape)
        drawn = base * np.exp(spread * noise) if base else spread * noise
        out[name] = __import__('jax').numpy.asarray(drawn.astype(out[name].dtype))
    for name, factor in factors.items():
        out[name] = (out[name] * factor).astype(out[name].dtype)
    return out
```

```python
from contextlib import ExitStack, contextmanager
import math

import concourse.bass as bass
from concourse import mybir

F32 = mybir.dt.float32
F32R = mybir.dt.float32r
I32 = mybir.dt.int32
ALU = mybir.AluOpType
ACT = mybir.ActivationFunctionType
AX = mybir.AxisListType

P = 128
DEPTH = 4
SEQ = 512
D = 1024
KD = D // P
ALPHA = (2.0 * DEPTH) ** 0.25
LN_EPS = 1e-5
RMS_EPS = 1e-6
TT = SEQ // P

DFF = 2816
NF = DFF // P
LRU_BLOCKS = 4
LRU_C = 8.0

HEADS = 16
NOPE, ROPE, VH = 64, 32, 64
QKH = NOPE + ROPE
Q_LORA, KV_LORA = 768, 256
KQ, KKV = Q_LORA // P, KV_LORA // P
MLA_SCALE = float(QKH) ** -0.5
MASKED = -1e30
CHUNK = 64

RH = 4
RQK, RV = D // RH, 2 * D // RH
EV = RV // P
KR = 2 * D // P

RING = 4
PAD = 3
STATS = 2

PC_LN = 0
PC_LRU = PC_LN + DEPTH * 4 * KD
LRU_COLS = 8 * KD
PC_FFN = PC_LRU + 2 * LRU_COLS
FFN_COLS = 4 * 2 * NF
PC_MLA = PC_FFN + DEPTH * FFN_COLS
PC_RET = PC_MLA + KQ + KKV
PC_RATE = PC_RET + KR
N_PC = PC_RATE + 2 * 2 * KD

ROW_GROUPS = [(4 * DEPTH * KD, PC_LN, [(n, slice(0, DEPTH)) for n in ("ln1_g", "ln1_b", "ln2_g", "ln2_b")])]
for _j in range(2):
    ROW_GROUPS.append((LRU_COLS, PC_LRU + _j * LRU_COLS,
                       [(n, _j) for n in ("lru_conv_w", "lru_conv_b", "lru_b_a", "lru_b_x", "lru_lambda")]))
for _l in range(DEPTH):
    ROW_GROUPS.append((4 * NF, PC_FFN + _l * FFN_COLS, [("ffn_conv_w", (_l, slice(0, 2)))]))
    ROW_GROUPS.append((4 * NF, PC_FFN + _l * FFN_COLS + 4 * NF, [("ffn_conv_w", (_l, slice(2, 3))), ("ffn_conv_b", _l)]))
ROW_GROUPS.append((KQ + KKV + KR, PC_MLA, [("mla_q_norm", 0), ("mla_kv_norm", 0), ("ret_gn_g", 0)]))
N_SMALL = sum(len(v) for _, _, v in ROW_GROUPS) + 1

TWO_PI = 2 * math.pi
ROUND = 1.5 * 2.0 ** 23
PI2_A = 6.28125
PI2_B = round((TWO_PI - PI2_A) * 2.0 ** 20) / 2.0 ** 20
PI2_C = TWO_PI - PI2_A - PI2_B
PI_CLAMP = 3.1415925


class Count:

    def __init__(self, sem, at=0):
        self.sem, self.at, self.roll = sem, at, 0

    def up(self, n=1):
        self.at += n
        return n

    def next(self, n=1):
        self.at += n
        return self.roll + self.at

    def now(self, more=0):
        return self.roll + (self.at + more)


@contextmanager
def loop(eng, times, per):
    first = [c.at for c, _ in per]
    with eng.Fori(0, times) as i:
        for c, n in per:
            c.roll = i * n
        yield i
    for (c, n), at in zip(per, first):
        assert c.at - at == n, (c.sem.name if hasattr(c.sem, "name") else c.sem, c.at - at, n)
        c.at, c.roll = at + times * n, 0


def col(i, n=1):
    return bass.ds(i, n)


def build(nc, a, out, depth=DEPTH):
    with ExitStack() as ctx:
        build_in(nc, a, out, ctx, depth)


def build_in(nc, a, out, ctx, depth):
    def sem(name):
        return ctx.enter_context(nc.semaphore(name))

    def sb(name, shape, dt=F32, on=ctx):
        return on.enter_context(nc.sbuf_tensor(name, shape, dt))

    XH = sb("x_hi", [P, KD, SEQ], F32R)
    XL = sb("x_lo", [P, KD, SEQ], F32R)
    R = sb("residual", [P, KD, SEQ])
    RAW = sb("w_raw", [P, RING, 8, P])
    WH = sb("w_hi", [P, RING, 8, P], F32R)
    WL = sb("w_lo", [P, RING, 8, P], F32R)
    ST = sb("staged", [P, RING, PAD + SEQ])
    PAR = sb("params", [P, N_PC])
    IDENT = sb("ident", [P, P])
    ONES = sb("ones", [P, P])
    FREQ = sb("freq", [P, 4])
    NM = sb("neg_max", [P, TT])
    NMS = sb("neg_max_scaled", [P, TT])
    RSUM = sb("row_sum", [P, TT])
    RINV = sb("row_sum_inv", [P, TT])
    LAM = sb("lambda_exp", [P, 2, KD])
    LAMT = sb("lambda_tmp", [P, 3, 2, KD])
    EPS = sb("rms_eps", [P, 1])
    MROW = sb("mask_row", [1, P + CHUNK])

    def stage(s, lag=0):
        return ST[:, s, PAD - lag:PAD - lag + SEQ]

    with ExitStack() as s:
        XT = sb("x_tokens", [P, TT, D], on=s)
        ROWS = sb("param_rows", [P, 12, P], on=s)
    with ExitStack() as s:
        U = sb("lru_u", [P, KD, SEQ], on=s)
        A = sb("lru_a", [P, KD, SEQ], on=s)
        I = sb("lru_i", [P, KD, SEQ], on=s)
        GATE = sb("lru_gate", [P, KD, SEQ], on=s)
        UH = sb("lru_u_hi", [P, KD, SEQ], F32R, on=s)
        UL = sb("lru_u_lo", [P, KD, SEQ], F32R, on=s)
        YH, YL = UH, UL
    with ExitStack() as s:
        AG = sb("ffn_gate", [P, SEQ], on=s)
        AU = sb("ffn_up", [P, SEQ], on=s)
        AT = sb("ffn_tmp", [P, SEQ], on=s)
        GH = sb("ffn_h_hi", [P, NF, SEQ], F32R, on=s)
        GL = sb("ffn_h_lo", [P, NF, SEQ], F32R, on=s)
    with ExitStack() as s:
        CNH = sb("c_hi", [P, KD, SEQ], F32R, on=s)
        CNL = sb("c_lo", [P, KD, SEQ], F32R, on=s)
        OH = sb("o_hi", [P, KD, SEQ], F32R, on=s)
        OL = sb("o_lo", [P, KD, SEQ], F32R, on=s)
        QB = sb("q_head", [QKH, 2, SEQ], on=s)
        KB = sb("k_head", [QKH, 2, SEQ], on=s)
        PB = sb("probs", [P, 2, SEQ], on=s)
        PT = sb("probs_t", [P, TT, SEQ], on=s)
        MCOS = sb("mla_cos", [P, SEQ], on=s)
        MSIN = sb("mla_sin", [P, SEQ], on=s)
        ROT = sb("mla_rot", [P, SEQ], on=s)
        VB = sb("v_head", [P, 2, TT, VH], on=s)
        MPOS = sb("mla_pos", [P, SEQ], I32, on=s)
    VM = R[:, :, :].rearrange("p a (b c) -> p (a b c)", b=1).rearrange("p (t f) -> p t f", t=TT)
    with ExitStack() as s:
        RYH = sb("ret_y_hi", [P, KR, SEQ], F32R, on=s)
        RYL = sb("ret_y_lo", [P, KR, SEQ], F32R, on=s)
        QT = sb("ret_q", [P, 2, SEQ], on=s)
        KT = sb("ret_k", [P, 2, SEQ], on=s)
        V = sb("ret_v", [P, TT, RV], on=s)
        SD = sb("ret_scores", [P, TT, SEQ], on=s)
        RCOS = sb("ret_cos", [P, SEQ], on=s)
        RSIN = sb("ret_sin", [P, SEQ], on=s)
        RTMP = sb("ret_tmp", [P, SEQ], on=s)
        DEC = sb("decay_table", [P, SEQ], on=s)
    RPOS = DEC[:, :].bitcast(I32)

    SUMS = {
        "lru": (A[:, 0, :], A[:, 1, :], A[:, 2, :]),
        "ffn": (AG[:, :], AU[:, :], AT[:, :]),
        "mla": (PB[:, 0, :], PB[:, 1, :], PT[:, 0, :]),
        "ret": (QT[:, 0, :], QT[:, 1, :], RTMP[:, :]),
    }

    BANK = [ctx.enter_context(nc.psum_tensor(f"bank{i}", [P, SEQ], F32)) for i in range(8)]
    SUMB = BANK[4:6]
    TURN = BANK[6]
    OB = BANK[7]

    s_raw = [sem(f"raw_loaded{i}") for i in range(RING)]
    s_rawk = [sem(f"raw_second_loaded{i}") for i in range(RING)]
    s_small = sem("small_loaded")
    s_xin = sem("x_loaded")
    s_pos = [sem("mla_pos_loaded"), sem("ret_pos_loaded")]
    s_dec = sem("decay_loaded")
    s_const = sem("consts_made")
    s_pads = sem("pads_zeroed")
    s_hi = sem("w_hi_done")
    s_lo = sem("w_lo_done")
    s_panel = sem("panel_done")
    s_evac = sem("evac_done")
    s_ev = sem("staged_used")
    s_act = sem("act_step")
    s_dve = sem("dve_step")
    s_turn = sem("turned")
    s_unturn = sem("turn_read")
    s_lam = sem("lambda_exp")
    s_res = sem("x_new")
    s_xh = sem("x_hi_done")
    s_x = sem("x_ready")
    s_gelu = sem("gelu_done")
    s_g = sem("hidden_ready")
    s_u = sem("u_ready")
    s_iu = sem("iu_done")
    s_ta = sem("decay_done")
    s_mul = sem("mult2_done")
    s_sq = sem("mult_done")
    s_y = sem("y_ready")
    s_sum = sem("sums_ready")
    s_stat = sem("sums_reduced")
    s_mom = sem("moments")
    s_var = sem("variance")
    s_std = sem("deviation")
    s_hin = sem("norm_tile")
    s_hout = sem("norm_tile_hi")
    s_rot = sem("rope_ready")
    s_trig = sem("trig_ready")
    s_cn = sem("latent_ready")
    s_kpe = sem("k_pe_ready")
    s_q = sem("q_ready")
    s_sc = sem("scores_done")
    s_max = sem("max_done")
    s_exp = sem("exp_done")
    s_prob = sem("probs_ready")
    s_o = sem("o_done")
    s_oh = sem("o_hi_done")
    s_ol = sem("o_ready")
    s_sd = sem("decayed_ready")
    s_go = sem("shuffle_may_go")
    s_store = sem("out_stored")

    block = ctx.enter_context(nc.Block())
    KINDS = ["lru", "mla", "ret"]
    layers = [(KINDS[i % 3], i // 3, i) for i in range(depth)]

    @block.sync
    def _(sp):
        n_panel = [0]
        lo = Count(s_lo)

        def slot():
            k = n_panel[0]
            n_panel[0] += 1
            if k >= RING:
                sp.wait_ge(s_lo, lo.next())
            return k % RING

        def panel(src, blocks=8, cols=P):
            s, half = slot(), blocks // 2
            sp.dma_start(RAW[:, s, 0:half, 0:cols], src[:, 0:half]).then_inc(s_raw[s], 16)
            sp.dma_start(RAW[:, s, half:blocks, 0:cols], src[:, half:blocks]).then_inc(s_rawk[s], 16)

        def ks(w):
            return w.rearrange("(c p) m -> p c m", p=P)

        def panels(times, per, load):
            start = 0
            if n_panel[0] == 0:
                load(0)
                start = 1
            if start < times:
                before = n_panel[0]
                at = lo.at
                with sp.Fori(start, times) as i:
                    lo.roll = (i - start) * per
                    load(i)
                assert n_panel[0] - before == per
                n_panel[0] = before + (times - start) * per
                lo.at, lo.roll = at + (times - start) * per, 0

        def lru(j):
            w = ks(a["lru_w_in"][j])

            def four(i, base):
                for u in range(4):
                    panel(w[:, :, col(base + i * (4 * P) + u * P, P)])
            panels(2, 4, lambda i: four(i, D))
            for g in range(LRU_BLOCKS):
                s = slot()
                for n, name in enumerate(("lru_w_a", "lru_w_x")):
                    src = a[name][j, g].rearrange("(k p) (m c) -> p k m c", p=P, c=P)
                    q = (s_raw, s_rawk)[n][s]
                    sp.dma_start(RAW[:, s, 4 * n:4 * n + 4, :].rearrange("p (k m) c -> p k m c", k=2), src).then_inc(q, 16)
            panels(2, 4, lambda i: four(i, 0))
            wo = ks(a["lru_w_out"][j])
            panels(2, 4, lambda i: [panel(wo[:, :, col(i * (4 * P) + u * P, P)]) for u in range(4)])

        def mla(j):
            w = ks(a["mla_w_in"][j])
            panels(2, 4, lambda i: [panel(w[:, :, col(i * (4 * P) + u * P, P)]) for u in range(4)])
            panel(w[:, :, Q_LORA + KV_LORA - NOPE:Q_LORA + KV_LORA + ROPE], 8, QKH)
            wkv = a["mla_w_ukv"][j].rearrange("(k p) (h two c) -> p k h two c", p=P, two=2, c=NOPE)
            for half in range(2):
                s = slot()
                for k in range(KKV):
                    q = (s_raw, s_rawk)[k][s]
                    sp.dma_start(RAW[:, s, 4 * k:4 * k + 4, :].rearrange("p m (t c) -> p (m t) c", c=VH),
                                 wkv[:, k, 8 * half:8 * half + 8, 1, :]).then_inc(q, 16)
            wq = ks(a["mla_w_uq"][j])
            wk = ks(a["mla_w_ukv"][j])

            def head(h):
                s = slot()
                sp.dma_start(RAW[:, s, 0:KQ, 0:QKH], wq[:, :, col(h * QKH, QKH)]).then_inc(s_raw[s], 16)
                sp.dma_start(RAW[:, s, KQ:8, 0:NOPE], wk[:, :, col(h * (2 * NOPE), NOPE)]).then_inc(s_rawk[s], 16)
            panels(HEADS // 4, 4, lambda i: [head(i * 4 + u) for u in range(4)])
            wo = ks(a["mla_w_out"][j])
            panels(2, 4, lambda i: [panel(wo[:, :, col(i * (4 * P) + u * P, P)]) for u in range(4)])

        def ret(j):
            w = ks(a["ret_w_in"][j])

            def head(h):
                for u in range(2):
                    panel(w[:, :, col(h * RQK + u * P, P)])
                for u in range(2):
                    panel(w[:, :, col(h * RQK + (D + u * P), P)])
                for base in (2 * D, 4 * D):
                    for u in range(EV):
                        panel(w[:, :, col(h * RV + (base + u * P), P)])
            panels(RH, 4 + 2 * EV, head)
            wo = ks(a["ret_w_out"][j])

            def four(i):
                for u in range(4):
                    for half in range(2):
                        panel(wo[:, 8 * half:8 * half + 8, col(i * (4 * P) + u * P, P)])
            panels(2, 8, four)

        def ffn(l):
            w = ks(a["ffn_w_up"][l])
            panels(NF // 2, 4, lambda i: [panel(w[:, :, col(i * (2 * P) + (u * P + half * DFF), P)])
                                          for u in range(2) for half in range(2)])
            wo = ks(a["ffn_w_down"][l])

            def four(i):
                for u in range(4):
                    for c0 in range(0, NF, 8):
                        c1 = min(NF, c0 + 8)
                        panel(wo[:, c0:c1, col(i * (4 * P) + u * P, P)], c1 - c0)
            panels(2, 12, four)

        sp.dma_start(XT[:, :, :], a["x"][0].rearrange("(t p) d -> p t d", p=P)).then_inc(s_xin, 16)
        for kind, j, l in layers:
            {"lru": lru, "mla": mla, "ret": ret}[kind](j)
            ffn(l)

    def total_panels():
        n = {"lru": 28, "mla": 35, "ret": 64}
        return sum(n[k] + 2 * NF + 8 * ((NF + 7) // 8) for k, _, _ in layers)

    NPAN = total_panels()

    @block.gpsimd
    def _(pool):
        con = Count(s_const)
        pool.memset(IDENT[:, :], 0.0).then_inc(s_const, con.up())
        pool.memset(ONES[:, :], 1.0).then_inc(s_const, con.up())
        pool.memset(MROW[:, 0:CHUNK], 1.0).then_inc(s_const, con.up())
        pool.memset(MROW[:, CHUNK:P], 0.0).then_inc(s_const, con.up())
        pool.memset(MROW[:, P:P + CHUNK], MASKED).then_inc(s_const, con.up())
        pool.wait_ge(s_const, con.now())
        pool.affine_select(out=IDENT[:, :], in_=IDENT[:, :], compare_op=ALU.not_equal, fill=1.0,
                                    base=0, pattern=[[-1, P]], channel_multiplier=1).then_inc(s_const, con.up())
        hi, lo = Count(s_hi), Count(s_lo)

        def part(s):
            pool.wait_ge(s_hi, hi.next())
            pool.tensor_tensor(WL[:, s], RAW[:, s], WH[:, s].bitcast(F32), ALU.subtract).then_inc(s_lo, lo.up())
        with loop(pool, NPAN // RING, [(hi, RING), (lo, RING)]):
            for s in range(RING):
                part(s)
        for s in range(NPAN % RING):
            part(s)

    @block.tensor
    def _(pe):
        lo, panel_c, bank = Count(s_lo), Count(s_panel), Count(s_evac)
        xr, turn, unturn = Count(s_x), Count(s_turn), Count(s_unturn)
        stat, sums, yr = Count(s_stat), Count(s_sum), Count(s_y)
        q, sc, exp_c, prob = Count(s_q), Count(s_sc), Count(s_exp), Count(s_prob)
        o, ol, sd = Count(s_o), Count(s_ol), Count(s_sd)
        x_at = [0]

        def take_panel():
            s = lo.at % RING
            pe.wait_ge(s_lo, lo.next())
            return s

        def take_bank():
            b = BANK[bank.at % RING]
            pe.wait_ge(s_evac, bank.next())
            return b

        def product(ps, s, c, m, xh, xl, first, last):
            pe.matmul(ps, WL[:, s, c, 0:m], xh, start=first, stop=False)
            pe.matmul(ps, WH[:, s, c, 0:m], xl, start=False, stop=False)
            return pe.matmul(ps, WH[:, s, c, 0:m], xh, start=False, stop=last)

        def tile(xh, xl, blocks, m=P, ready=None):
            b = take_bank()
            for c in range(blocks):
                if c % 8 == 0:
                    s = take_panel()
                if ready is not None:
                    ready(c)
                last = product(b[0:m, :], s, c % 8, m, xh[:, c, :], xl[:, c, :], c == 0, c == blocks - 1)
                if c % 8 == 7 or c == blocks - 1:
                    last.then_inc(s_panel, panel_c.up())

        def x_ready(c):
            pe.wait_ge(s_x, x_at[0] - KD + c + 1)

        def x_tiles(times, each):
            with loop(pe, times, [(lo, each), (bank, each), (panel_c, each)]):
                for u in range(each):
                    tile(XH, XL, KD, ready=x_ready if u == 0 else None)

        def out_tiles(xh, xl, blocks, ready):
            n = 4 * ((blocks + 7) // 8)
            with loop(pe, 2, [(lo, n), (bank, 4), (panel_c, n)]):
                for u in range(4):
                    tile(xh, xl, blocks, ready=ready if u == 0 else None)

        def reduce_sums(s1, s2, n):
            pe.wait_ge(s_sum, sums.next(n))
            pe.matmul(SUMB[0][:, :], ONES[:, :], s1, start=True, stop=True)
            pe.matmul(SUMB[1][:, :], ONES[:, :], s2, start=True, stop=True).then_inc(s_stat, stat.up())

        def norm(kind):
            reduce_sums(SUMS[kind][0], SUMS[kind][1], KD)
            x_at[0] += KD

        def take_turn():
            pe.wait_ge(s_unturn, unturn.next())

        pe.wait_ge(s_const, 6)
        pe.wait_ge(s_small, 16 * N_SMALL)
        for n, (rows, _, _) in enumerate(ROW_GROUPS):
            b = take_bank()
            pe.transpose(b[:, 0:rows], ROWS[0:rows, n, :], IDENT[0:rows, 0:rows]).then_inc(s_turn, turn.up())
        pe.wait_ge(s_xin, 16)
        for m in range(KD):
            b = take_bank()
            for t in range(TT):
                ins = pe.transpose(b[:, t * P:(t + 1) * P], XT[:, t, m * P:(m + 1) * P], IDENT[:, :])
            ins.then_inc(s_turn, turn.up())
        x_at[0] += KD

        def lru():
            x_tiles(2, 4)
            for g in range(LRU_BLOCKS):
                pe.wait_ge(s_u, lru_u[0] + 2 * g + 2)
                s = take_panel()
                for n in range(4):
                    b = take_bank()
                    for k in range(2):
                        c = 4 * (n // 2) + 2 * k + n % 2
                        last = product(b[:, :], s, c, P, UH[:, 2 * g + k, :], UL[:, 2 * g + k, :], k == 0, k == 1)
                last.then_inc(s_panel, panel_c.up())
            lru_u[0] += KD
            x_tiles(2, 4)
            base = yr.at
            out_tiles(YH, YL, KD, lambda c: pe.wait_ge(s_y, base + c + 1))
            yr.at += KD
            norm("lru")
        lru_u = [0]

        def ffn():
            x_tiles(NF // 2, 4)
            base = hid[0]
            out_tiles(GH, GL, NF, lambda c: pe.wait_ge(s_g, base + c + 1))
            hid[0] += NF
            norm("ffn")
        hid = [0]

        def mla():
            x_tiles(2, 4)
            tile(XH, XL, KD, QKH)
            reduce_sums(PB[:, 0, :], PB[:, 1, :], KD)
            pe.wait_ge(s_cn, KD)
            for half in range(2):
                s = take_panel()
                for m in range(4):
                    b = take_bank()
                    for k in range(KKV):
                        last = product(b[:, :], s, 4 * k + m, P, CNH[:, KQ + k, :], CNL[:, KQ + k, :], k == 0, k == KKV - 1)
                last.then_inc(s_panel, panel_c.up())
                for m in range(4):
                    pe.wait_ge(s_evac, RING + bank.at - 3 + m)
                    take_turn()
                    for t in range(TT):
                        ins = pe.transpose(TURN[:, t * P:(t + 1) * P], PB[:, m % 2, t * P:(t + 1) * P], IDENT[:, :])
                    ins.then_inc(s_turn, turn.up())
            pe.wait_ge(s_kpe, 1)
            with loop(pe, HEADS // 4, [(lo, 4), (bank, 8), (panel_c, 4), (q, 4), (sc, 16), (exp_c, 16),
                                       (prob, 16), (turn, 16), (unturn, 16), (o, 2), (ol, 2)]):
                for u in range(4):
                    s = take_panel()
                    b = take_bank()
                    for c in range(KQ):
                        product(b[0:QKH, :], s, c, QKH, CNH[:, c, :], CNL[:, c, :], c == 0, c == KQ - 1)
                    b = take_bank()
                    for k in range(KKV):
                        last = product(b[0:NOPE, :], s, KQ + k, NOPE, CNH[:, KQ + k, :], CNL[:, KQ + k, :],
                                       k == 0, k == KKV - 1)
                    last.then_inc(s_panel, panel_c.up())
                    pe.wait_ge(s_evac, bank.now(RING))
                    pe.wait_ge(s_q, q.next())
                    for qt in range(TT):
                        kv = (qt + 1) * P
                        b = SUMB[qt % 2]
                        pe.wait_ge(s_exp, exp_c.next())
                        pe.matmul(b[:, 0:kv], QB[:, u % 2, qt * P:(qt + 1) * P], KB[:, u % 2, 0:kv], start=True, stop=False)
                        pe.matmul(b[:, kv - CHUNK:kv], MROW[0:1, 0:P], MROW[0:1, P:P + CHUNK], start=False, stop=True).then_inc(s_sc, sc.up())
                    for qt in range(TT):
                        pe.wait_ge(s_prob, prob.next())
                        take_turn()
                        for kt in range(qt + 1):
                            ins = pe.transpose(TURN[:, kt * P:(kt + 1) * P], PB[:, qt % 2, kt * P:(kt + 1) * P], IDENT[:, :])
                        ins.then_inc(s_turn, turn.up())
                    pe.wait_ge(s_unturn, unturn.now(1))
                    if u % 2 == 0:
                        pe.wait_ge(s_ol, ol.next())
                    r0 = VH * (u % 2)
                    for kt in range(TT):
                        ins = pe.matmul(OB[r0:r0 + VH, kt * P:SEQ], VB[:, u % 2, kt, :], PT[:, kt, kt * P:SEQ],
                                        start=kt == 0, stop=kt == TT - 1)
                    if u % 2 == 1:
                        ins.then_inc(s_o, o.up())
            out_tiles(OH, OL, KD, lambda c: pe.wait_ge(s_ol, 1 + c + 1))
            norm("mla")

        def ret():
            n = 4 + 2 * EV

            def turn_v(j):
                pe.wait_ge(s_evac, bank.roll + (RING + bank.at - 1))
                take_turn()
                for t in range(TT):
                    ins = pe.transpose(TURN[:, t * P:(t + 1) * P], R[:, j, t * P:(t + 1) * P], IDENT[:, :])
                ins.then_inc(s_turn, turn.up())
            with loop(pe, RH, [(lo, n), (bank, n + EV), (panel_c, n), (turn, EV), (unturn, EV), (q, 2),
                               (sd, TT), (sc, TT), (o, EV), (sums, EV), (stat, 1)]):
                for u in range(4):
                    tile(XH, XL, KD, ready=x_ready if u == 0 else None)
                tile(XH, XL, KD)
                for j in range(1, EV):
                    tile(XH, XL, KD)
                    turn_v(j - 1)
                tile(XH, XL, KD)
                turn_v(EV - 1)
                pe.wait_ge(s_q, q.next(2))
                for kt in range(TT):
                    b = SUMB[kt % 2]
                    pe.wait_ge(s_sd, sd.next())
                    for c in range(2):
                        ins = pe.matmul(b[:, 0:SEQ - kt * P], KT[:, c, kt * P:(kt + 1) * P], QT[:, c, kt * P:SEQ],
                                        start=c == 0, stop=c == 1)
                    ins.then_inc(s_sc, sc.up())
                for _ in range(EV - 1):
                    tile(XH, XL, KD)
                pe.wait_ge(s_unturn, unturn.now(1))
                pe.wait_ge(s_sd, sd.now(2))
                for j in range(EV):
                    b = take_bank()
                    for kt in range(TT):
                        ins = pe.matmul(b[:, kt * P:SEQ], V[:, kt, j * P:(j + 1) * P], SD[:, kt, kt * P:SEQ],
                                        start=kt == 0, stop=kt == TT - 1)
                    ins.then_inc(s_o, o.up())
                reduce_sums(QT[:, 0, :], QT[:, 1, :], EV)
            base = yr.at
            out_tiles(RYH, RYL, KR, lambda c: pe.wait_ge(s_y, base + c + 1))
            yr.at += KR
            norm("ret")

        for kind, j, l in layers:
            {"lru": lru, "mla": mla, "ret": ret}[kind]()
            ffn()
        pe.wait_ge(s_res, x_at[0] - KD)
        for t in range(TT):
            for half in range(2):
                b = take_bank()
                for m in range(4):
                    ins = pe.transpose(b[:, m * P:(m + 1) * P], R[:, 4 * half + m, t * P:(t + 1) * P], IDENT[:, :])
                ins.then_inc(s_turn, turn.up())

    @block.scalar
    def _(act):
        hi, panel_c, evac, ev = Count(s_hi), Count(s_panel), Count(s_evac, RING), Count(s_ev)
        raw = [Count(q) for q in s_raw + s_rawk]
        step, res, xh = Count(s_act), Count(s_res), Count(s_xh)
        turn, unturn = Count(s_turn), Count(s_unturn, 1)
        stat, mom, var, std = Count(s_stat), Count(s_mom), Count(s_var), Count(s_std)
        hin, hout, gelu = Count(s_hin), Count(s_hout), Count(s_gelu)
        iu, ta, mul, sq, yr = Count(s_iu), Count(s_ta), Count(s_mul), Count(s_sq), Count(s_y)
        rot, trig, dec = Count(s_rot), Count(s_trig), Count(s_dec)
        q, mx, exp_c, o, oh = Count(s_q), Count(s_max), Count(s_exp, 2), Count(s_o), Count(s_oh)
        sd = Count(s_sd, 2)
        act.sem_inc(s_evac, RING)
        act.sem_inc(s_unturn, 1)
        act.sem_inc(s_exp, 2)

        def split():
            if hi.at == NPAN:
                return
            s = hi.at % RING
            act.wait_ge(s_raw[s], raw[s].next(16))
            act.wait_ge(s_rawk[s], raw[RING + s].next(16))
            act.activation(WH[:, s], RAW[:, s], ACT.Copy).then_inc(s_hi, hi.up())

        def panels_per(n):
            return [(hi, n), (panel_c, n)] + [(c, 16 * n // RING) for c in raw]

        def used(*evacs):
            act.wait_ge(s_panel, panel_c.next())
            for e in evacs:
                e().then_inc(s_evac, evac.up())
            split()

        def to_stage():
            b, s = BANK[(evac.at - RING) % RING], ev.at % RING
            act.wait_ge(s_ev, ev.next())
            return act.activation(stage(s), b[:, :], ACT.Copy)

        def now(rows=slice(0, P)):
            return BANK[(evac.at - RING) % RING][rows, :]

        def par(c):
            return PAR[:, col(c)]

        for n, (rows, _, vectors) in enumerate(ROW_GROUPS):
            r = 0
            for name, pick in vectors:
                src = a[name][pick] if not isinstance(pick, tuple) else a[name][pick[0], pick[1]]
                dims = len(src.shape)
                names = "abc"[:dims - 1]
                flat = src.rearrange(f"{' '.join(names)} (t p) -> ({' '.join(names)} t) p", p=P) if dims > 1 else \
                    src.rearrange("(t p) -> t p", p=P)
                k = flat.shape[0]
                act.dma_start(ROWS[r:r + k, n, :], flat).then_inc(s_small, 16)
                r += k
            assert r == rows
        act.dma_start(FREQ[:, :], a["rope_freq"]).then_inc(s_small, 16)
        for _ in range(RING):
            split()
        for n, (rows, c0, _) in enumerate(ROW_GROUPS):
            act.wait_ge(s_turn, turn.next())
            act.activation(PAR[:, c0:c0 + rows], now()[:, 0:rows], ACT.Copy).then_inc(s_evac, evac.up())
        act.wait_ge(s_evac, evac.now())
        for j in range(2):
            lam = PC_LRU + j * LRU_COLS + 7 * KD
            act.activation(LAM[:, j, :], PAR[:, lam:lam + KD], ACT.Abs).then_inc(s_act, step.up())
        act.wait_ge(s_act, step.now())
        act.activation(LAM[:, :, :], LAM[:, :, :], ACT.Exp, scale=-1.0).then_inc(s_lam, 1)
        for m in range(KD):
            act.wait_ge(s_turn, turn.next())
            act.activation(XH[:, m], now(), ACT.Copy).then_inc(s_xh, xh.up())
            act.activation(R[:, m], now(), ACT.Copy).then_inc(s_evac, evac.up())

        def moments(n):
            act.wait_ge(s_stat, stat.next())
            act.activation(stage(0), SUMB[0][:, :], ACT.Copy, scale=1.0 / n).then_inc(s_mom, mom.up())
            act.activation(stage(1), SUMB[0][:, :], ACT.Square, scale=1.0 / n).then_inc(s_mom, mom.up())
            act.wait_ge(s_var, var.next())
            act.activation(stage(1), stage(1), ACT.Sqrt).then_inc(s_std, std.up())

        def norm(last=False):
            moments(D)
            for m in range(0 if last else KD):
                act.wait_ge(s_res, res.next())
                act.activation(XH[:, m], R[:, m], ACT.Copy).then_inc(s_xh, xh.up())

        def x_tiles(times, each, e):
            with loop(act, times, panels_per(each) + [(evac, each), (ev, each if e is to_stage else 0)]):
                for _ in range(each):
                    used(e)

        def out_tiles(blocks, peel=False):
            n = (blocks + 7) // 8

            def body():
                for _ in range(4):
                    for _ in range(n - 1):
                        used()
                    used(to_stage)
            if peel:
                body()
                body()
            else:
                with loop(act, 2, panels_per(4 * n) + [(evac, 4), (ev, 4)]):
                    body()

        def lru(j):
            base, rate = PC_LRU + j * LRU_COLS, PC_RATE + j * 2 * KD
            x_tiles(2, 4, to_stage)
            for g in range(LRU_BLOCKS):
                used(*[lambda n=n, m=m: act.activation((A, I)[n][:, 2 * g + m], now(), ACT.Sigmoid,
                                                       bias=par(base + (5 + n) * KD + 2 * g + m))
                       for n in range(2) for m in range(2)])
            for c in range(KD):
                act.wait_ge(s_iu, iu.next())
                act.activation(I[:, c], A[:, c], ACT.Tanh, scale=par(rate + c))
                act.activation(A[:, c], A[:, c], ACT.Exp, scale=par(rate + KD + c)).then_inc(s_ta, ta.up())
            for c in range(KD):
                act.wait_ge(s_mul, mul.next())
                act.activation(I[:, c], I[:, c], ACT.Sqrt).then_inc(s_sq, sq.up())
            for c in range(KD):
                used(lambda: act.activation(GATE[:, c], now(), ACT.Gelu_apprx_tanh))
            yr.at += KD
            out_tiles(KD)
            norm()

        def ffn(last):
            with loop(act, NF // 2, panels_per(4) + [(evac, 4), (ev, 4), (gelu, 2)]):
                for _ in range(2):
                    used(to_stage)
                    used(to_stage)
                    act.wait_ge(s_ev, ev.now(RING - 1))
                    act.activation(AG[:, :], AG[:, :], ACT.Gelu_apprx_tanh).then_inc(s_gelu, gelu.up())
            out_tiles(NF, peel=last)
            norm(last)

        def angles(cos, sin):
            act.wait_ge(s_rot, rot.next())
            act.activation(sin, sin, ACT.Sin).then_inc(s_trig, trig.up())
            act.activation(cos, cos, ACT.Sin).then_inc(s_trig, trig.up())

        def mla():
            act.dma_start(MPOS[:, :], a["positions"].broadcast_to([P, SEQ])).then_inc(s_pos[0], 16)
            angles(MCOS[:, :], MSIN[:, :])
            for m in range(KD):
                used(lambda: act.activation(R[:, m], now(), ACT.Copy))
            used(lambda: act.activation(KB[NOPE:QKH, 0], now(slice(NOPE, QKH)), ACT.Copy))
            act.wait_ge(s_stat, stat.next())
            act.activation(stage(0), SUMB[0][:, :], ACT.Sqrt, scale=1.0 / Q_LORA, bias=EPS[:, 0:1]).then_inc(s_act, step.up())
            act.activation(stage(1), SUMB[1][:, :], ACT.Sqrt, scale=1.0 / KV_LORA, bias=EPS[:, 0:1]).then_inc(s_std, std.up())
            for m in range(KD):
                act.wait_ge(s_hin, hin.next())
                act.activation(CNH[:, m], R[:, m], ACT.Copy).then_inc(s_hout, hout.up())
            for half in range(2):
                act.wait_ge(s_panel, panel_c.next())
                split()
                for m in range(4):
                    act.activation(PB[:, m % 2], now(), ACT.Copy).then_inc(s_evac, evac.up())
                    act.wait_ge(s_turn, turn.next())
                    f = (4 * half + m) * P
                    act.activation(VM[:, :, f:f + P], TURN[:, :].rearrange("p (t f) -> p t f", t=TT), ACT.Copy).then_inc(s_unturn, unturn.up())
            with loop(act, HEADS // 4, panels_per(4) + [(evac, 8), (mx, 16), (exp_c, 16), (turn, 16), (unturn, 16),
                                                       (o, 2), (oh, 2)]) as i:
                for u in range(4):
                    used(lambda: act.activation(QB[:, u % 2], now(slice(0, QKH)), ACT.Copy),
                         lambda: act.activation(KB[0:NOPE, u % 2], now(slice(0, NOPE)), ACT.Copy))

                    def soft(qt):
                        kv = (qt + 1) * P
                        act.wait_ge(s_max, mx.next())
                        act.activation(PB[:, qt % 2, 0:kv], SUMB[qt % 2][:, 0:kv], ACT.Exp, scale=MLA_SCALE,
                                                  bias=NMS[:, qt:qt + 1], accum_out=RSUM[:, qt:qt + 1]).then_inc(s_exp, exp_c.up())

                    def turned(qt):
                        act.wait_ge(s_turn, turn.next())
                        act.activation(PT[:, 0:qt + 1, qt * P:(qt + 1) * P],
                                                   TURN[:, 0:(qt + 1) * P].rearrange("p (k q) -> p k q", q=P), ACT.Copy).then_inc(s_unturn, unturn.up())
                    soft(0)
                    soft(1)
                    turned(0)
                    soft(2)
                    turned(1)
                    soft(3)
                    turned(2)
                    turned(3)
                    if u % 2 == 1:
                        act.wait_ge(s_o, o.next())
                        act.activation(OH[:, col(i * 2 + u // 2)].rearrange("p a b -> p (a b)"), OB[:, :], ACT.Copy).then_inc(s_oh, oh.up())
            out_tiles(KD)
            norm()

        def ret():
            act.dma_start(RPOS, a["positions"].broadcast_to([P, SEQ])).then_inc(s_pos[1], 16)
            angles(RCOS[:, :], RSIN[:, :])
            n = 4 + 2 * EV
            with loop(act, RH, panels_per(n) + [(evac, n + EV), (ev, 4), (turn, EV), (unturn, EV), (yr, EV), (o, EV), (dec, 16),
                                                (stat, 1), (mom, 2), (var, 1), (std, 1), (hin, EV), (hout, EV), (sd, TT)]) as i:
                act.wait_ge(s_sd, sd.now())
                act.dma_start(DEC[:, :], a["ret_decay"][col(i)].rearrange("a p q -> (a p) q")).then_inc(s_dec, dec.up(16))
                for _ in range(4):
                    used(to_stage)
                act.wait_ge(s_y, yr.now())

                def place(j):
                    act.wait_ge(s_turn, turn.next())
                    act.activation(V[:, :, j * P:(j + 1) * P], TURN[:, :].rearrange("p (t f) -> p t f", t=TT), ACT.Copy).then_inc(s_unturn, unturn.up())
                for j in range(EV):
                    used(lambda: act.activation(R[:, j], now(), ACT.Copy))
                    if j:
                        place(j - 1)
                used(lambda: act.activation(R[:, EV], now(), ACT.Silu))
                place(EV - 1)
                for j in range(1, EV):
                    used(lambda: act.activation(R[:, EV + j], now(), ACT.Silu))
                for j in range(EV):
                    act.wait_ge(s_o, o.next())
                    act.activation(R[:, j], now(), ACT.Copy).then_inc(s_evac, evac.up())
                moments(RV)
                for j in range(EV):
                    act.wait_ge(s_hin, hin.next())
                    act.activation(RYH[:, col(i * EV + j)].rearrange("p a b -> p (a b)"), R[:, j], ACT.Copy).then_inc(s_hout, hout.up())
                sd.at += TT
                yr.at += EV
            out_tiles(KR)
            norm()

        for kind, j, l in layers:
            if kind == "lru":
                lru(j)
            else:
                (mla if kind == "mla" else ret)()
            ffn(l == depth - 1)
        for t in range(TT):
            for half in range(2):
                act.wait_ge(s_turn, turn.next())
                act.activation(XT[:, t, half * SEQ:(half + 1) * SEQ], now(), ACT.Copy).then_inc(s_evac, evac.up())
            act.wait_ge(s_evac, evac.now())
            act.dma_start(out[0, t * P:(t + 1) * P, :], XT[:, t, :]).then_inc(s_store, 16)
        act.wait_ge(s_store, 16 * TT)

    @block.vector
    def _(dve):
        evac, ev, step = Count(s_evac, RING), Count(s_ev, RING), Count(s_dve)
        res, xh, x, sums = Count(s_res), Count(s_xh), Count(s_x), Count(s_sum)
        mom, var, std, hin, hout = Count(s_mom), Count(s_var), Count(s_std), Count(s_hin), Count(s_hout)
        gelu, g_c, u_c, iu, ta = Count(s_gelu), Count(s_g), Count(s_u), Count(s_iu), Count(s_ta)
        mul, sq, yr, rot, trig = Count(s_mul), Count(s_sq), Count(s_y), Count(s_rot), Count(s_trig)
        cn, kpe, q, sc, mx, exp_c = Count(s_cn), Count(s_kpe), Count(s_q), Count(s_sc), Count(s_max), Count(s_exp, 2)
        prob, oh, ol, sd, dec, unturn = Count(s_prob), Count(s_oh), Count(s_ol, 1), Count(s_sd, 2), Count(s_dec), Count(s_unturn, 1)
        staged = [0]
        dve.sem_inc(s_ev, RING)
        dve.sem_inc(s_ol, 1)
        dve.sem_inc(s_sd, 2)

        def par(c):
            return PAR[:, col(c)]

        def next_stage():
            s = staged[0] % RING
            staged[0] += 1
            return s

        dve.memset(ST[:, :, 0:PAD], 0.0).then_inc(s_dve, step.up())
        dve.wait_ge(s_dve, step.now())
        dve.memset(EPS[:, :], RMS_EPS).then_inc(s_dve, step.up())
        dve.wait_ge(s_dve, step.now())
        dve.wait_ge(s_evac, evac.next(len(ROW_GROUPS)))
        dve.wait_ge(s_lam, 1)
        dve.tensor_scalar(LAMT[:, 0], LAM[:, :, :], 2.0, None, ALU.add).then_inc(s_dve, step.up())
        dve.wait_ge(s_dve, step.now())
        dve.reciprocal(LAMT[:, 0], LAMT[:, 0]).then_inc(s_dve, step.up())
        dve.wait_ge(s_dve, step.now())
        dve.tensor_tensor(LAMT[:, 0], LAMT[:, 0], LAM[:, :, :], ALU.mult).then_inc(s_dve, step.up())
        dve.wait_ge(s_dve, step.now())
        dve.tensor_tensor(LAMT[:, 1], LAMT[:, 0], LAMT[:, 0], ALU.mult).then_inc(s_dve, step.up())
        dve.wait_ge(s_dve, step.now())
        dve.tensor_scalar(LAMT[:, 2], LAMT[:, 1], 1.0 / 19, None, ALU.mult).then_inc(s_dve, step.up())
        dve.wait_ge(s_dve, step.now())
        for k in (17, 15, 13, 11, 9, 7, 5, 3):
            dve.scalar_tensor_tensor(LAMT[:, 2], LAMT[:, 2], 1.0 / k, LAMT[:, 1], ALU.add, ALU.mult).then_inc(s_dve, step.up())
            dve.wait_ge(s_dve, step.now())
        dve.scalar_tensor_tensor(LAMT[:, 2], LAMT[:, 2], 1.0, LAMT[:, 0], ALU.add, ALU.mult).then_inc(s_dve, step.up())
        dve.wait_ge(s_dve, step.now())
        for j in range(2):
            lam, rate = PC_LRU + j * LRU_COLS + 7 * KD, PC_RATE + j * 2 * KD
            dve.tensor_scalar(LAMT[:, 0, j], PAR[:, lam:lam + KD], -1.0, 0.0, ALU.mult, ALU.max).then_inc(s_dve, step.up())
            dve.wait_ge(s_dve, step.now())
            dve.scalar_tensor_tensor(LAMT[:, 0, j], LAMT[:, 2, j], 2.0, LAMT[:, 0, j], ALU.mult, ALU.add).then_inc(s_dve, step.up())
            dve.wait_ge(s_dve, step.now())
            dve.tensor_scalar(PAR[:, rate:rate + KD], LAMT[:, 0, j], LRU_C, None, ALU.mult).then_inc(s_dve, step.up())
            dve.wait_ge(s_dve, step.now())
            dve.tensor_scalar(PAR[:, rate + KD:rate + 2 * KD], LAMT[:, 0, j], -LRU_C, None, ALU.mult).then_inc(s_dve, step.up())
            dve.wait_ge(s_dve, step.now())
        for m in range(KD):
            dve.wait_ge(s_xh, xh.next())
            dve.wait_ge(s_evac, evac.next())
            dve.tensor_tensor(XL[:, m], R[:, m], XH[:, m].bitcast(F32), ALU.subtract).then_inc(s_x, x.up())
            dve.wait_ge(s_x, x.now())

        def add_sums(kind, tile):
            s1, s2, t = SUMS[kind]
            dve.tensor_tensor(s1, s1, tile, ALU.add).then_inc(s_dve, step.up())
            dve.wait_ge(s_dve, step.now())
            dve.tensor_tensor(t, tile, tile, ALU.mult).then_inc(s_dve, step.up())
            dve.wait_ge(s_dve, step.now())
            dve.tensor_tensor(s2, s2, t, ALU.add).then_inc(s_sum, sums.up())
            dve.wait_ge(s_sum, sums.now())

        def clear_sums(kind):
            dve.memset(SUMS[kind][0], 0.0).then_inc(s_dve, step.up())
            dve.wait_ge(s_dve, step.now())
            dve.memset(SUMS[kind][1], 0.0).then_inc(s_dve, step.up())
            dve.wait_ge(s_dve, step.now())

        def inverse_std(n):
            dve.wait_ge(s_mom, mom.next(2))
            dve.scalar_tensor_tensor(stage(1), SUMB[1][:, :], 1.0 / n, stage(1), ALU.mult, ALU.subtract).then_inc(s_dve, step.up())
            dve.wait_ge(s_dve, step.now())
            dve.tensor_scalar(stage(1), stage(1), 0.0, LN_EPS, ALU.max, ALU.add).then_inc(s_var, var.up())
            dve.wait_ge(s_var, var.now())
            dve.wait_ge(s_std, std.next())
            dve.reciprocal(stage(2), stage(1)).then_inc(s_dve, step.up())
            dve.wait_ge(s_dve, step.now())

        def residual(kind, per_step):
            clear_sums(kind)
            with loop(dve, 2, [(evac, 4), (ev, 4), (sums, 4), (step, 4 * per_step)]) as i:
                for u in range(4):
                    m = i * 4 + u

                    def at(t):
                        return t[:, col(m)].rearrange("p a b -> p (a b)")
                    dve.wait_ge(s_evac, evac.next())
                    s = next_stage()
                    if kind in ("mla", "ret"):
                        dve.scalar_tensor_tensor(at(R), at(XH).bitcast(F32), ALPHA, stage(s), ALU.mult, ALU.add).then_inc(s_ev, ev.up())
                        dve.wait_ge(s_ev, ev.now())
                        dve.scalar_tensor_tensor(at(R), at(XL).bitcast(F32), ALPHA, at(R), ALU.mult, ALU.add).then_inc(s_dve, step.up())
                        dve.wait_ge(s_dve, step.now())
                    else:
                        dve.scalar_tensor_tensor(at(R), at(R), ALPHA, stage(s), ALU.mult, ALU.add).then_inc(s_ev, ev.up())
                        dve.wait_ge(s_ev, ev.now())
                    add_sums(kind, at(R))
            staged[0] += 4

        def norm(gain, shift, last=False):
            inverse_std(D)

            def lo(m):
                dve.wait_ge(s_xh, xh.next())
                dve.tensor_tensor(XL[:, m], R[:, m], XH[:, m].bitcast(F32), ALU.subtract).then_inc(s_x, x.up())
                dve.wait_ge(s_x, x.now())
            for m in range(KD):
                dve.tensor_tensor(R[:, m], R[:, m], stage(0), ALU.subtract).then_inc(s_dve, step.up())
                dve.wait_ge(s_dve, step.now())
                dve.tensor_tensor(R[:, m], R[:, m], stage(2), ALU.mult).then_inc(s_dve, step.up())
                dve.wait_ge(s_dve, step.now())
                dve.tensor_scalar(R[:, m], R[:, m], par(gain + m), par(shift + m), ALU.mult, ALU.add).then_inc(s_res, res.up())
                dve.wait_ge(s_res, res.now())
                if m and not last:
                    lo(m - 1)
            if not last:
                lo(KD - 1)

        def lnorm(which, l, last=False):
            c = PC_LN + 2 * which * DEPTH * KD + l * KD
            norm(c, c + DEPTH * KD, last)

        def conv(dst, s, taps, w, b):
            dve.tensor_scalar(dst, stage(s), par(w(0)), par(b), ALU.mult, ALU.add).then_inc(s_dve, step.up())
            dve.wait_ge(s_dve, step.now())
            for lag in range(1, taps):
                done = ev if lag == taps - 1 else step
                dve.scalar_tensor_tensor(dst, stage(s, lag), par(w(lag)), dst, ALU.mult, ALU.add).then_inc(done.sem, done.up())
                dve.wait_ge(done.sem, done.now())

        def lru(j):
            base = PC_LRU + j * LRU_COLS
            for m in range(KD):
                dve.wait_ge(s_evac, evac.next())
                conv(U[:, m], next_stage(), 4, lambda lag: base + (3 - lag) * KD + m, base + 4 * KD + m)
                dve.tensor_copy(UH[:, m], U[:, m]).then_inc(s_dve, step.up())
                dve.wait_ge(s_dve, step.now())
                dve.tensor_tensor(UL[:, m], U[:, m], UH[:, m].bitcast(F32), ALU.subtract).then_inc(s_u, u_c.up())
                dve.wait_ge(s_u, u_c.now())
            for g in range(LRU_BLOCKS):
                dve.wait_ge(s_evac, evac.next(4))
                for c in (2 * g, 2 * g + 1):
                    dve.tensor_tensor(U[:, c], U[:, c], I[:, c], ALU.mult).then_inc(s_iu, iu.up())
                    dve.wait_ge(s_iu, iu.now())
            for c in range(KD):
                dve.wait_ge(s_ta, ta.next())
                dve.tensor_tensor(stage(3), A[:, c], A[:, c], ALU.mult).then_inc(s_dve, step.up())
                dve.wait_ge(s_dve, step.now())
                dve.scalar_tensor_tensor(I[:, c], stage(3), 1.0, I[:, c], ALU.add, ALU.mult).then_inc(s_mul, mul.up())
                dve.wait_ge(s_mul, mul.now())
            for c in range(KD):
                dve.wait_ge(s_sq, sq.next())
                dve.tensor_tensor(I[:, c], I[:, c], U[:, c], ALU.mult).then_inc(s_dve, step.up())
                dve.wait_ge(s_dve, step.now())
                dve.tensor_tensor_scan(U[:, c], A[:, c], I[:, c], 0.0, ALU.mult, ALU.add).then_inc(s_dve, step.up())
                dve.wait_ge(s_dve, step.now())
                dve.wait_ge(s_evac, evac.next())
                dve.tensor_tensor(U[:, c], U[:, c], GATE[:, c], ALU.mult).then_inc(s_dve, step.up())
                dve.wait_ge(s_dve, step.now())
                dve.tensor_copy(YH[:, c], U[:, c]).then_inc(s_dve, step.up())
                dve.wait_ge(s_dve, step.now())
                dve.tensor_tensor(YL[:, c], U[:, c], YH[:, c].bitcast(F32), ALU.subtract).then_inc(s_y, yr.up())
                dve.wait_ge(s_y, yr.now())
            residual("lru", 2)

        def ffn(l, last):
            base = PC_FFN + l * FFN_COLS
            with loop(dve, NF // 2, [(evac, 4), (ev, 4), (gelu, 2), (g_c, 2), (step, 12)]) as i:
                for u in range(2):
                    f = i * 2 + u
                    for half, dst in enumerate((AG, AU)):
                        dve.wait_ge(s_evac, evac.next())
                        conv(dst[:, :], next_stage(), 3, lambda lag: f + (base + (2 - lag) * 2 * NF + half * NF),
                             f + (base + 6 * NF + half * NF))
                    dve.wait_ge(s_gelu, gelu.next())
                    dve.tensor_tensor(AU[:, :], AU[:, :], AG[:, :], ALU.mult).then_inc(s_dve, step.up())
                    dve.wait_ge(s_dve, step.now())
                    gh, gl = (t[:, col(f)].rearrange("p a b -> p (a b)") for t in (GH, GL))
                    dve.tensor_copy(gh, AU[:, :]).then_inc(s_dve, step.up())
                    dve.wait_ge(s_dve, step.now())
                    dve.tensor_tensor(gl, AU[:, :], gh.bitcast(F32), ALU.subtract).then_inc(s_g, g_c.up())
                    dve.wait_ge(s_g, g_c.now())
            residual("ffn", 2)
            lnorm(1, l, last)

        def angles(pos, k, freq, cos, sin, tmp):
            dve.wait_ge(s_pos[k], 16)
            dve.tensor_copy(cos, pos).then_inc(s_dve, step.up())
            dve.wait_ge(s_dve, step.now())
            dve.tensor_scalar(cos, cos, freq, None, ALU.mult).then_inc(s_dve, step.up())
            dve.wait_ge(s_dve, step.now())
            for dst, turn, done in ((sin, 0.0, step), (cos, 0.25, rot)):
                dve.tensor_scalar(tmp, cos, 1 / TWO_PI, turn, ALU.mult, ALU.add).then_inc(s_dve, step.up())
                dve.wait_ge(s_dve, step.now())
                dve.tensor_scalar(tmp, tmp, ROUND, None, ALU.add).then_inc(s_dve, step.up())
                dve.wait_ge(s_dve, step.now())
                dve.tensor_scalar(tmp, tmp, ROUND, None, ALU.subtract).then_inc(s_dve, step.up())
                dve.wait_ge(s_dve, step.now())
                dve.scalar_tensor_tensor(dst, tmp, -PI2_A, cos, ALU.mult, ALU.add).then_inc(s_dve, step.up())
                dve.wait_ge(s_dve, step.now())
                dve.scalar_tensor_tensor(dst, tmp, -PI2_B, dst, ALU.mult, ALU.add).then_inc(s_dve, step.up())
                dve.wait_ge(s_dve, step.now())
                dve.scalar_tensor_tensor(dst, tmp, -PI2_C, dst, ALU.mult, ALU.add).then_inc(s_dve, step.up())
                dve.wait_ge(s_dve, step.now())
                dve.tensor_scalar(dst, dst, turn * TWO_PI, PI_CLAMP, ALU.add, ALU.min).then_inc(s_dve, step.up())
                dve.wait_ge(s_dve, step.now())
                dve.tensor_scalar(dst, dst, -PI_CLAMP, None, ALU.max).then_inc(done.sem, done.up())
                dve.wait_ge(done.sem, done.now())
            dve.wait_ge(s_trig, trig.next(2))

        rows = slice(NOPE, QKH)
        swap = [(r + ROPE // 2) % ROPE for r in range(ROPE)]

        def mla_rope(t, done):
            dve.sem_inc(s_go, 1)
            dve.stream_shuffle(ROT[rows, :], t, swap).then_inc(s_dve, step.up())
            dve.wait_ge(s_dve, step.now())
            dve.tensor_tensor(ROT[rows, :], ROT[rows, :], MSIN[rows, :], ALU.mult).then_inc(s_dve, step.up())
            dve.wait_ge(s_dve, step.now())
            dve.tensor_tensor(t, t, MCOS[rows, :], ALU.mult).then_inc(s_dve, step.up())
            dve.wait_ge(s_dve, step.now())
            dve.tensor_tensor(t, t, ROT[rows, :], ALU.add).then_inc(done.sem, done.up())
            dve.wait_ge(done.sem, done.now())

        def mla():
            angles(MPOS[:, :], 0, FREQ[:, 0:1], MCOS[:, :], MSIN[:, :], ROT[:, :])
            dve.tensor_scalar(MSIN[:, :], MSIN[:, :], FREQ[:, 2:3], None, ALU.mult).then_inc(s_dve, step.up())
            dve.wait_ge(s_dve, step.now())
            clear_sums("mla")
            for m in range(KD):
                dve.wait_ge(s_evac, evac.next())
                acc = PB[:, 0] if m < KQ else PB[:, 1]
                dve.tensor_tensor(PT[:, 0], R[:, m], R[:, m], ALU.mult).then_inc(s_dve, step.up())
                dve.wait_ge(s_dve, step.now())
                dve.tensor_tensor(acc, acc, PT[:, 0], ALU.add).then_inc(s_sum, sums.up())
                dve.wait_ge(s_sum, sums.now())
            dve.wait_ge(s_std, std.next())
            dve.reciprocal(stage(0), stage(0)).then_inc(s_dve, step.up())
            dve.wait_ge(s_dve, step.now())
            dve.reciprocal(stage(1), stage(1)).then_inc(s_dve, step.up())
            dve.wait_ge(s_dve, step.now())

            def lo(m):
                dve.wait_ge(s_hout, hout.next())
                dve.tensor_tensor(CNL[:, m], R[:, m], CNH[:, m].bitcast(F32), ALU.subtract).then_inc(s_cn, cn.up())
                dve.wait_ge(s_cn, cn.now())
            for m in range(KD):
                dve.scalar_tensor_tensor(R[:, m], R[:, m], par(PC_MLA + m), stage(0 if m < KQ else 1), ALU.mult, ALU.mult).then_inc(s_hin, hin.up())
                dve.wait_ge(s_hin, hin.now())
                if m:
                    lo(m - 1)
            lo(KD - 1)
            dve.wait_ge(s_evac, evac.next())
            mla_rope(KB[rows, 0], step)
            dve.tensor_copy(KB[rows, 1], KB[rows, 0]).then_inc(s_kpe, kpe.up())
            dve.wait_ge(s_kpe, kpe.now())
            dve.wait_ge(s_evac, evac.next(KD))
            dve.wait_ge(s_unturn, unturn.next(KD))
            with loop(dve, HEADS // 4, [(evac, 8), (q, 4), (sc, 16), (mx, 16), (exp_c, 16), (prob, 16), (oh, 2), (ol, 2),
                                       (step, 4 * (3 + 1 + 4 + 4)), (unturn, 16)]) as i:
                for u in range(4):
                    dve.wait_ge(s_evac, evac.next())
                    mla_rope(QB[rows, u % 2], q)
                    evac.at += 1

                    def max_of(qt):
                        dve.wait_ge(s_sc, sc.next())
                        dve.tensor_reduce(NM[:, qt:qt + 1], SUMB[qt % 2][:, 0:(qt + 1) * P], AX.X, ALU.max).then_inc(s_dve, step.up())
                        dve.wait_ge(s_dve, step.now())
                        dve.tensor_scalar(NMS[:, qt:qt + 1], NM[:, qt:qt + 1], -MLA_SCALE, None, ALU.mult).then_inc(s_max, mx.up())
                        dve.wait_ge(s_max, mx.now())

                    def scale(qt):
                        dve.wait_ge(s_exp, exp_c.next())
                        dve.reciprocal(RINV[:, qt:qt + 1], RSUM[:, qt:qt + 1]).then_inc(s_dve, step.up())
                        dve.wait_ge(s_dve, step.now())
                        p = PB[:, qt % 2, 0:(qt + 1) * P]
                        dve.tensor_scalar(p, p, RINV[:, qt:qt + 1], None, ALU.mult).then_inc(s_prob, prob.up())
                        dve.wait_ge(s_prob, prob.now())
                    max_of(0)
                    max_of(1)
                    dve.tensor_copy(VB[:, u % 2], VM[:, :, col((i * 4 + u) * VH, VH)]).then_inc(s_dve, step.up())
                    dve.wait_ge(s_dve, step.now())
                    scale(0)
                    max_of(2)
                    scale(1)
                    max_of(3)
                    scale(2)
                    scale(3)
                    unturn.at += 4
                    if u % 2 == 1:
                        dve.wait_ge(s_oh, oh.next())
                        o_hi, o_lo = (t[:, col(i * 2 + u // 2)].rearrange("p a b -> p (a b)") for t in (OH, OL))
                        dve.tensor_tensor(o_lo, OB[:, :], o_hi.bitcast(F32), ALU.subtract).then_inc(s_ol, ol.up())
                        dve.wait_ge(s_ol, ol.now())
            residual("mla", 3)

        def ret():
            angles(RPOS, 1, FREQ[:, 1:2], RCOS[:, :], RSIN[:, :], RTMP[:, :])
            n = 4 + 2 * EV
            with loop(dve, RH, [(evac, n + EV), (ev, 4), (q, 2), (dec, 16), (sc, TT), (sd, TT), (sums, EV), (mom, 2), (var, 1),
                                (std, 1), (hin, EV), (hout, EV), (yr, EV), (step, 2 * 3 + 2 + 2 * EV + 2 + 2 * EV)]) as i:
                for t in (QT, KT):
                    dve.wait_ge(s_evac, evac.next(2))
                    s1, s2 = next_stage(), next_stage()
                    dve.tensor_tensor(t[:, 0], stage(s1), RCOS[:, :], ALU.mult).then_inc(s_dve, step.up())
                    dve.wait_ge(s_dve, step.now())
                    dve.tensor_tensor(RTMP[:, :], stage(s2), RSIN[:, :], ALU.mult).then_inc(s_dve, step.up())
                    dve.wait_ge(s_dve, step.now())
                    dve.tensor_tensor(t[:, 0], t[:, 0], RTMP[:, :], ALU.subtract).then_inc(s_dve, step.up())
                    dve.wait_ge(s_dve, step.now())
                    dve.tensor_tensor(t[:, 1], stage(s1), RSIN[:, :], ALU.mult).then_inc(s_ev, ev.up())
                    dve.wait_ge(s_ev, ev.now())
                    dve.tensor_tensor(RTMP[:, :], stage(s2), RCOS[:, :], ALU.mult).then_inc(s_ev, ev.up())
                    dve.wait_ge(s_ev, ev.now())
                    dve.tensor_tensor(t[:, 1], t[:, 1], RTMP[:, :], ALU.add).then_inc(s_q, q.up())
                    dve.wait_ge(s_q, q.now())
                dve.wait_ge(s_dec, dec.next(16))
                for kt in range(TT):
                    dve.wait_ge(s_sc, sc.next())
                    w = SEQ - kt * P
                    dve.tensor_tensor(SD[:, kt, kt * P:SEQ], SUMB[kt % 2][:, 0:w], DEC[:, 0:w], ALU.mult).then_inc(s_sd, sd.up())
                    dve.wait_ge(s_sd, sd.now())
                evac.at += 2 * EV
                clear_sums("ret")
                for j in range(EV):
                    dve.wait_ge(s_evac, evac.next())
                    add_sums("ret", R[:, j])
                inverse_std(RV)

                def lo(j):
                    dve.wait_ge(s_hout, hout.next())
                    y_hi, y_lo = (t[:, col(i * EV + j)].rearrange("p a b -> p (a b)") for t in (RYH, RYL))
                    dve.tensor_tensor(y_lo, R[:, j], y_hi.bitcast(F32), ALU.subtract).then_inc(s_y, yr.up())
                    dve.wait_ge(s_y, yr.now())
                for j in range(EV):
                    dve.tensor_tensor(R[:, j], R[:, j], stage(0), ALU.subtract).then_inc(s_dve, step.up())
                    dve.wait_ge(s_dve, step.now())
                    dve.tensor_tensor(R[:, j], R[:, j], stage(2), ALU.mult).then_inc(s_dve, step.up())
                    dve.wait_ge(s_dve, step.now())
                    dve.scalar_tensor_tensor(R[:, j], R[:, j], par(i * EV + (PC_RET + j)), R[:, EV + j], ALU.mult, ALU.mult).then_inc(s_hin, hin.up())
                    dve.wait_ge(s_hin, hin.now())
                    if j:
                        lo(j - 1)
                lo(EV - 1)
            residual("ret", 3)

        for kind, j, l in layers:
            if kind == "lru":
                lru(j)
            else:
                (mla if kind == "mla" else ret)()
            lnorm(0, l)
            ffn(l, l == depth - 1)


def constants():
    import numpy as np

    def freq(d):
        return (10000.0 ** (-np.arange(0, d, 2, dtype=np.float64) / d)).astype(np.float32)
    f = np.zeros((P, 4), np.float32)
    f[:, 0] = np.tile(freq(ROPE), 2 * P // ROPE)
    f[:, 1] = freq(RQK)
    f[:, 2] = np.tile(np.repeat([-1.0, 1.0], ROPE // 2), P // ROPE)
    k, q = np.arange(P)[:, None], np.arange(SEQ)[None, :]
    log_gamma = np.log1p(-np.exp2(-5.0 - np.arange(RH, dtype=np.float64)))
    decay = np.exp(log_gamma[:, None, None] * np.abs(q - k)) * (k // CHUNK <= q // CHUNK) * float(RQK) ** -0.5
    return {"rope_freq": f, "ret_decay": decay.astype(np.float32)}


def kernel(**inputs):
    import numpy as np
    import concourse.bacc as bacc
    from concourse.bass_utils import run_bass_kernel_spmd

    nc = bacc.Bacc("TRN2", target_bir_lowering=False, num_devices=1)
    arrays = {n: np.ascontiguousarray(v) for n, v in {**inputs, **constants()}.items()}
    aps = {n: nc.dram_tensor(n, v.shape, mybir.dt.from_np(v.dtype), kind="ExternalInput").ap() for n, v in arrays.items()}
    out = nc.dram_tensor("out", (1, SEQ, D), F32, kind="ExternalOutput").ap()
    build(nc, aps, out)
    r = run_bass_kernel_spmd(nc, [arrays], core_ids=[0])
    return r.results[0]["out"]
```

```python
from contextlib import ExitStack, contextmanager
import math

import concourse.bass as bass
from concourse import mybir

F32 = mybir.dt.float32
F32R = mybir.dt.float32r
I32 = mybir.dt.int32
ALU = mybir.AluOpType
ACT = mybir.ActivationFunctionType
AX = mybir.AxisListType

P = 128
DEPTH = 4
SEQ = 512
D = 1024
KD = D // P
ALPHA = (2.0 * DEPTH) ** 0.25
LN_EPS = 1e-5
RMS_EPS = 1e-6
TT = SEQ // P

DFF = 2816
NF = DFF // P
LRU_BLOCKS = 4
LRU_C = 8.0

HEADS = 16
NOPE, ROPE, VH = 64, 32, 64
QKH = NOPE + ROPE
Q_LORA, KV_LORA = 768, 256
KQ, KKV = Q_LORA // P, KV_LORA // P
MLA_SCALE = float(QKH) ** -0.5
MASKED = -1e30
CHUNK = 64

RH = 4
RQK, RV = D // RH, 2 * D // RH
EV = RV // P
KR = 2 * D // P

RING = 4
OUT_PARTS = 2
QT_ORDER = (3, 2, 1, 0)
PAD = 3

PC_LN = 0
PC_LRU = PC_LN + DEPTH * 4 * KD
LRU_COLS = 8 * KD
PC_FFN = PC_LRU + 2 * LRU_COLS
FFN_COLS = 4 * 2 * NF
PC_MLA = PC_FFN + DEPTH * FFN_COLS
PC_RET = PC_MLA + KQ + KKV
PC_RATE = PC_RET + KR
N_PC = PC_RATE + 2 * 2 * KD

ROW_GROUPS = [(4 * DEPTH * KD, PC_LN, [(n, slice(0, DEPTH)) for n in ("ln1_g", "ln1_b", "ln2_g", "ln2_b")])]
for _j in range(2):
    ROW_GROUPS.append((LRU_COLS, PC_LRU + _j * LRU_COLS,
                       [(n, _j) for n in ("lru_conv_w", "lru_conv_b", "lru_b_a", "lru_b_x", "lru_lambda")]))
for _l in range(DEPTH):
    ROW_GROUPS.append((4 * NF, PC_FFN + _l * FFN_COLS, [("ffn_conv_w", (_l, slice(0, 2)))]))
    ROW_GROUPS.append((4 * NF, PC_FFN + _l * FFN_COLS + 4 * NF, [("ffn_conv_w", (_l, slice(2, 3))), ("ffn_conv_b", _l)]))
ROW_GROUPS.append((KQ + KKV + KR, PC_MLA, [("mla_q_norm", 0), ("mla_kv_norm", 0), ("ret_gn_g", 0)]))
N_SMALL = sum(len(v) for _, _, v in ROW_GROUPS) + 1

TWO_PI = 2 * math.pi
ROUND = 1.5 * 2.0 ** 23
PI2_A = 6.28125
PI2_B = round((TWO_PI - PI2_A) * 2.0 ** 20) / 2.0 ** 20
PI2_C = TWO_PI - PI2_A - PI2_B
PI_CLAMP = 3.1415925


class Count:

    def __init__(self, sem, at=0):
        self.sem, self.at, self.roll = sem, at, 0

    def up(self, n=1):
        self.at += n
        return n

    def next(self, n=1):
        self.at += n
        return self.roll + self.at

    def now(self, more=0):
        return self.roll + (self.at + more)


@contextmanager
def loop(eng, times, per):
    first = [c.at for c, _ in per]
    with eng.Fori(0, times) as i:
        for c, n in per:
            c.roll = i * n
        yield i
    for (c, n), at in zip(per, first):
        assert c.at - at == n, (c.sem.name if hasattr(c.sem, "name") else c.sem, c.at - at, n)
        c.at, c.roll = at + times * n, 0


def col(i, n=1):
    return bass.ds(i, n)


def build(nc, a, out, depth=DEPTH):
    with ExitStack() as ctx:
        build_in(nc, a, out, ctx, depth)


def build_in(nc, a, out, ctx, depth):
    def sem(name):
        return ctx.enter_context(nc.semaphore(name))

    def sb(name, shape, dt=F32, on=ctx):
        return on.enter_context(nc.sbuf_tensor(name, shape, dt))

    XH = sb("x_hi", [P, KD, SEQ], F32R)
    XL = sb("x_lo", [P, KD, SEQ], F32R)
    R = sb("residual", [P, KD, SEQ])
    RAW = sb("w_raw", [P, RING, 8, P])
    WH = sb("w_hi", [P, RING, 8, P], F32R)
    WL = sb("w_lo", [P, RING, 8, P], F32R)
    ST = sb("staged", [P, RING, PAD + SEQ])
    PAR = sb("params", [P, N_PC])
    IDENT = sb("ident", [P, P])
    ONES = sb("ones", [P, P])
    FREQ = sb("freq", [P, 4])
    NM = sb("neg_max", [P, TT])
    NMS = sb("neg_max_scaled", [P, TT])
    RSUM = sb("row_sum", [P, TT])
    RINV = sb("row_sum_inv", [P, TT])
    LAM = sb("lambda_exp", [P, 2, KD])
    LAMT = sb("lambda_tmp", [P, 3, 2, KD])
    NORM = sb("norm_small", [P, 4, TT])
    MEAN, TMP4, VINV, RSTD = (NORM[:, i, :] for i in range(4))
    WARM = sb("table_ahead", [P, 1])
    MROW = sb("mask_row", [1, P + CHUNK])

    def stage(s, lag=0):
        return ST[:, s, PAD - lag:PAD - lag + SEQ]

    with ExitStack() as s:
        XT = sb("x_tokens", [P, TT, D], on=s)
        ROWS = sb("param_rows", [P, 12, P], on=s)
    with ExitStack() as s:
        U = sb("lru_u", [P, KD, SEQ], on=s)
        A = sb("lru_a", [P, KD, SEQ], on=s)
        I = sb("lru_i", [P, KD, SEQ], on=s)
        GATE = sb("lru_gate", [P, KD, SEQ], on=s)
        UH = sb("lru_u_hi", [P, KD, SEQ], F32R, on=s)
        UL = sb("lru_u_lo", [P, KD, SEQ], F32R, on=s)
        YH, YL = UH, UL
    with ExitStack() as s:
        AG = sb("ffn_gate", [P, SEQ], on=s)
        AU = sb("ffn_up", [P, SEQ], on=s)
        AT = sb("ffn_tmp", [P, SEQ], on=s)
        GH = sb("ffn_h_hi", [P, NF, SEQ], F32R, on=s)
        GL = sb("ffn_h_lo", [P, NF, SEQ], F32R, on=s)
    with ExitStack() as s:
        CNH = sb("c_hi", [P, KD, SEQ], F32R, on=s)
        CNL = sb("c_lo", [P, KD, SEQ], F32R, on=s)
        OH = sb("o_hi", [P, KD, SEQ], F32R, on=s)
        OL = sb("o_lo", [P, KD, SEQ], F32R, on=s)
        QB = sb("q_head", [QKH, 2, SEQ], on=s)
        KB = sb("k_head", [QKH, 2, SEQ], on=s)
        PB = sb("probs", [P, TT, SEQ], on=s)
        PT = sb("probs_t", [P, TT, SEQ], on=s)
        MCOS = sb("mla_cos", [P, SEQ], on=s)
        MSIN = sb("mla_sin", [P, SEQ], on=s)
        ROT = sb("mla_rot", [P, SEQ], on=s)
        VB = sb("v_head", [P, 2, TT, VH], on=s)
    MPOS = PT[:, TT - 1].bitcast(I32)
    VM = R[:, :, :].rearrange("p a (b c) -> p (a b c)", b=1).rearrange("p (t f) -> p t f", t=TT)
    with ExitStack() as s:
        RYH = sb("ret_y_hi", [P, KR, SEQ], F32R, on=s)
        RYL = sb("ret_y_lo", [P, KR, SEQ], F32R, on=s)
        QT = sb("ret_q", [P, 2, SEQ], on=s)
        KT = sb("ret_k", [P, 2, SEQ], on=s)
        V = sb("ret_v", [P, TT, RV], on=s)
        SD = sb("ret_scores", [P, TT, SEQ], on=s)
        RCOS = sb("ret_cos", [P, SEQ], on=s)
        RSIN = sb("ret_sin", [P, SEQ], on=s)
        RTMP = sb("ret_tmp", [P, SEQ], on=s)
        DEC = sb("decay_table", [P, SEQ], on=s)
    RPOS = DEC[:, :].bitcast(I32)

    SUMS = {
        "lru": (A[:, 0, :], A[:, 1, :], A[:, 2, :]),
        "ffn": (AG[:, :], AU[:, :], AT[:, :]),
        "mla": (PB[:, 0, :], PB[:, 1, :], PT[:, 0, :]),
        "ret": (QT[:, 0, :], QT[:, 1, :], RTMP[:, :]),
    }

    BANK = [ctx.enter_context(nc.psum_tensor(f"bank{i}", [P, SEQ], F32)) for i in range(8)]
    SUMB = BANK[4:6]
    HEADB = BANK[2:6]
    TURN = BANK[6]
    OB = BANK[7]

    s_raw = [sem(f"raw_loaded{i}") for i in range(RING)]
    s_rawk = [sem(f"raw_second_loaded{i}") for i in range(RING)]
    s_small = sem("small_loaded")
    s_xin = sem("x_loaded")
    s_pos = [sem("mla_pos_loaded"), sem("ret_pos_loaded")]
    s_dec = sem("decay_loaded")
    s_const = sem("consts_made")
    s_pads = sem("pads_zeroed")
    s_hi = sem("w_hi_done")
    s_lo = sem("w_lo_done")
    s_panel = sem("panel_done")
    s_evac = sem("evac_done")
    s_ev = sem("staged_used")
    s_act = sem("act_step")
    s_dve = sem("dve_step")
    s_turn = sem("turned")
    s_unturn = sem("turn_read")
    s_lam = sem("lambda_exp")
    s_res = sem("x_normal")
    s_xh = sem("x_hi_done")
    s_xr = sem("x_new")
    s_x = sem("x_ready")
    s_gelu = sem("gelu_done")
    s_g = sem("hidden_ready")
    s_u = sem("u_ready")
    s_iu = sem("iu_done")
    s_ta = sem("decay_done")
    s_mul = sem("mult2_done")
    s_sq = sem("mult_done")
    s_y = sem("y_ready")
    s_sum = sem("sums_ready")
    s_stat = sem("sums_reduced")
    s_dmean = sem("mean_diagonal")
    s_bmean = sem("mean_spread")
    s_var = sem("inverse_variance")
    s_std = sem("inverse_deviation")
    s_drstd = sem("deviation_diagonal")
    s_brstd = sem("deviation_spread")
    s_hin = sem("norm_tile")
    s_hout = sem("norm_tile_hi")
    s_rot = sem("rope_ready")
    s_trig = sem("trig_ready")
    s_cn = sem("latent_ready")
    s_kpe = sem("k_pe_ready")
    s_q = sem("q_ready")
    s_sc = sem("scores_done")
    s_max = sem("max_done")
    s_exp = sem("exp_done")
    s_qlat = sem("q_product_done")
    s_prob = sem("probs_ready")
    s_o = sem("o_done")
    s_oh = sem("o_hi_done")
    s_ol = sem("o_ready")
    s_sd = sem("decayed_ready")
    s_go = sem("shuffle_may_go")
    s_store = sem("out_stored")

    block = ctx.enter_context(nc.Block())
    KINDS = ["lru", "mla", "ret"]
    layers = [(KINDS[i % 3], i // 3, i) for i in range(depth)]

    @block.sync
    def _(sp):
        n_panel = [0]
        lo = Count(s_lo)

        def slot():
            k = n_panel[0]
            n_panel[0] += 1
            if k >= RING:
                sp.wait_ge(s_lo, lo.next())
            return k % RING

        def panel(src, blocks=8, cols=P):
            s, half = slot(), blocks // 2
            sp.dma_start(RAW[:, s, 0:half, 0:cols], src[:, 0:half]).then_inc(s_raw[s], 16)
            sp.dma_start(RAW[:, s, half:blocks, 0:cols], src[:, half:blocks]).then_inc(s_rawk[s], 16)

        def ks(w):
            return w.rearrange("(c p) m -> p c m", p=P)

        def panels(times, per, load):
            start = 0
            if n_panel[0] == 0:
                load(0)
                start = 1
            if start < times:
                before = n_panel[0]
                at = lo.at
                with sp.Fori(start, times) as i:
                    lo.roll = (i - start) * per
                    load(i)
                assert n_panel[0] - before == per
                n_panel[0] = before + (times - start) * per
                lo.at, lo.roll = at + (times - start) * per, 0

        def lru(j):
            w = ks(a["lru_w_in"][j])

            def four(i, base):
                for u in range(4):
                    panel(w[:, :, col(base + i * (4 * P) + u * P, P)])
            panels(2, 4, lambda i: four(i, D))
            for g in range(LRU_BLOCKS):
                s = slot()
                for n, name in enumerate(("lru_w_a", "lru_w_x")):
                    src = a[name][j, g].rearrange("(k p) (m c) -> p k m c", p=P, c=P)
                    q = (s_raw, s_rawk)[n][s]
                    sp.dma_start(RAW[:, s, 4 * n:4 * n + 4, :].rearrange("p (k m) c -> p k m c", k=2), src).then_inc(q, 16)
            panels(2, 4, lambda i: four(i, 0))
            wo = ks(a["lru_w_out"][j])
            panels(2, 4, lambda i: [panel(wo[:, :, col(i * (4 * P) + u * P, P)]) for u in range(4)])

        def mla(j):
            w = ks(a["mla_w_in"][j])
            for m in range(KQ, KD):
                panel(w[:, :, m * P:(m + 1) * P])
            panel(w[:, :, Q_LORA + KV_LORA - NOPE:Q_LORA + KV_LORA + ROPE], 8, QKH)
            for m in range(KQ):
                panel(w[:, :, m * P:(m + 1) * P])
            wkv = a["mla_w_ukv"][j].rearrange("(k p) (h two c) -> p k h two c", p=P, two=2, c=NOPE)
            for half in range(2):
                s = slot()
                for k in range(KKV):
                    q = (s_raw, s_rawk)[k][s]
                    sp.dma_start(RAW[:, s, 4 * k:4 * k + 4, :].rearrange("p m (t c) -> p (m t) c", c=VH),
                                 wkv[:, k, 8 * half:8 * half + 8, 1, :]).then_inc(q, 16)
            wq = ks(a["mla_w_uq"][j])
            wk = ks(a["mla_w_ukv"][j])

            def head(h):
                s = slot()
                sp.dma_start(RAW[:, s, 0:KQ, 0:QKH], wq[:, :, col(h * QKH, QKH)]).then_inc(s_raw[s], 16)
                sp.dma_start(RAW[:, s, KQ:8, 0:NOPE], wk[:, :, col(h * (2 * NOPE), NOPE)]).then_inc(s_rawk[s], 16)
            panels(HEADS // 4, 4, lambda i: [head(i * 4 + u) for u in range(4)])
            wo = ks(a["mla_w_out"][j])
            panels(2, 4, lambda i: [panel(wo[:, :, col(i * (4 * P) + u * P, P)]) for u in range(4)])

        def ret(j):
            w = ks(a["ret_w_in"][j])

            def head(h):
                for u in range(2):
                    panel(w[:, :, col(h * RQK + u * P, P)])
                for u in range(2):
                    panel(w[:, :, col(h * RQK + (D + u * P), P)])
                for base in (2 * D, 4 * D):
                    for u in range(EV):
                        panel(w[:, :, col(h * RV + (base + u * P), P)])
            panels(RH, 4 + 2 * EV, head)
            wo = ks(a["ret_w_out"][j])

            def four(i):
                for u in range(4):
                    for half in range(2):
                        panel(wo[:, 8 * half:8 * half + 8, col(i * (4 * P) + u * P, P)])
            panels(2, 8, four)

        def ffn(l):
            w = ks(a["ffn_w_up"][l])
            panels(NF // 2, 4, lambda i: [panel(w[:, :, col(i * (2 * P) + (u * P + half * DFF), P)])
                                          for u in range(2) for half in range(2)])
            wo = ks(a["ffn_w_down"][l])

            def four(i):
                for u in range(4):
                    for c0 in range(0, NF, 8):
                        c1 = min(NF, c0 + 8)
                        panel(wo[:, c0:c1, col(i * (4 * P) + u * P, P)], c1 - c0)
            panels(2, 12, four)

        sp.dma_start(XT[:, :, :], a["x"][0].rearrange("(t p) d -> p t d", p=P)).then_inc(s_xin, 16)
        for kind, j, l in layers:
            {"lru": lru, "mla": mla, "ret": ret}[kind](j)
            ffn(l)

    def total_panels():
        n = {"lru": 28, "mla": 35, "ret": 64}
        return sum(n[k] + 2 * NF + 8 * ((NF + 7) // 8) for k, _, _ in layers)

    NPAN = total_panels()

    @block.gpsimd
    def _(pool):
        con = Count(s_const)
        pool.memset(IDENT[:, :], 0.0).then_inc(s_const, con.up())
        pool.memset(ONES[:, :], 1.0).then_inc(s_const, con.up())
        pool.memset(MROW[:, 0:CHUNK], 1.0).then_inc(s_const, con.up())
        pool.memset(MROW[:, CHUNK:P], 0.0).then_inc(s_const, con.up())
        pool.memset(MROW[:, P:P + CHUNK], MASKED).then_inc(s_const, con.up())
        pool.wait_ge(s_const, con.now())
        pool.affine_select(out=IDENT[:, :], in_=IDENT[:, :], compare_op=ALU.not_equal, fill=1.0,
                                    base=0, pattern=[[-1, P]], channel_multiplier=1).then_inc(s_const, con.up())
        hi, lo = Count(s_hi), Count(s_lo)

        def part(s):
            pool.wait_ge(s_hi, hi.next())
            pool.tensor_tensor(WL[:, s], RAW[:, s], WH[:, s].bitcast(F32), ALU.subtract).then_inc(s_lo, lo.up())
        with loop(pool, NPAN // RING, [(hi, RING), (lo, RING)]):
            for s in range(RING):
                part(s)
        for s in range(NPAN % RING):
            part(s)

    @block.tensor
    def _(pe):
        lo, panel_c, bank = Count(s_lo), Count(s_panel), Count(s_evac)
        xr, turn, unturn = Count(s_x), Count(s_turn), Count(s_unturn)
        stat, sums, yr = Count(s_stat), Count(s_sum), Count(s_y)
        dmean, bmean, drstd, brstd = Count(s_dmean), Count(s_bmean), Count(s_drstd), Count(s_brstd)
        q, sc, prob, qlat = Count(s_q), Count(s_sc), Count(s_prob), Count(s_qlat)
        o, ol, sd = Count(s_o), Count(s_ol), Count(s_sd)
        x_at = [0]

        def take_panel():
            s = lo.at % RING
            pe.wait_ge(s_lo, lo.next())
            return s

        def take_bank():
            b = BANK[bank.at % RING]
            pe.wait_ge(s_evac, bank.next())
            return b

        def product(ps, s, c, m, xh, xl, first, last):
            pe.matmul(ps, WL[:, s, c, 0:m], xh, start=first, stop=False)
            pe.matmul(ps, WH[:, s, c, 0:m], xl, start=False, stop=False)
            return pe.matmul(ps, WH[:, s, c, 0:m], xh, start=False, stop=last)

        def tile(xh, xl, blocks, m=P, ready=None):
            b = take_bank()
            for c in range(blocks):
                if c % 8 == 0:
                    s = take_panel()
                if ready is not None:
                    ready(c)
                last = product(b[0:m, :], s, c % 8, m, xh[:, c, :], xl[:, c, :], c == 0, c == blocks - 1)
                if c % 8 == 7 or c == blocks - 1:
                    last.then_inc(s_panel, panel_c.up())

        def x_ready(c):
            pe.wait_ge(s_x, x_at[0] - KD + c + 1)

        def first_tiles(rows=(P, P, P)):
            slots, banks = [take_panel() for _ in rows], [take_bank() for _ in rows]
            for c in range(KD):
                x_ready(c)
                for s, b, m in zip(slots, banks, rows):
                    last = product(b[0:m, :], s, c, m, XH[:, c, :], XL[:, c, :], c == 0, c == KD - 1)
                    if c == KD - 1:
                        last.then_inc(s_panel, panel_c.up())

        def x_tiles(times):
            with loop(pe, times, [(lo, 4), (bank, 4), (panel_c, 4)]):
                for _ in range(4):
                    tile(XH, XL, KD)

        def out_tiles(xh, xl, blocks, ready):
            n = 4 * ((blocks + 7) // 8)
            with loop(pe, 2, [(lo, n), (bank, 4), (panel_c, n)]):
                for u in range(4):
                    tile(xh, xl, blocks, ready=ready if u == 0 else None)

        def token_sums(sources, n):
            pe.wait_ge(s_sum, sums.next(n))
            pe.wait_ge(s_unturn, unturn.now(1))
            for i, src in enumerate(sources):
                for t in range(TT):
                    ins = pe.matmul(TURN[:, i * TT + t:i * TT + t + 1], src[:, t * P:(t + 1) * P], ONES[:, 0:1],
                                    start=True, stop=True)
            ins.then_inc(s_stat, stat.up())

        def spread_mean():
            pe.wait_ge(s_dmean, dmean.next())
            pe.matmul(SUMB[0][:, :], ONES[:, :], stage(0), start=True, stop=True).then_inc(s_bmean, bmean.up())

        def spread_rstd():
            pe.wait_ge(s_drstd, drstd.next())
            pe.matmul(SUMB[1][:, :], ONES[:, :], stage(1), start=True, stop=True).then_inc(s_brstd, brstd.up())

        def norm(kind):
            token_sums(SUMS[kind][0:2], KD)
            spread_mean()
            spread_rstd()
            x_at[0] += KD

        def take_turn():
            pe.wait_ge(s_unturn, unturn.next())

        pe.wait_ge(s_const, 6)
        pe.wait_ge(s_small, 16 * N_SMALL)
        for n, (rows, _, _) in enumerate(ROW_GROUPS):
            b = take_bank()
            pe.transpose(b[:, 0:rows], ROWS[0:rows, n, :], IDENT[0:rows, 0:rows]).then_inc(s_turn, turn.up())
        pe.wait_ge(s_xin, 16)
        for m in range(KD):
            b = take_bank()
            for t in range(TT):
                ins = pe.transpose(b[:, t * P:(t + 1) * P], XT[:, t, m * P:(m + 1) * P], IDENT[:, :])
            ins.then_inc(s_turn, turn.up())
        x_at[0] += KD

        def lru():
            first_tiles()
            for _ in range(KD - 3):
                tile(XH, XL, KD)
            for g in range(LRU_BLOCKS):
                pe.wait_ge(s_u, lru_u[0] + 2 * g + 2)
                s = take_panel()
                for n in range(4):
                    b = take_bank()
                    for k in range(2):
                        c = 4 * (n // 2) + 2 * k + n % 2
                        last = product(b[:, :], s, c, P, UH[:, 2 * g + k, :], UL[:, 2 * g + k, :], k == 0, k == 1)
                last.then_inc(s_panel, panel_c.up())
            lru_u[0] += KD
            x_tiles(2)
            base = yr.at
            out_tiles(YH, YL, KD, lambda c: pe.wait_ge(s_y, base + c + 1))
            yr.at += KD
            norm("lru")
        lru_u = [0]

        def ffn():
            first_tiles()
            tile(XH, XL, KD)
            x_tiles(NF // 2 - 1)
            base = hid[0]
            out_tiles(GH, GL, NF, lambda c: pe.wait_ge(s_g, base + c + 1))
            hid[0] += NF
            norm("ffn")
        hid = [0]

        def mla():
            first_tiles((P, P, QKH))
            tile(XH, XL, KD)
            token_sums([PT[:, 1, :]], KKV)
            tile(XH, XL, KD)
            spread_rstd()
            for _ in range(KQ - 2):
                tile(XH, XL, KD)
            pe.wait_ge(s_cn, KKV)

            def v_tiles():
                s = take_panel()
                for m in range(4):
                    b = take_bank()
                    for k in range(KKV):
                        last = product(b[:, :], s, 4 * k + m, P, CNH[:, KQ + k, :], CNL[:, KQ + k, :], k == 0, k == KKV - 1)
                last.then_inc(s_panel, panel_c.up())

            def v_turns():
                for m in range(4):
                    b = take_bank()
                    for t in range(TT):
                        ins = pe.transpose(b[:, t * P:(t + 1) * P], PB[:, m, t * P:(t + 1) * P], IDENT[:, :])
                    ins.then_inc(s_turn, turn.up())
            v_tiles()
            token_sums([PT[:, 2, :]], KQ)
            v_turns()
            spread_rstd()
            v_tiles()
            v_turns()
            pe.wait_ge(s_cn, KD)
            pe.wait_ge(s_evac, bank.now(RING))

            def q_product():
                s = take_panel()
                for c in range(KQ):
                    last = product(BANK[0][0:QKH, :], s, c, QKH, CNH[:, c, :], CNL[:, c, :], c == 0, c == KQ - 1)
                last.then_inc(s_qlat, qlat.up())
                return s

            def k_product(s):
                for k in range(KKV):
                    last = product(BANK[1][0:NOPE, :], s, KQ + k, NOPE, CNH[:, KQ + k, :], CNL[:, KQ + k, :],
                                   k == 0, k == KKV - 1)
                last.then_inc(s_panel, panel_c.up())
                bank.at += 2

            def head(u, more=True):
                pe.wait_ge(s_evac, bank.now(RING))
                pe.wait_ge(s_q, q.next())
                for qt in QT_ORDER:
                    kv, b = (qt + 1) * P, HEADB[qt]
                    pe.matmul(b[:, 0:kv], QB[:, u % 2, qt * P:(qt + 1) * P], KB[:, u % 2, 0:kv], start=True, stop=False)
                    pe.matmul(b[:, kv - CHUNK:kv], MROW[0:1, 0:P], MROW[0:1, P:P + CHUNK], start=False, stop=True).then_inc(s_sc, sc.up())
                if more:
                    s = q_product()
                for qt in QT_ORDER:
                    pe.wait_ge(s_prob, prob.next())
                    for kt in range(qt + 1):
                        ins = pe.transpose(HEADB[qt][:, kt * P:(kt + 1) * P], PB[:, qt, kt * P:(kt + 1) * P], IDENT[:, :])
                    ins.then_inc(s_turn, turn.up())
                if more:
                    k_product(s)
                unturn.at += TT
                pe.wait_ge(s_unturn, unturn.now(1))
                if u % 2 == 0:
                    pe.wait_ge(s_ol, ol.next())
                r0 = VH * (u % 2)
                for kt in range(TT):
                    ins = pe.matmul(OB[r0:r0 + VH, kt * P:SEQ], VB[:, u % 2, kt, :], PT[:, kt, kt * P:SEQ],
                                    start=kt == 0, stop=kt == TT - 1)
                if u % 2 == 1:
                    ins.then_inc(s_o, o.up())
            k_product(q_product())
            pe.wait_ge(s_kpe, 1)
            with loop(pe, HEADS // 4 - 1, [(lo, 4), (bank, 8), (panel_c, 4), (qlat, 4), (q, 4), (sc, 16),
                                           (prob, 16), (turn, 16), (unturn, 16), (o, 2), (ol, 2)]):
                for u in range(4):
                    head(u)
            for u in range(4):
                head(u, more=u < 3)
            out_tiles(OH, OL, KD, lambda c: pe.wait_ge(s_ol, 1 + c + 1))
            norm("mla")

        def ret():
            n = 4 + 2 * EV

            def turn_v(j):
                pe.wait_ge(s_evac, bank.roll + (RING + bank.at - 1))
                take_turn()
                for t in range(TT):
                    ins = pe.transpose(TURN[:, t * P:(t + 1) * P], R[:, j, t * P:(t + 1) * P], IDENT[:, :])
                ins.then_inc(s_turn, turn.up())
            with loop(pe, RH, [(lo, n), (bank, n + EV), (panel_c, n), (turn, EV), (unturn, EV), (q, 2), (sd, TT), (sc, TT),
                               (o, EV), (sums, EV), (stat, 1), (dmean, 1), (bmean, 1), (drstd, 1), (brstd, 1)]):
                first_tiles()
                tile(XH, XL, KD)
                tile(XH, XL, KD)
                for j in range(1, EV):
                    tile(XH, XL, KD)
                    turn_v(j - 1)
                pe.wait_ge(s_q, q.next(2))
                for kt in range(TT):
                    b = SUMB[kt % 2]
                    pe.wait_ge(s_sd, sd.next())
                    for c in range(2):
                        ins = pe.matmul(b[:, 0:SEQ - kt * P], KT[:, c, kt * P:(kt + 1) * P], QT[:, c, kt * P:SEQ],
                                        start=c == 0, stop=c == 1)
                    ins.then_inc(s_sc, sc.up())
                turn_v(EV - 1)
                tile(XH, XL, KD)
                pe.wait_ge(s_unturn, unturn.now(1))
                pe.wait_ge(s_sd, sd.now(2))
                for j in range(EV):
                    b = take_bank()
                    for kt in range(TT):
                        ins = pe.matmul(b[:, kt * P:SEQ], V[:, kt, j * P:(j + 1) * P], SD[:, kt, kt * P:SEQ],
                                        start=kt == 0, stop=kt == TT - 1)
                    ins.then_inc(s_o, o.up())
                for _ in range(EV - 2):
                    tile(XH, XL, KD)
                token_sums(SUMS["ret"][0:2], EV)
                tile(XH, XL, KD)
                spread_mean()
                spread_rstd()
            base = yr.at
            out_tiles(RYH, RYL, KR, lambda c: pe.wait_ge(s_y, base + c + 1))
            yr.at += KR
            norm("ret")

        for kind, j, l in layers:
            {"lru": lru, "mla": mla, "ret": ret}[kind]()
            ffn()
        for m in range(KD):
            pe.wait_ge(s_xr, x_at[0] - 2 * KD + m + 1)
            b = take_bank()
            for t in range(TT):
                ins = pe.transpose(b[:, t * P:(t + 1) * P], R[:, m, t * P:(t + 1) * P], IDENT[:, :])
            ins.then_inc(s_turn, turn.up())

    @block.scalar
    def _(act):
        hi, panel_c, evac, ev = Count(s_hi), Count(s_panel), Count(s_evac, RING), Count(s_ev)
        raw = [Count(q) for q in s_raw + s_rawk]
        step, res, xh = Count(s_act), Count(s_res), Count(s_xh)
        turn, unturn = Count(s_turn), Count(s_unturn, 1)
        xr, var, std = Count(s_xr), Count(s_var), Count(s_std)
        qlat = Count(s_qlat)
        hin, hout, gelu = Count(s_hin), Count(s_hout), Count(s_gelu)
        iu, ta, mul, sq, yr = Count(s_iu), Count(s_ta), Count(s_mul), Count(s_sq), Count(s_y)
        rot, trig, dec = Count(s_rot), Count(s_trig), Count(s_dec)
        q, mx, exp_c, o, oh = Count(s_q), Count(s_max), Count(s_exp), Count(s_o), Count(s_oh)
        sd = Count(s_sd, 2)
        act.sem_inc(s_evac, RING)
        act.sem_inc(s_unturn, 1)

        def split():
            if hi.at == NPAN:
                return
            s = hi.at % RING
            act.wait_ge(s_raw[s], raw[s].next(16))
            act.wait_ge(s_rawk[s], raw[RING + s].next(16))
            act.activation(WH[:, s], RAW[:, s], ACT.Copy).then_inc(s_hi, hi.up())

        def panels_per(n):
            return [(hi, n), (panel_c, n)] + [(c, 16 * n // RING) for c in raw]

        def used(*evacs):
            act.wait_ge(s_panel, panel_c.next())
            for e in evacs:
                e().then_inc(s_evac, evac.up())
            split()

        def to_stage():
            b, s = BANK[(evac.at - RING) % RING], ev.at % RING
            act.wait_ge(s_ev, ev.next())
            return act.activation(stage(s), b[:, :], ACT.Copy)

        def now(rows=slice(0, P)):
            return BANK[(evac.at - RING) % RING][rows, :]

        def par(c):
            return PAR[:, col(c)]

        for n, (rows, _, vectors) in enumerate(ROW_GROUPS):
            r = 0
            for name, pick in vectors:
                src = a[name][pick] if not isinstance(pick, tuple) else a[name][pick[0], pick[1]]
                dims = len(src.shape)
                names = "abc"[:dims - 1]
                flat = src.rearrange(f"{' '.join(names)} (t p) -> ({' '.join(names)} t) p", p=P) if dims > 1 else \
                    src.rearrange("(t p) -> t p", p=P)
                k = flat.shape[0]
                act.dma_start(ROWS[r:r + k, n, :], flat).then_inc(s_small, 16)
                r += k
            assert r == rows
        act.dma_start(FREQ[:, :], a["rope_freq"]).then_inc(s_small, 16)
        for _ in range(RING):
            split()
        for n, (rows, c0, _) in enumerate(ROW_GROUPS):
            act.wait_ge(s_turn, turn.next())
            act.activation(PAR[:, c0:c0 + rows], now()[:, 0:rows], ACT.Copy).then_inc(s_evac, evac.up())
        act.wait_ge(s_evac, evac.now())
        for j in range(2):
            lam = PC_LRU + j * LRU_COLS + 7 * KD
            act.activation(LAM[:, j, :], PAR[:, lam:lam + KD], ACT.Abs).then_inc(s_act, step.up())
        act.wait_ge(s_act, step.now())
        act.activation(LAM[:, :, :], LAM[:, :, :], ACT.Exp, scale=-1.0).then_inc(s_lam, 1)
        for m in range(KD):
            act.wait_ge(s_turn, turn.next())
            act.activation(XH[:, m], now(), ACT.Copy).then_inc(s_xh, xh.up())
            act.activation(R[:, m], now(), ACT.Copy).then_inc(s_evac, evac.up())

        def root():
            act.wait_ge(s_act, step.now())
            act.activation(WARM[:, :], ONES[:, 0:1], ACT.Sqrt).then_inc(s_act, step.up())
            act.wait_ge(s_var, var.next())
            act.activation(RSTD, VINV, ACT.Sqrt).then_inc(s_std, std.up())

        def norm(gain, shift, last=False):
            root()
            for m in range(KD):
                act.wait_ge(s_res, res.next())
                if not last:
                    act.activation(XH[:, m], R[:, m], ACT.Identity, scale=par(gain + m), bias=par(shift + m)).then_inc(s_xh, xh.up())
                    act.wait_ge(s_xh, xh.now())
                act.activation(R[:, m], R[:, m], ACT.Identity, scale=par(gain + m), bias=par(shift + m)).then_inc(s_xr, xr.up())

        def lnorm(which, l, last=False):
            c = PC_LN + 2 * which * DEPTH * KD + l * KD
            norm(c, c + DEPTH * KD, last)

        def x_tiles(times, each, e):
            with loop(act, times, panels_per(each) + [(evac, each), (ev, each if e is to_stage else 0)]):
                for _ in range(each):
                    used(e)

        def out_tiles(blocks, peel=False):
            n = (blocks + 7) // 8

            def body():
                for _ in range(4):
                    for _ in range(n - 1):
                        used()
                    used(to_stage)
            if peel:
                body()
                body()
            else:
                with loop(act, 2, panels_per(4 * n) + [(evac, 4), (ev, 4)]):
                    body()

        def lru(j):
            base, rate = PC_LRU + j * LRU_COLS, PC_RATE + j * 2 * KD
            x_tiles(2, 4, to_stage)
            for g in range(LRU_BLOCKS):
                used(*[lambda n=n, m=m: act.activation((A, I)[n][:, 2 * g + m], now(), ACT.Sigmoid,
                                                       bias=par(base + (5 + n) * KD + 2 * g + m))
                       for n in range(2) for m in range(2)])
            for c in range(KD):
                act.wait_ge(s_iu, iu.next())
                act.activation(I[:, c], A[:, c], ACT.Tanh, scale=par(rate + c))
                act.activation(A[:, c], A[:, c], ACT.Exp, scale=par(rate + KD + c)).then_inc(s_ta, ta.up())
            for c in range(KD):
                act.wait_ge(s_mul, mul.next())
                act.activation(I[:, c], I[:, c], ACT.Sqrt).then_inc(s_sq, sq.up())
            for c in range(KD):
                used(lambda: act.activation(GATE[:, c], now(), ACT.Gelu_apprx_tanh))
            yr.at += KD
            out_tiles(KD)

        def ffn(l, last):
            with loop(act, NF // 2, panels_per(4) + [(evac, 4), (ev, 4), (gelu, 2)]):
                for _ in range(2):
                    used(to_stage)
                    used(to_stage)
                    act.wait_ge(s_ev, ev.now(RING - 1))
                    act.activation(AG[:, :], AG[:, :], ACT.Gelu_apprx_tanh).then_inc(s_gelu, gelu.up())
            out_tiles(NF, peel=last)
            lnorm(1, l, last)

        def angles(cos, sin):
            act.wait_ge(s_rot, rot.next())
            act.activation(sin, sin, ACT.Sin).then_inc(s_trig, trig.up())
            act.activation(cos, cos, ACT.Sin).then_inc(s_trig, trig.up())

        def mla():
            act.dma_start(MPOS[:, :], a["positions"].broadcast_to([P, SEQ])).then_inc(s_pos[0], 16)
            angles(MCOS[:, :], MSIN[:, :])
            for m in range(KQ, KD):
                used(lambda: act.activation(R[:, m], now(), ACT.Copy))
            used(lambda: act.activation(KB[NOPE:QKH, 0], now(slice(NOPE, QKH)), ACT.Copy))

            def hi_parts(tiles):
                root()
                for m in tiles:
                    act.wait_ge(s_hin, hin.next())
                    act.activation(CNH[:, m], R[:, m], ACT.Copy).then_inc(s_hout, hout.up())
            used(lambda: act.activation(R[:, 0], now(), ACT.Copy))
            hi_parts(range(KQ, KD))
            for m in range(1, KQ):
                used(lambda: act.activation(R[:, m], now(), ACT.Copy))

            def v_tiles():
                act.wait_ge(s_panel, panel_c.next())
                for m in range(4):
                    act.activation(PB[:, m], now(), ACT.Copy).then_inc(s_evac, evac.up())
                split()

            def v_turns(half):
                for m in range(4):
                    act.wait_ge(s_turn, turn.next())
                    f = (4 * half + m) * P
                    act.activation(VM[:, :, f:f + P], now().rearrange("p (t f) -> p t f", t=TT), ACT.Copy).then_inc(s_evac, evac.up())
            v_tiles()
            hi_parts(range(KQ))
            act.wait_ge(s_cn, KD)
            v_turns(0)
            v_tiles()
            v_turns(1)

            def k_product(u):
                act.wait_ge(s_panel, panel_c.next())
                act.activation(KB[0:NOPE, u % 2], BANK[1][0:NOPE, :], ACT.Copy).then_inc(s_evac, evac.up())
                split()

            def q_product(u):
                act.wait_ge(s_qlat, qlat.next())
                act.activation(QB[:, u % 2], BANK[0][0:QKH, :], ACT.Copy).then_inc(s_evac, evac.up())

            def head(u, pair, more=True):
                for qt in QT_ORDER:
                    kv = (qt + 1) * P
                    act.wait_ge(s_max, mx.next())
                    act.activation(PB[:, qt, 0:kv], HEADB[qt][:, 0:kv], ACT.Exp, scale=MLA_SCALE,
                                   bias=NMS[:, qt:qt + 1], accum_out=RSUM[:, qt:qt + 1]).then_inc(s_exp, exp_c.up())
                if more:
                    q_product(u + 1)
                for qt in QT_ORDER:
                    act.wait_ge(s_turn, turn.next())
                    act.activation(PT[:, 0:qt + 1, qt * P:(qt + 1) * P],
                                   HEADB[qt][:, 0:(qt + 1) * P].rearrange("p (k q) -> p k q", q=P), ACT.Copy).then_inc(s_unturn, unturn.up())
                if more:
                    k_product(u + 1)
                if u % 2 == 1:
                    act.wait_ge(s_o, o.next())
                    act.activation(OH[:, pair].rearrange("p a b -> p (a b)"), OB[:, :], ACT.Copy).then_inc(s_oh, oh.up())
            q_product(0)
            k_product(0)
            with loop(act, HEADS // 4 - 1, panels_per(4) + [(evac, 8), (qlat, 4), (mx, 16), (exp_c, 16), (turn, 16), (unturn, 16),
                                                           (o, 2), (oh, 2)]) as i:
                for u in range(4):
                    head(u, col(i * 2 + u // 2))
            for u in range(4):
                head(u, col(HEADS // 2 - 2 + u // 2), more=u < 3)
            out_tiles(KD)

        def ret():
            act.dma_start(RPOS, a["positions"].broadcast_to([P, SEQ])).then_inc(s_pos[1], 16)
            angles(RCOS[:, :], RSIN[:, :])
            n = 4 + 2 * EV
            with loop(act, RH, panels_per(n) + [(evac, n + EV), (ev, 4), (turn, EV), (unturn, EV), (yr, EV), (o, EV), (dec, 16),
                                                (step, 1), (var, 1), (std, 1), (hin, EV), (hout, EV), (sd, TT)]) as i:
                act.wait_ge(s_sd, sd.now())
                act.dma_start(DEC[:, :], a["ret_decay"][col(i)].rearrange("a p q -> (a p) q")).then_inc(s_dec, dec.up(16))
                for _ in range(4):
                    used(to_stage)
                act.wait_ge(s_y, yr.now())

                def place(j):
                    act.wait_ge(s_turn, turn.next())
                    act.activation(V[:, :, j * P:(j + 1) * P], TURN[:, :].rearrange("p (t f) -> p t f", t=TT), ACT.Copy).then_inc(s_unturn, unturn.up())
                for j in range(EV):
                    used(lambda: act.activation(R[:, j], now(), ACT.Copy))
                    if j:
                        place(j - 1)
                place(EV - 1)
                used(lambda: act.activation(R[:, EV], now(), ACT.Silu))
                for j in range(EV):
                    act.wait_ge(s_o, o.next())
                    act.activation(R[:, j], now(), ACT.Copy).then_inc(s_evac, evac.up())
                for j in range(1, EV):
                    used(lambda: act.activation(R[:, EV + j], now(), ACT.Silu))
                root()
                for j in range(EV):
                    act.wait_ge(s_hin, hin.next())
                    act.activation(RYH[:, col(i * EV + j)].rearrange("p a b -> p (a b)"), R[:, j], ACT.Copy).then_inc(s_hout, hout.up())
                sd.at += TT
                yr.at += EV
            out_tiles(KR)

        for kind, j, l in layers:
            if kind == "lru":
                lru(j)
            else:
                (mla if kind == "mla" else ret)()
            lnorm(0, l)
            ffn(l, l == depth - 1)
        for m in range(KD):
            act.wait_ge(s_turn, turn.next())
            act.activation(XT[:, :, m * P:(m + 1) * P], now().rearrange("p (t f) -> p t f", t=TT), ACT.Copy).then_inc(s_evac, evac.up())
        for part in range(OUT_PARTS):
            sl = slice(part * (D // OUT_PARTS), (part + 1) * (D // OUT_PARTS))
            act.wait_ge(s_evac, evac.now(-(OUT_PARTS - 1 - part) * (KD // OUT_PARTS)))
            act.dma_start(out[0, :, sl].rearrange("(t p) d -> p t d", p=P), XT[:, :, sl]).then_inc(s_store, 16)
        act.wait_ge(s_store, 16 * OUT_PARTS)

    @block.vector
    def _(dve):
        evac, ev, step = Count(s_evac, RING), Count(s_ev, RING), Count(s_dve)
        res, xr, xh, x, sums = Count(s_res), Count(s_xr), Count(s_xh), Count(s_x), Count(s_sum)
        stat, dmean, bmean, drstd, brstd = Count(s_stat), Count(s_dmean), Count(s_bmean), Count(s_drstd), Count(s_brstd)
        var, std, hin, hout = Count(s_var), Count(s_std), Count(s_hin), Count(s_hout)
        gelu, g_c, u_c, iu, ta = Count(s_gelu), Count(s_g), Count(s_u), Count(s_iu), Count(s_ta)
        mul, sq, yr, rot, trig = Count(s_mul), Count(s_sq), Count(s_y), Count(s_rot), Count(s_trig)
        cn, kpe, q, sc, mx, exp_c = Count(s_cn), Count(s_kpe), Count(s_q), Count(s_sc), Count(s_max), Count(s_exp)
        prob, oh, ol, sd, dec = Count(s_prob), Count(s_oh), Count(s_ol, 1), Count(s_sd, 2), Count(s_dec)
        staged = [0]
        dve.sem_inc(s_ev, RING)
        dve.sem_inc(s_ol, 1)
        dve.sem_inc(s_sd, 2)

        def par(c):
            return PAR[:, col(c)]

        def next_stage():
            s = staged[0] % RING
            staged[0] += 1
            return s

        dve.memset(ST[:, :, 0:PAD], 0.0).then_inc(s_dve, step.up())
        dve.wait_ge(s_dve, step.now())
        dve.wait_ge(s_evac, evac.next(len(ROW_GROUPS)))
        dve.wait_ge(s_lam, 1)
        dve.tensor_scalar(LAMT[:, 0], LAM[:, :, :], 2.0, None, ALU.add).then_inc(s_dve, step.up())
        dve.wait_ge(s_dve, step.now())
        dve.reciprocal(LAMT[:, 0], LAMT[:, 0]).then_inc(s_dve, step.up())
        dve.wait_ge(s_dve, step.now())
        dve.tensor_tensor(LAMT[:, 0], LAMT[:, 0], LAM[:, :, :], ALU.mult).then_inc(s_dve, step.up())
        dve.wait_ge(s_dve, step.now())
        dve.tensor_tensor(LAMT[:, 1], LAMT[:, 0], LAMT[:, 0], ALU.mult).then_inc(s_dve, step.up())
        dve.wait_ge(s_dve, step.now())
        dve.tensor_scalar(LAMT[:, 2], LAMT[:, 1], 1.0 / 19, None, ALU.mult).then_inc(s_dve, step.up())
        dve.wait_ge(s_dve, step.now())
        for k in (17, 15, 13, 11, 9, 7, 5, 3):
            dve.scalar_tensor_tensor(LAMT[:, 2], LAMT[:, 2], 1.0 / k, LAMT[:, 1], ALU.add, ALU.mult).then_inc(s_dve, step.up())
            dve.wait_ge(s_dve, step.now())
        dve.scalar_tensor_tensor(LAMT[:, 2], LAMT[:, 2], 1.0, LAMT[:, 0], ALU.add, ALU.mult).then_inc(s_dve, step.up())
        dve.wait_ge(s_dve, step.now())
        for j in range(2):
            lam, rate = PC_LRU + j * LRU_COLS + 7 * KD, PC_RATE + j * 2 * KD
            dve.tensor_scalar(LAMT[:, 0, j], PAR[:, lam:lam + KD], -1.0, 0.0, ALU.mult, ALU.max).then_inc(s_dve, step.up())
            dve.wait_ge(s_dve, step.now())
            dve.scalar_tensor_tensor(LAMT[:, 0, j], LAMT[:, 2, j], 2.0, LAMT[:, 0, j], ALU.mult, ALU.add).then_inc(s_dve, step.up())
            dve.wait_ge(s_dve, step.now())
            dve.tensor_scalar(PAR[:, rate:rate + KD], LAMT[:, 0, j], LRU_C, None, ALU.mult).then_inc(s_dve, step.up())
            dve.wait_ge(s_dve, step.now())
            dve.tensor_scalar(PAR[:, rate + KD:rate + 2 * KD], LAMT[:, 0, j], -LRU_C, None, ALU.mult).then_inc(s_dve, step.up())
            dve.wait_ge(s_dve, step.now())
        for m in range(KD):
            dve.wait_ge(s_xh, xh.next())
            dve.wait_ge(s_evac, evac.next())
            dve.tensor_tensor(XL[:, m], R[:, m], XH[:, m].bitcast(F32), ALU.subtract).then_inc(s_x, x.up())
            dve.wait_ge(s_x, x.now())

        def add_sums(kind, tile):
            s1, s2, t = SUMS[kind]
            dve.tensor_tensor(s1, s1, tile, ALU.add).then_inc(s_dve, step.up())
            dve.wait_ge(s_dve, step.now())
            dve.tensor_tensor(t, tile, tile, ALU.mult).then_inc(s_dve, step.up())
            dve.wait_ge(s_dve, step.now())
            dve.tensor_tensor(s2, s2, t, ALU.add).then_inc(s_sum, sums.up())
            dve.wait_ge(s_sum, sums.now())

        def clear_sums(kind):
            dve.memset(SUMS[kind][0], 0.0).then_inc(s_dve, step.up())
            dve.wait_ge(s_dve, step.now())
            dve.memset(SUMS[kind][1], 0.0).then_inc(s_dve, step.up())
            dve.wait_ge(s_dve, step.now())

        def diagonals(dst, values, done):
            for t in range(TT):
                signal = done if t == TT - 1 else step
                dve.tensor_scalar(dst[:, t * P:(t + 1) * P], IDENT[:, :], values[:, t:t + 1], None, ALU.mult).then_inc(signal.sem, signal.up())
                dve.wait_ge(signal.sem, signal.now())

        def inverse_std(n):
            dve.wait_ge(s_stat, stat.next())
            dve.tensor_scalar(MEAN, TURN[:, 0:TT], 1.0 / n, None, ALU.mult).then_inc(s_dve, step.up())
            dve.wait_ge(s_dve, step.now())
            dve.tensor_tensor(TMP4, MEAN, MEAN, ALU.mult).then_inc(s_dve, step.up())
            dve.wait_ge(s_dve, step.now())
            dve.scalar_tensor_tensor(TMP4, TURN[:, TT:2 * TT], 1.0 / n, TMP4, ALU.mult, ALU.subtract).then_inc(s_dve, step.up())
            dve.wait_ge(s_dve, step.now())
            dve.tensor_scalar(TMP4, TMP4, 0.0, LN_EPS, ALU.max, ALU.add).then_inc(s_dve, step.up())
            dve.wait_ge(s_dve, step.now())
            dve.reciprocal(VINV, TMP4).then_inc(s_var, var.up())
            dve.wait_ge(s_var, var.now())
            diagonals(stage(0), MEAN, dmean)
            dve.wait_ge(s_std, std.next())
            diagonals(stage(1), RSTD, drstd)

        def inverse_rms(n):
            dve.wait_ge(s_stat, stat.next())
            dve.tensor_scalar(TMP4, TURN[:, 0:TT], 1.0 / n, RMS_EPS, ALU.mult, ALU.add).then_inc(s_dve, step.up())
            dve.wait_ge(s_dve, step.now())
            dve.reciprocal(VINV, TMP4).then_inc(s_var, var.up())
            dve.wait_ge(s_var, var.now())
            dve.wait_ge(s_std, std.next())
            diagonals(stage(1), RSTD, drstd)
            dve.wait_ge(s_brstd, brstd.next())

        def residual(kind, per_step):
            clear_sums(kind)
            with loop(dve, 2, [(evac, 4), (ev, 4), (sums, 4), (step, 4 * per_step)]) as i:
                for u in range(4):
                    m = i * 4 + u

                    def at(t):
                        return t[:, col(m)].rearrange("p a b -> p (a b)")
                    dve.wait_ge(s_evac, evac.next())
                    s = next_stage()
                    if kind in ("mla", "ret"):
                        dve.scalar_tensor_tensor(at(R), at(XH).bitcast(F32), ALPHA, stage(s), ALU.mult, ALU.add).then_inc(s_ev, ev.up())
                        dve.wait_ge(s_ev, ev.now())
                        dve.scalar_tensor_tensor(at(R), at(XL).bitcast(F32), ALPHA, at(R), ALU.mult, ALU.add).then_inc(s_dve, step.up())
                        dve.wait_ge(s_dve, step.now())
                    else:
                        dve.scalar_tensor_tensor(at(R), at(R), ALPHA, stage(s), ALU.mult, ALU.add).then_inc(s_ev, ev.up())
                        dve.wait_ge(s_ev, ev.now())
                    add_sums(kind, at(R))
            staged[0] += 4

        def norm(last=False):
            inverse_std(D)
            dve.wait_ge(s_bmean, bmean.next())

            def lo(m):
                dve.wait_ge(s_xr, xr.next())
                dve.tensor_tensor(XL[:, m], R[:, m], XH[:, m].bitcast(F32), ALU.subtract).then_inc(s_x, x.up())
                dve.wait_ge(s_x, x.now())
            for m in range(KD):
                dve.tensor_tensor(R[:, m], R[:, m], SUMB[0][:, :], ALU.subtract).then_inc(s_dve, step.up())
                dve.wait_ge(s_dve, step.now())
                if m == 0:
                    dve.wait_ge(s_brstd, brstd.next())
                dve.tensor_tensor(R[:, m], R[:, m], SUMB[1][:, :], ALU.mult).then_inc(s_res, res.up())
                dve.wait_ge(s_res, res.now())
                if m and not last:
                    lo(m - 1)
            if not last:
                lo(KD - 1)

        def conv(dst, s, taps, w, b):
            dve.tensor_scalar(dst, stage(s), par(w(0)), par(b), ALU.mult, ALU.add).then_inc(s_dve, step.up())
            dve.wait_ge(s_dve, step.now())
            for lag in range(1, taps):
                done = ev if lag == taps - 1 else step
                dve.scalar_tensor_tensor(dst, stage(s, lag), par(w(lag)), dst, ALU.mult, ALU.add).then_inc(done.sem, done.up())
                dve.wait_ge(done.sem, done.now())

        def lru(j):
            base = PC_LRU + j * LRU_COLS
            for m in range(KD):
                dve.wait_ge(s_evac, evac.next())
                conv(U[:, m], next_stage(), 4, lambda lag: base + (3 - lag) * KD + m, base + 4 * KD + m)
                dve.tensor_copy(UH[:, m], U[:, m]).then_inc(s_dve, step.up())
                dve.wait_ge(s_dve, step.now())
                dve.tensor_tensor(UL[:, m], U[:, m], UH[:, m].bitcast(F32), ALU.subtract).then_inc(s_u, u_c.up())
                dve.wait_ge(s_u, u_c.now())
            for g in range(LRU_BLOCKS):
                dve.wait_ge(s_evac, evac.next(4))
                for c in (2 * g, 2 * g + 1):
                    dve.tensor_tensor(U[:, c], U[:, c], I[:, c], ALU.mult).then_inc(s_iu, iu.up())
                    dve.wait_ge(s_iu, iu.now())
            for c in range(KD):
                dve.wait_ge(s_ta, ta.next())
                dve.tensor_tensor(stage(3), A[:, c], A[:, c], ALU.mult).then_inc(s_dve, step.up())
                dve.wait_ge(s_dve, step.now())
                dve.scalar_tensor_tensor(I[:, c], stage(3), 1.0, I[:, c], ALU.add, ALU.mult).then_inc(s_mul, mul.up())
                dve.wait_ge(s_mul, mul.now())
            for c in range(KD):
                dve.wait_ge(s_sq, sq.next())
                dve.tensor_tensor(I[:, c], I[:, c], U[:, c], ALU.mult).then_inc(s_dve, step.up())
                dve.wait_ge(s_dve, step.now())
                dve.tensor_tensor_scan(U[:, c], A[:, c], I[:, c], 0.0, ALU.mult, ALU.add).then_inc(s_dve, step.up())
                dve.wait_ge(s_dve, step.now())
                dve.wait_ge(s_evac, evac.next())
                dve.tensor_tensor(U[:, c], U[:, c], GATE[:, c], ALU.mult).then_inc(s_dve, step.up())
                dve.wait_ge(s_dve, step.now())
                dve.tensor_copy(YH[:, c], U[:, c]).then_inc(s_dve, step.up())
                dve.wait_ge(s_dve, step.now())
                dve.tensor_tensor(YL[:, c], U[:, c], YH[:, c].bitcast(F32), ALU.subtract).then_inc(s_y, yr.up())
                dve.wait_ge(s_y, yr.now())
            residual("lru", 2)

        def ffn(l, last):
            base = PC_FFN + l * FFN_COLS
            with loop(dve, NF // 2, [(evac, 4), (ev, 4), (gelu, 2), (g_c, 2), (step, 12)]) as i:
                for u in range(2):
                    f = i * 2 + u
                    for half, dst in enumerate((AG, AU)):
                        dve.wait_ge(s_evac, evac.next())
                        conv(dst[:, :], next_stage(), 3, lambda lag: f + (base + (2 - lag) * 2 * NF + half * NF),
                             f + (base + 6 * NF + half * NF))
                    dve.wait_ge(s_gelu, gelu.next())
                    dve.tensor_tensor(AU[:, :], AU[:, :], AG[:, :], ALU.mult).then_inc(s_dve, step.up())
                    dve.wait_ge(s_dve, step.now())
                    gh, gl = (t[:, col(f)].rearrange("p a b -> p (a b)") for t in (GH, GL))
                    dve.tensor_copy(gh, AU[:, :]).then_inc(s_dve, step.up())
                    dve.wait_ge(s_dve, step.now())
                    dve.tensor_tensor(gl, AU[:, :], gh.bitcast(F32), ALU.subtract).then_inc(s_g, g_c.up())
                    dve.wait_ge(s_g, g_c.now())
            residual("ffn", 2)
            norm(last)

        def angles(pos, k, freq, cos, sin, tmp):
            dve.wait_ge(s_pos[k], 16)
            dve.tensor_copy(cos, pos).then_inc(s_dve, step.up())
            dve.wait_ge(s_dve, step.now())
            dve.tensor_scalar(cos, cos, freq, None, ALU.mult).then_inc(s_dve, step.up())
            dve.wait_ge(s_dve, step.now())
            for dst, turn, done in ((sin, 0.0, step), (cos, 0.25, rot)):
                dve.tensor_scalar(tmp, cos, 1 / TWO_PI, turn, ALU.mult, ALU.add).then_inc(s_dve, step.up())
                dve.wait_ge(s_dve, step.now())
                dve.tensor_scalar(tmp, tmp, ROUND, None, ALU.add).then_inc(s_dve, step.up())
                dve.wait_ge(s_dve, step.now())
                dve.tensor_scalar(tmp, tmp, ROUND, None, ALU.subtract).then_inc(s_dve, step.up())
                dve.wait_ge(s_dve, step.now())
                dve.scalar_tensor_tensor(dst, tmp, -PI2_A, cos, ALU.mult, ALU.add).then_inc(s_dve, step.up())
                dve.wait_ge(s_dve, step.now())
                dve.scalar_tensor_tensor(dst, tmp, -PI2_B, dst, ALU.mult, ALU.add).then_inc(s_dve, step.up())
                dve.wait_ge(s_dve, step.now())
                dve.scalar_tensor_tensor(dst, tmp, -PI2_C, dst, ALU.mult, ALU.add).then_inc(s_dve, step.up())
                dve.wait_ge(s_dve, step.now())
                dve.tensor_scalar(dst, dst, turn * TWO_PI, PI_CLAMP, ALU.add, ALU.min).then_inc(s_dve, step.up())
                dve.wait_ge(s_dve, step.now())
                dve.tensor_scalar(dst, dst, -PI_CLAMP, None, ALU.max).then_inc(done.sem, done.up())
                dve.wait_ge(done.sem, done.now())
            dve.wait_ge(s_trig, trig.next(2))

        rows = slice(NOPE, QKH)
        swap = [(r + ROPE // 2) % ROPE for r in range(ROPE)]

        def mla_rope(t, done):
            dve.sem_inc(s_go, 1)
            dve.stream_shuffle(ROT[rows, :], t, swap).then_inc(s_dve, step.up())
            dve.wait_ge(s_dve, step.now())
            dve.tensor_tensor(ROT[rows, :], ROT[rows, :], MSIN[rows, :], ALU.mult).then_inc(s_dve, step.up())
            dve.wait_ge(s_dve, step.now())
            dve.tensor_tensor(t, t, MCOS[rows, :], ALU.mult).then_inc(s_dve, step.up())
            dve.wait_ge(s_dve, step.now())
            dve.tensor_tensor(t, t, ROT[rows, :], ALU.add).then_inc(done.sem, done.up())
            dve.wait_ge(done.sem, done.now())

        def mla():
            angles(MPOS[:, :], 0, FREQ[:, 0:1], MCOS[:, :], MSIN[:, :], ROT[:, :])
            dve.tensor_scalar(MSIN[:, :], MSIN[:, :], FREQ[:, 2:3], None, ALU.mult).then_inc(s_dve, step.up())
            dve.wait_ge(s_dve, step.now())
            dve.memset(PT[:, 1], 0.0).then_inc(s_dve, step.up())
            dve.wait_ge(s_dve, step.now())
            dve.memset(PT[:, 2], 0.0).then_inc(s_dve, step.up())
            dve.wait_ge(s_dve, step.now())

            def add_square(m):
                dve.wait_ge(s_evac, evac.next())
                acc = PT[:, 2] if m < KQ else PT[:, 1]
                dve.tensor_tensor(PT[:, 0], R[:, m], R[:, m], ALU.mult).then_inc(s_dve, step.up())
                dve.wait_ge(s_dve, step.now())
                dve.tensor_tensor(acc, acc, PT[:, 0], ALU.add).then_inc(s_sum, sums.up())
                dve.wait_ge(s_sum, sums.now())

            def lo(m):
                dve.wait_ge(s_hout, hout.next())
                dve.tensor_tensor(CNL[:, m], R[:, m], CNH[:, m].bitcast(F32), ALU.subtract).then_inc(s_cn, cn.up())
                dve.wait_ge(s_cn, cn.now())

            def latents(tiles):
                for m in tiles:
                    dve.scalar_tensor_tensor(R[:, m], R[:, m], par(PC_MLA + m), SUMB[1][:, :], ALU.mult, ALU.mult).then_inc(s_hin, hin.up())
                    dve.wait_ge(s_hin, hin.now())
                    if m != tiles[0]:
                        lo(m - 1)
                lo(tiles[-1])
            for m in range(KQ, KD):
                add_square(m)
            inverse_rms(KV_LORA)
            latents(range(KQ, KD))
            dve.wait_ge(s_evac, evac.next())
            mla_rope(KB[rows, 0], step)
            dve.tensor_copy(KB[rows, 1], KB[rows, 0]).then_inc(s_kpe, kpe.up())
            dve.wait_ge(s_kpe, kpe.now())
            for m in range(KQ):
                add_square(m)
            inverse_rms(Q_LORA)
            latents(range(KQ))
            evac.at += 2 * KD

            def new_q(u, i):
                dve.wait_ge(s_evac, evac.next())
                mla_rope(QB[rows, u % 2], q)
                evac.at += 1
                dve.tensor_copy(VB[:, u % 2], VM[:, :, col((i * 4 + u) * VH, VH)]).then_inc(s_dve, step.up())
                dve.wait_ge(s_dve, step.now())

            def head(u, i, more=True):
                for n in range(TT + 1):
                    if n < TT:
                        qt = QT_ORDER[n]
                        dve.wait_ge(s_sc, sc.next())
                        dve.tensor_reduce(NM[:, qt:qt + 1], HEADB[qt][:, 0:(qt + 1) * P], AX.X, ALU.max).then_inc(s_dve, step.up())
                        dve.wait_ge(s_dve, step.now())
                        dve.tensor_scalar(NMS[:, qt:qt + 1], NM[:, qt:qt + 1], -MLA_SCALE, None, ALU.mult).then_inc(s_max, mx.up())
                        dve.wait_ge(s_max, mx.now())
                    if n:
                        qt = QT_ORDER[n - 1]
                        dve.wait_ge(s_exp, exp_c.next())
                        dve.reciprocal(RINV[:, qt:qt + 1], RSUM[:, qt:qt + 1]).then_inc(s_dve, step.up())
                        dve.wait_ge(s_dve, step.now())
                        p = PB[:, qt, 0:(qt + 1) * P]
                        dve.tensor_scalar(p, p, RINV[:, qt:qt + 1], None, ALU.mult).then_inc(s_prob, prob.up())
                        dve.wait_ge(s_prob, prob.now())
                if more:
                    new_q(u + 1, i)
                if u % 2 == 1:
                    dve.wait_ge(s_oh, oh.next())
                    o_hi, o_lo = (t[:, col(i * 2 + u // 2)].rearrange("p a b -> p (a b)") for t in (OH, OL))
                    dve.tensor_tensor(o_lo, OB[:, :], o_hi.bitcast(F32), ALU.subtract).then_inc(s_ol, ol.up())
                    dve.wait_ge(s_ol, ol.now())
            dve.wait_ge(s_evac, evac.now())
            new_q(0, 0)
            with loop(dve, HEADS // 4 - 1, [(evac, 8), (q, 4), (sc, 16), (mx, 16), (exp_c, 16), (prob, 16), (oh, 2), (ol, 2),
                                            (step, 4 * (3 + 1 + 4 + 4))]) as i:
                for u in range(4):
                    head(u, i)
            for u in range(4):
                head(u, HEADS // 4 - 1, more=u < 3)
            residual("mla", 3)

        def ret():
            angles(RPOS, 1, FREQ[:, 1:2], RCOS[:, :], RSIN[:, :], RTMP[:, :])
            n = 4 + 2 * EV
            with loop(dve, RH, [(evac, n + EV), (ev, 4), (q, 2), (dec, 16), (sc, TT), (sd, TT), (sums, EV), (stat, 1), (dmean, 1),
                                (bmean, 1), (var, 1), (std, 1), (drstd, 1), (brstd, 1), (hin, EV), (hout, EV), (yr, EV),
                                (step, 2 * 3 + 2 + 2 * EV + 4 + 2 * (TT - 1) + 2 * EV)]) as i:
                for t in (QT, KT):
                    dve.wait_ge(s_evac, evac.next(2))
                    s1, s2 = next_stage(), next_stage()
                    dve.tensor_tensor(t[:, 0], stage(s1), RCOS[:, :], ALU.mult).then_inc(s_dve, step.up())
                    dve.wait_ge(s_dve, step.now())
                    dve.tensor_tensor(RTMP[:, :], stage(s2), RSIN[:, :], ALU.mult).then_inc(s_dve, step.up())
                    dve.wait_ge(s_dve, step.now())
                    dve.tensor_tensor(t[:, 0], t[:, 0], RTMP[:, :], ALU.subtract).then_inc(s_dve, step.up())
                    dve.wait_ge(s_dve, step.now())
                    dve.tensor_tensor(t[:, 1], stage(s1), RSIN[:, :], ALU.mult).then_inc(s_ev, ev.up())
                    dve.wait_ge(s_ev, ev.now())
                    dve.tensor_tensor(RTMP[:, :], stage(s2), RCOS[:, :], ALU.mult).then_inc(s_ev, ev.up())
                    dve.wait_ge(s_ev, ev.now())
                    dve.tensor_tensor(t[:, 1], t[:, 1], RTMP[:, :], ALU.add).then_inc(s_q, q.up())
                    dve.wait_ge(s_q, q.now())
                dve.wait_ge(s_dec, dec.next(16))
                for kt in range(TT):
                    dve.wait_ge(s_sc, sc.next())
                    w = SEQ - kt * P
                    dve.tensor_tensor(SD[:, kt, kt * P:SEQ], SUMB[kt % 2][:, 0:w], DEC[:, 0:w], ALU.mult).then_inc(s_sd, sd.up())
                    dve.wait_ge(s_sd, sd.now())
                evac.at += EV + 1
                clear_sums("ret")
                for j in range(EV):
                    dve.wait_ge(s_evac, evac.next())
                    add_sums("ret", R[:, j])
                inverse_std(RV)
                dve.wait_ge(s_bmean, bmean.next())
                dve.wait_ge(s_brstd, brstd.next())
                dve.wait_ge(s_evac, evac.next(EV - 1))

                def lo(j):
                    dve.wait_ge(s_hout, hout.next())
                    y_hi, y_lo = (t[:, col(i * EV + j)].rearrange("p a b -> p (a b)") for t in (RYH, RYL))
                    dve.tensor_tensor(y_lo, R[:, j], y_hi.bitcast(F32), ALU.subtract).then_inc(s_y, yr.up())
                    dve.wait_ge(s_y, yr.now())
                for j in range(EV):
                    dve.tensor_tensor(R[:, j], R[:, j], SUMB[0][:, :], ALU.subtract).then_inc(s_dve, step.up())
                    dve.wait_ge(s_dve, step.now())
                    dve.tensor_tensor(R[:, j], R[:, j], SUMB[1][:, :], ALU.mult).then_inc(s_dve, step.up())
                    dve.wait_ge(s_dve, step.now())
                    dve.scalar_tensor_tensor(R[:, j], R[:, j], par(i * EV + (PC_RET + j)), R[:, EV + j], ALU.mult, ALU.mult).then_inc(s_hin, hin.up())
                    dve.wait_ge(s_hin, hin.now())
                    if j:
                        lo(j - 1)
                lo(EV - 1)
            residual("ret", 3)

        for kind, j, l in layers:
            if kind == "lru":
                lru(j)
            else:
                (mla if kind == "mla" else ret)()
            norm()
            ffn(l, l == depth - 1)


def constants():
    import numpy as np

    def freq(d):
        return (10000.0 ** (-np.arange(0, d, 2, dtype=np.float64) / d)).astype(np.float32)
    f = np.zeros((P, 4), np.float32)
    f[:, 0] = np.tile(freq(ROPE), 2 * P // ROPE)
    f[:, 1] = freq(RQK)
    f[:, 2] = np.tile(np.repeat([-1.0, 1.0], ROPE // 2), P // ROPE)
    k, q = np.arange(P)[:, None], np.arange(SEQ)[None, :]
    log_gamma = np.log1p(-np.exp2(-5.0 - np.arange(RH, dtype=np.float64)))
    decay = np.exp(log_gamma[:, None, None] * np.abs(q - k)) * (k // CHUNK <= q // CHUNK) * float(RQK) ** -0.5
    return {"rope_freq": f, "ret_decay": decay.astype(np.float32)}


def kernel(**inputs):
    import numpy as np
    import concourse.bacc as bacc
    from concourse.bass_utils import run_bass_kernel_spmd

    nc = bacc.Bacc("TRN2", target_bir_lowering=False, num_devices=1)
    arrays = {n: np.ascontiguousarray(v) for n, v in {**inputs, **constants()}.items()}
    aps = {n: nc.dram_tensor(n, v.shape, mybir.dt.from_np(v.dtype), kind="ExternalInput").ap() for n, v in arrays.items()}
    out = nc.dram_tensor("out", (1, SEQ, D), F32, kind="ExternalOutput").ap()
    build(nc, aps, out)
    r = run_bass_kernel_spmd(nc, [arrays], core_ids=[0])
    return r.results[0]["out"]
```

```python
from contextlib import ExitStack, contextmanager
import math

import concourse.bass as bass
from concourse import mybir

F32 = mybir.dt.float32
F32R = mybir.dt.float32r
I32 = mybir.dt.int32
ALU = mybir.AluOpType
ACT = mybir.ActivationFunctionType
AX = mybir.AxisListType

P = 128
DEPTH = 4
SEQ = 512
D = 1024
KD = D // P
ALPHA = (2.0 * DEPTH) ** 0.25
LN_EPS = 1e-5
RMS_EPS = 1e-6
TT = SEQ // P

DFF = 2816
NF = DFF // P
LRU_BLOCKS = 4
LRU_C = 8.0

HEADS = 16
NOPE, ROPE, VH = 64, 32, 64
QKH = NOPE + ROPE
Q_LORA, KV_LORA = 768, 256
KQ, KKV = Q_LORA // P, KV_LORA // P
MLA_SCALE = float(QKH) ** -0.5
MASKED = -1e30
CHUNK = 64

RH = 4
RQK, RV = D // RH, 2 * D // RH
EV = RV // P
KR = 2 * D // P

RING = 4
PLAIN_GATES = 3
OUT_TILES = 2
Q_EARLY = 2
QT_ORDER = (3, 2, 1, 0)
PAD = 3

PC_LN = 0
PC_LRU = PC_LN + DEPTH * 4 * KD
LRU_COLS = 8 * KD
PC_FFN = PC_LRU + 2 * LRU_COLS
FFN_COLS = 4 * 2 * NF
PC_MLA = PC_FFN + DEPTH * FFN_COLS
PC_RET = PC_MLA + KQ + KKV
PC_RATE = PC_RET + KR
N_PC = PC_RATE + 2 * 2 * KD

ROW_GROUPS = [(4 * DEPTH * KD, PC_LN, [(n, slice(0, DEPTH)) for n in ("ln1_g", "ln1_b", "ln2_g", "ln2_b")])]
for _j in range(2):
    ROW_GROUPS.append((LRU_COLS, PC_LRU + _j * LRU_COLS,
                       [(n, _j) for n in ("lru_conv_w", "lru_conv_b", "lru_b_a", "lru_b_x", "lru_lambda")]))
for _l in range(DEPTH):
    ROW_GROUPS.append((4 * NF, PC_FFN + _l * FFN_COLS, [("ffn_conv_w", (_l, slice(0, 2)))]))
    ROW_GROUPS.append((4 * NF, PC_FFN + _l * FFN_COLS + 4 * NF, [("ffn_conv_w", (_l, slice(2, 3))), ("ffn_conv_b", _l)]))
ROW_GROUPS.append((KQ + KKV + KR, PC_MLA, [("mla_q_norm", 0), ("mla_kv_norm", 0), ("ret_gn_g", 0)]))
N_SMALL = sum(len(v) for _, _, v in ROW_GROUPS) + 1

TWO_PI = 2 * math.pi
ROUND = 1.5 * 2.0 ** 23
PI2_A = 6.28125
PI2_B = round((TWO_PI - PI2_A) * 2.0 ** 20) / 2.0 ** 20
PI2_C = TWO_PI - PI2_A - PI2_B
PI_CLAMP = 3.1415925


class Count:

    def __init__(self, sem, at=0):
        self.sem, self.at, self.roll = sem, at, 0

    def up(self, n=1):
        self.at += n
        return n

    def next(self, n=1):
        self.at += n
        return self.roll + self.at

    def now(self, more=0):
        return self.roll + (self.at + more)


@contextmanager
def loop(eng, times, per):
    first = [c.at for c, _ in per]
    with eng.Fori(0, times) as i:
        for c, n in per:
            c.roll = i * n
        yield i
    for (c, n), at in zip(per, first):
        assert c.at - at == n, (c.sem.name if hasattr(c.sem, "name") else c.sem, c.at - at, n)
        c.at, c.roll = at + times * n, 0


def col(i, n=1):
    return bass.ds(i, n)


def build(nc, a, out, depth=DEPTH):
    with ExitStack() as ctx:
        build_in(nc, a, out, ctx, depth)


def build_in(nc, a, out, ctx, depth):
    def sem(name):
        return ctx.enter_context(nc.semaphore(name))

    def sb(name, shape, dt=F32, on=ctx):
        return on.enter_context(nc.sbuf_tensor(name, shape, dt))

    XH = sb("x_hi", [P, KD, SEQ], F32R)
    XL = sb("x_lo", [P, KD, SEQ], F32R)
    R = sb("residual", [P, KD, SEQ])
    RAW = sb("w_raw", [P, RING, 8, P])
    WH = sb("w_hi", [P, RING, 8, P], F32R)
    WL = sb("w_lo", [P, RING, 8, P], F32R)
    ST = sb("staged", [P, RING, PAD + SEQ])
    PAR = sb("params", [P, N_PC])
    IDENT = sb("ident", [P, P])
    ONES = sb("ones", [P, P])
    FREQ = sb("freq", [P, 4])
    NM = sb("neg_max", [P, TT])
    RSUM = sb("row_sum", [P, TT])
    RINV = sb("row_sum_inv", [P, TT])
    LAM = sb("lambda_exp", [P, 2, KD])
    LAMT = sb("lambda_tmp", [P, 3, 2, KD])
    NORM = sb("norm_small", [P, 5, TT])
    MEAN, SQUARE, TMP4, VINV, RSTD = (NORM[:, i, :] for i in range(5))
    MEANS = NORM[:, 0:2, :].rearrange("p a b -> p (a b)")
    INV_D = sb("one_over_d", [P, 1])
    WARM = sb("table_ahead", [P, 1])
    MROW = sb("mask_row", [1, P + CHUNK])

    def stage(s, lag=0):
        return ST[:, s, PAD - lag:PAD - lag + SEQ]

    with ExitStack() as s:
        XT = sb("x_tokens", [P, TT, D], on=s)
        ROWS = sb("param_rows", [P, 12, P], on=s)
    with ExitStack() as s:
        U = sb("lru_u", [P, KD, SEQ], on=s)
        A = sb("lru_a", [P, KD, SEQ], on=s)
        I = sb("lru_i", [P, KD, SEQ], on=s)
        GATE = sb("lru_gate", [P, KD, SEQ], on=s)
        UH = sb("lru_u_hi", [P, KD, SEQ], F32R, on=s)
        UL = sb("lru_u_lo", [P, KD, SEQ], F32R, on=s)
        YH, YL = UH, UL
    with ExitStack() as s:
        AG = sb("ffn_gate", [P, SEQ], on=s)
        AU = sb("ffn_up", [P, SEQ], on=s)
        AT = sb("ffn_tmp", [P, SEQ], on=s)
        GH = sb("ffn_h_hi", [P, NF, SEQ], F32R, on=s)
        GL = sb("ffn_h_lo", [P, NF, SEQ], F32R, on=s)
    with ExitStack() as s:
        CNH = sb("c_hi", [P, KD, SEQ], F32R, on=s)
        CNL = sb("c_lo", [P, KD, SEQ], F32R, on=s)
        OH = sb("o_hi", [P, KD, SEQ], F32R, on=s)
        OL = sb("o_lo", [P, KD, SEQ], F32R, on=s)
        QB = sb("q_head", [QKH, 2, SEQ], on=s)
        KB = sb("k_head", [QKH, 2, SEQ], on=s)
        PB = sb("probs", [P, TT, SEQ], on=s)
        PT = sb("probs_t", [P, TT, SEQ], on=s)
        MSIN = sb("mla_sin", [P, SEQ], on=s)
        ROT = sb("mla_rot", [P, SEQ], on=s)
        VB = sb("v_head", [P, 2, TT, VH], on=s)
        MCOS = sb("mla_cos", [P, SEQ], on=s)
    with ExitStack() as s:
        sb("under_latents", [P, 2 * KD, SEQ], on=s)
        LAT = sb("latents", [P, KD, SEQ], on=s)
    VM = R[:, :, :].rearrange("p a (b c) -> p (a b c)", b=1).rearrange("p (t f) -> p t f", t=TT)
    with ExitStack() as s:
        RYH = sb("ret_y_hi", [P, KR, SEQ], F32R, on=s)
        RYL = sb("ret_y_lo", [P, KR, SEQ], F32R, on=s)
        QT = sb("ret_q", [P, 2, SEQ], on=s)
        KT = sb("ret_k", [P, 2, SEQ], on=s)
        V = sb("ret_v", [P, TT, RV], on=s)
        SD = sb("ret_scores", [P, TT, SEQ], on=s)
        RTMP = sb("ret_tmp", [P, SEQ], on=s)
        RSQ = sb("ret_square", [P, SEQ], on=s)
        DEC = sb("decay_table", [P, SEQ], on=s)
        RCOS = sb("ret_cos", [P, SEQ], on=s)

    SUMS = {
        "lru": (A[:, 0, :], A[:, 1, :], A[:, 2, :]),
        "ffn": (AG[:, :], AU[:, :], AT[:, :]),
        "mla": (PB[:, 0, :], PB[:, 1, :], PT[:, 0, :]),
        "ret": (QT[:, 0, :], QT[:, 1, :], RSQ[:, :]),
    }

    BANK = [ctx.enter_context(nc.psum_tensor(f"bank{i}", [P, SEQ], F32)) for i in range(8)]
    SUMB = BANK[4:6]
    HEADB = BANK[2:6]
    TURN = BANK[6]
    OB = BANK[7]
    RSIN = OB

    s_raw = [sem(f"raw_loaded{i}") for i in range(RING)]
    s_rawk = [sem(f"raw_second_loaded{i}") for i in range(RING)]
    s_small = sem("small_loaded")
    s_xin = [sem(f"x_loaded{i}") for i in range(KD // 2)]
    s_pos = [sem("mla_pos_loaded"), sem("ret_pos_loaded")]
    s_dec = sem("decay_loaded")
    s_const = sem("consts_made")
    s_hi = sem("w_hi_done")
    s_lo = sem("w_lo_done")
    s_panel = sem("panel_done")
    s_evac = sem("evac_done")
    s_ev = sem("staged_used")
    s_act = sem("act_step")
    s_dve = sem("dve_step")
    s_turn = sem("turned")
    s_unturn = sem("turn_read")
    s_lam = sem("lambda_exp")
    s_res = sem("x_normal")
    s_xh = sem("x_hi_done")
    s_xr = sem("x_new")
    s_x = sem("x_ready")
    s_gelu = sem("gelu_done")
    s_g = sem("hidden_ready")
    s_u = sem("u_ready")
    s_iu = sem("iu_done")
    s_ta = sem("decay_done")
    s_mul = sem("mult2_done")
    s_sq = sem("mult_done")
    s_y = sem("y_ready")
    s_sum = sem("sums_ready")
    s_stat = sem("sums_reduced")
    s_mean = sem("mean_made")
    s_bmean = sem("mean_spread")
    s_smean = sem("mean_in_sbuf")
    s_cen = sem("centred")
    s_var = sem("inverse_variance")
    s_std = sem("inverse_deviation")
    s_brstd = sem("deviation_spread")
    s_hin = sem("norm_tile")
    s_hout = sem("norm_tile_hi")
    s_rot = sem("rope_ready")
    s_trig = sem("trig_ready")
    s_cn = sem("latent_ready")
    s_kpe = sem("k_pe_ready")
    s_q = sem("q_ready")
    s_sc = sem("scores_done")
    s_max = sem("max_done")
    s_exp = sem("exp_done")
    s_part = sem("part_of_panel_done")
    s_prob = sem("probs_ready")
    s_o = sem("o_done")
    s_oh = sem("o_hi_done")
    s_ol = sem("o_ready")
    s_sd = sem("decayed_ready")
    s_go = sem("shuffle_may_go")
    s_store = sem("out_stored")

    ANGLES = {"mla": (MCOS, FREQ[:, 0:1], s_pos[0]), "ret": (RCOS, FREQ[:, 1:2], s_pos[1])}

    block = ctx.enter_context(nc.Block())
    KINDS = ["lru", "mla", "ret"]
    layers = [(KINDS[i % 3], i // 3, i) for i in range(depth)]

    @block.sync
    def _(sp):
        n_panel = [0]
        lo = Count(s_lo)

        def slot():
            k = n_panel[0]
            n_panel[0] += 1
            if k >= RING:
                sp.wait_ge(s_lo, lo.next())
            return k % RING

        def x_in(tiles):
            for m in tiles:
                sp.dma_start(XT[:, :, m * P:(m + 2) * P],
                             a["x"][0, :, m * P:(m + 2) * P].rearrange("(t p) d -> p t d", p=P)).then_inc(s_xin[m // 2], 16)

        def panel(src, blocks=8, cols=P):
            s, half = slot(), blocks // 2
            sp.dma_start(RAW[:, s, 0:half, 0:cols], src[:, 0:half]).then_inc(s_raw[s], 16)
            sp.dma_start(RAW[:, s, half:blocks, 0:cols], src[:, half:blocks]).then_inc(s_rawk[s], 16)
            if n_panel[0] == 1:
                x_in(range(KD // 2, KD, 2))

        def ks(w):
            return w.rearrange("(c p) m -> p c m", p=P)

        def vectors_in():
            for n, (rows, _, vectors) in enumerate(ROW_GROUPS):
                r = 0
                for name, pick in vectors:
                    src = a[name][pick] if not isinstance(pick, tuple) else a[name][pick[0], pick[1]]
                    dims = len(src.shape)
                    names = "abc"[:dims - 1]
                    flat = src.rearrange(f"{' '.join(names)} (t p) -> ({' '.join(names)} t) p", p=P) if dims > 1 else \
                        src.rearrange("(t p) -> t p", p=P)
                    k = flat.shape[0]
                    sp.dma_start(ROWS[r:r + k, n, :], flat).then_inc(s_small, 16)
                    r += k
                assert r == rows
            sp.dma_start(FREQ[:, :], a["rope_freq"]).then_inc(s_small, 16)

        def panels(times, per, load):
            start = 0
            if n_panel[0] == 0:
                load(0)
                vectors_in()
                start = 1
            if start < times:
                before = n_panel[0]
                at = lo.at
                with sp.Fori(start, times) as i:
                    lo.roll = (i - start) * per
                    load(i)
                assert n_panel[0] - before == per
                n_panel[0] = before + (times - start) * per
                lo.at, lo.roll = at + (times - start) * per, 0

        def lru(j):
            w = ks(a["lru_w_in"][j])

            def four(i, base):
                for u in range(4):
                    panel(w[:, :, col(base + i * (4 * P) + u * P, P)])
            panels(2, 4, lambda i: four(i, D))
            for g in range(LRU_BLOCKS):
                s = slot()
                for n, name in enumerate(("lru_w_a", "lru_w_x")):
                    src = a[name][j, g].rearrange("(k p) (m c) -> p k m c", p=P, c=P)
                    q = (s_raw, s_rawk)[n][s]
                    sp.dma_start(RAW[:, s, 4 * n:4 * n + 4, :].rearrange("p (k m) c -> p k m c", k=2), src).then_inc(q, 16)
            panels(2, 4, lambda i: four(i, 0))
            wo = ks(a["lru_w_out"][j])
            panels(2, 4, lambda i: [panel(wo[:, :, col(i * (4 * P) + u * P, P)]) for u in range(4)])

        def mla(j):
            w = ks(a["mla_w_in"][j])
            for m in range(KQ, KD):
                panel(w[:, :, m * P:(m + 1) * P])
            panel(w[:, :, Q_LORA + KV_LORA - NOPE:Q_LORA + KV_LORA + ROPE], 8, QKH)
            for m in range(KQ):
                panel(w[:, :, m * P:(m + 1) * P])
            wkv = a["mla_w_ukv"][j].rearrange("(k p) (h two c) -> p k h two c", p=P, two=2, c=NOPE)
            for half in range(2):
                s = slot()
                for k in range(KKV):
                    q = (s_raw, s_rawk)[k][s]
                    sp.dma_start(RAW[:, s, 4 * k:4 * k + 4, :].rearrange("p m (t c) -> p (m t) c", c=VH),
                                 wkv[:, k, 8 * half:8 * half + 8, 1, :]).then_inc(q, 16)
            wq = ks(a["mla_w_uq"][j])
            wk = ks(a["mla_w_ukv"][j])

            def head(h):
                s = slot()
                sp.dma_start(RAW[:, s, 0:KQ, 0:QKH], wq[:, :, col(h * QKH, QKH)]).then_inc(s_raw[s], 16)
                sp.dma_start(RAW[:, s, KQ:8, 0:NOPE], wk[:, :, col(h * (2 * NOPE), NOPE)]).then_inc(s_rawk[s], 16)
            panels(HEADS // 4, 4, lambda i: [head(i * 4 + u) for u in range(4)])
            wo = ks(a["mla_w_out"][j])
            panels(2, 4, lambda i: [panel(wo[:, :, col(i * (4 * P) + u * P, P)]) for u in range(4)])

        def ret(j):
            w = ks(a["ret_w_in"][j])

            def head(h):
                for u in range(2):
                    panel(w[:, :, col(h * RQK + u * P, P)])
                for u in range(2):
                    panel(w[:, :, col(h * RQK + (D + u * P), P)])
                for base in (2 * D, 4 * D):
                    for u in range(EV):
                        panel(w[:, :, col(h * RV + (base + u * P), P)])
            panels(RH, 4 + 2 * EV, head)
            wo = ks(a["ret_w_out"][j])

            def four(i):
                for pair in range(2):
                    for half in range(2):
                        for u in (2 * pair, 2 * pair + 1):
                            panel(wo[:, 8 * half:8 * half + 8, col(i * (4 * P) + u * P, P)])
            panels(2, 8, four)

        def ffn(l):
            w = ks(a["ffn_w_up"][l])
            panels(NF // 2, 4, lambda i: [panel(w[:, :, col(i * (2 * P) + (u * P + half * DFF), P)])
                                          for u in range(2) for half in range(2)])
            wo = ks(a["ffn_w_down"][l])

            def four(i):
                for u in range(4):
                    for c0 in range(0, NF, 8):
                        c1 = min(NF, c0 + 8)
                        panel(wo[:, c0:c1, col(i * (4 * P) + u * P, P)], c1 - c0)
            panels(2, 12, four)

        x_in(range(0, KD // 2, 2))
        for kind, j, l in layers:
            {"lru": lru, "mla": mla, "ret": ret}[kind](j)
            ffn(l)

    PANELS = {"lru": 4 * KD - LRU_BLOCKS, "mla": 2 * KD + 1 + 2 + HEADS, "ret": RH * (4 + 2 * EV) + 2 * KD,
              "ffn": 2 * NF + KD * ((NF + 7) // 8)}
    NPAN = sum(PANELS[kind] + PANELS["ffn"] for kind, _, _ in layers)

    @block.gpsimd
    def _(pool):
        con = Count(s_const)
        pool.memset(IDENT[:, :], 0.0).then_inc(s_const, con.up())
        pool.memset(ONES[:, :], 1.0).then_inc(s_const, con.up())
        pool.memset(INV_D[:, :], 1.0 / D).then_inc(s_const, con.up())
        pool.memset(MROW[:, 0:CHUNK], 1.0).then_inc(s_const, con.up())
        pool.memset(MROW[:, CHUNK:P], 0.0).then_inc(s_const, con.up())
        pool.memset(MROW[:, P:P + CHUNK], MASKED).then_inc(s_const, con.up())
        pool.wait_ge(s_const, con.now())
        pool.affine_select(out=IDENT[:, :], in_=IDENT[:, :], compare_op=ALU.not_equal, fill=1.0,
                                    base=0, pattern=[[-1, P]], channel_multiplier=1).then_inc(s_const, con.up())
        hi, lo = Count(s_hi), Count(s_lo)

        def part(s):
            pool.wait_ge(s_hi, hi.next())
            pool.tensor_tensor(WL[:, s], RAW[:, s], WH[:, s].bitcast(F32), ALU.subtract).then_inc(s_lo, lo.up())

        def lo_parts(upto):
            n = upto - lo.at
            if n >= RING:
                with loop(pool, n // RING, [(hi, RING), (lo, RING)]):
                    for _ in range(RING):
                        part(lo.at % RING)
            for _ in range(n % RING):
                part(lo.at % RING)
        smean, cen = Count(s_smean), Count(s_cen)
        end = 0
        for kind, _, _ in layers:
            for section in (kind, "ffn"):
                end += PANELS[section]
                lo_parts(min(NPAN, end + RING))
                pool.wait_ge(s_smean, smean.next())
                for m in range(1, KD):
                    pool.tensor_tensor(R[:, m], R[:, m], stage(0), ALU.subtract).then_inc(s_cen, cen.up())

    @block.tensor
    def _(pe):
        lo, panel_c, bank = Count(s_lo), Count(s_panel), Count(s_evac)
        xr, turn, unturn = Count(s_x), Count(s_turn), Count(s_unturn)
        stat, sums, yr = Count(s_stat), Count(s_sum), Count(s_y)
        mean, bmean, std, brstd = Count(s_mean), Count(s_bmean), Count(s_std), Count(s_brstd)
        q, sc, prob, part = Count(s_q), Count(s_sc), Count(s_prob), Count(s_part)
        o, ol, sd = Count(s_o), Count(s_ol), Count(s_sd)
        x_at = [0]

        def take_panel():
            s = lo.at % RING
            pe.wait_ge(s_lo, lo.next())
            return s

        def take_bank():
            b = BANK[bank.at % RING]
            pe.wait_ge(s_evac, bank.next())
            return b

        def product(ps, s, c, m, xh, xl, first, last):
            pe.matmul(ps, WL[:, s, c, 0:m], xh, start=first, stop=False)
            pe.matmul(ps, WH[:, s, c, 0:m], xl, start=False, stop=False)
            return pe.matmul(ps, WH[:, s, c, 0:m], xh, start=False, stop=last)

        def tile(xh, xl, blocks, m=P, ready=None):
            b = take_bank()
            for c in range(blocks):
                if c % 8 == 0:
                    s = take_panel()
                if ready is not None:
                    ready(c)
                last = product(b[0:m, :], s, c % 8, m, xh[:, c, :], xl[:, c, :], c == 0, c == blocks - 1)
                if c % 8 == 7 or c == blocks - 1:
                    last.then_inc(s_panel, panel_c.up())

        def x_ready(c):
            pe.wait_ge(s_x, x_at[0] - KD + c + 1)

        def first_tiles(rows=(P, P, P), xh=XH, xl=XL, ready=x_ready):
            slots, banks = [take_panel() for _ in rows], [take_bank() for _ in rows]
            for c in range(KD):
                ready(c)
                for s, b, m in zip(slots, banks, rows):
                    last = product(b[0:m, :], s, c, m, xh[:, c, :], xl[:, c, :], c == 0, c == KD - 1)
                    if c == KD - 1:
                        last.then_inc(s_panel, panel_c.up())

        def x_tiles(times):
            with loop(pe, times, [(lo, 4), (bank, 4), (panel_c, 4)]):
                for _ in range(4):
                    tile(XH, XL, KD)

        def out_tiles(xh, xl, blocks, ready):
            n = 4 * ((blocks + 7) // 8)
            with loop(pe, 2, [(lo, n), (bank, 4), (panel_c, n)]):
                for u in range(4):
                    tile(xh, xl, blocks, ready=ready if u == 0 else None)

        def token_sums(sources, n, at=None, weight=ONES):
            pe.wait_ge(s_sum, sums.next(n))
            if at is None:
                at = TURN
                pe.wait_ge(s_unturn, unturn.now(1))
            for i, src in enumerate(sources):
                for t in range(TT):
                    c = i * TT + t
                    ins = pe.matmul(at[:, c:c + 1], src[:, t * P:(t + 1) * P], weight[:, 0:1], start=True, stop=True)
            return ins

        def spread(bank, values):
            for t in range(TT):
                ins = pe.matmul(bank[:, t * P:(t + 1) * P], values[:, t:t + 1].broadcast_to([P, P]), IDENT[:, :],
                                start=True, stop=True)
            return ins

        def spread_mean():
            pe.wait_ge(s_mean, mean.next())
            spread(SUMB[0], MEAN).then_inc(s_bmean, bmean.up())

        def spread_rstd():
            pe.wait_ge(s_std, std.next())
            spread(SUMB[1], RSTD).then_inc(s_brstd, brstd.up())

        def norm(kind):
            s1, s2, square = SUMS[kind]
            token_sums([s1, s2], KD - 1, weight=INV_D).then_inc(s_stat, stat.up())
            token_sums([R[:, KD - 1]], 1, at=SUMB[0], weight=INV_D)
            token_sums([square], 1, at=SUMB[0][:, TT:2 * TT], weight=INV_D).then_inc(s_stat, stat.up())
            spread_mean()
            spread_rstd()
            x_at[0] += KD

        def take_turn():
            pe.wait_ge(s_unturn, unturn.next())

        pe.wait_ge(s_const, 7)
        for m in range(KD):
            if m % 2 == 0:
                pe.wait_ge(s_xin[m // 2], 16)
            b = take_bank()
            for t in range(TT):
                ins = pe.transpose(b[:, t * P:(t + 1) * P], XT[:, t, m * P:(m + 1) * P], IDENT[:, :])
            ins.then_inc(s_turn, turn.up())
        x_at[0] += KD

        def turn_params():
            pe.wait_ge(s_small, 16 * N_SMALL)
            for n, (rows, _, _) in enumerate(ROW_GROUPS):
                b = take_bank()
                pe.transpose(b[:, 0:rows], ROWS[0:rows, n, :], IDENT[0:rows, 0:rows]).then_inc(s_turn, turn.up())

        def lru(j):
            if j == 0:
                for m in range(3):
                    tile(XH, XL, KD, ready=None if m else x_ready)
                turn_params()
            else:
                first_tiles()
            for _ in range(KD - 3):
                tile(XH, XL, KD)
            for g in range(LRU_BLOCKS):
                pe.wait_ge(s_u, lru_u[0] + 2 * g + 2)
                s = take_panel()
                for n in range(4):
                    b = take_bank()
                    for k in range(2):
                        c = 4 * (n // 2) + 2 * k + n % 2
                        last = product(b[:, :], s, c, P, UH[:, 2 * g + k, :], UL[:, 2 * g + k, :], k == 0, k == 1)
                    if n == 1:
                        last.then_inc(s_part, part.up())
                last.then_inc(s_panel, panel_c.up())
            lru_u[0] += KD
            x_tiles(2)
            base = yr.at
            first_tiles(xh=YH, xl=YL, ready=lambda c: pe.wait_ge(s_y, base + c + 1))
            for _ in range(KD - 3):
                tile(YH, YL, KD)
            yr.at += KD
            norm("lru")
        lru_u = [0]

        def ffn():
            first_tiles()
            tile(XH, XL, KD)
            x_tiles(NF // 2 - 1)
            base = hid[0]
            out_tiles(GH, GL, NF, lambda c: pe.wait_ge(s_g, base + c + 1))
            hid[0] += NF
            norm("ffn")
        hid = [0]

        def mla():
            first_tiles((P, P, QKH))
            tile(XH, XL, KD)
            token_sums([PT[:, 1, :]], KKV).then_inc(s_stat, stat.up())
            tile(XH, XL, KD)
            spread_rstd()
            for _ in range(KQ - 2):
                tile(XH, XL, KD)
            pe.wait_ge(s_cn, KKV)

            def v_tile(s, t):
                b, tok = take_bank(), slice(t * P, (t + 1) * P)
                for k in range(KKV):
                    w_hi, w_lo = (w[:, s, 4 * k:4 * k + 4, :].rearrange("p a b -> p (a b)") for w in (WH, WL))
                    pe.matmul(b[:, :], CNL[:, KQ + k, tok], w_hi, start=k == 0, stop=False)
                    pe.matmul(b[:, :], CNH[:, KQ + k, tok], w_lo, start=False, stop=False)
                    last = pe.matmul(b[:, :], CNH[:, KQ + k, tok], w_hi, start=False, stop=k == KKV - 1)
                return last
            s = take_panel()
            v_tile(s, 0)
            token_sums([PT[:, 2, :]], KQ).then_inc(s_stat, stat.up())
            v_tile(s, 1)
            spread_rstd()
            v_tile(s, 2)
            v_tile(s, 3).then_inc(s_panel, panel_c.up())
            s = take_panel()
            for t in range(TT):
                last = v_tile(s, t)
            last.then_inc(s_panel, panel_c.up())
            pe.wait_ge(s_cn, KD)
            for i in range(2):
                pe.wait_ge(s_evac, RING + bank.at - (bank.at - 1 - i) % RING)

            def q_product(s, blocks):
                for c in blocks:
                    last = product(BANK[0][0:QKH, :], s, c, QKH, CNH[:, c, :], CNL[:, c, :], c == 0, c == KQ - 1)
                if c == KQ - 1:
                    last.then_inc(s_part, part.up())

            def k_product(s):
                for k in range(KKV):
                    last = product(BANK[1][0:NOPE, :], s, KQ + k, NOPE, CNH[:, KQ + k, :], CNL[:, KQ + k, :],
                                   k == 0, k == KKV - 1)
                last.then_inc(s_panel, panel_c.up())
                bank.at += 2

            def head(u, more=True):
                if more:
                    s = take_panel()
                    pe.wait_ge(s_evac, bank.now(RING - 1))
                    q_product(s, range(Q_EARLY))
                pe.wait_ge(s_evac, bank.now(RING))
                pe.wait_ge(s_q, q.next())
                for qt in QT_ORDER:
                    kv, b = (qt + 1) * P, HEADB[qt]
                    pe.matmul(b[:, 0:kv], QB[:, u % 2, qt * P:(qt + 1) * P], KB[:, u % 2, 0:kv], start=True, stop=False)
                    pe.matmul(b[:, kv - CHUNK:kv], MROW[0:1, 0:P], MROW[0:1, P:P + CHUNK], start=False, stop=True).then_inc(s_sc, sc.up())
                if more:
                    q_product(s, range(Q_EARLY, KQ))
                for qt in QT_ORDER:
                    pe.wait_ge(s_prob, prob.next())
                    for kt in range(qt + 1):
                        ins = pe.transpose(HEADB[qt][:, kt * P:(kt + 1) * P], PB[:, qt, kt * P:(kt + 1) * P], IDENT[:, :])
                    ins.then_inc(s_turn, turn.up())
                if more:
                    k_product(s)
                unturn.at += TT
                pe.wait_ge(s_unturn, unturn.now(1))
                if u % 2 == 0:
                    pe.wait_ge(s_ol, ol.next())
                r0 = VH * (u % 2)
                for kt in range(TT):
                    ins = pe.matmul(OB[r0:r0 + VH, kt * P:SEQ], VB[:, u % 2, kt, :], PT[:, kt, kt * P:SEQ],
                                    start=kt == 0, stop=kt == TT - 1)
                if u % 2 == 1:
                    ins.then_inc(s_o, o.up())
            s = take_panel()
            q_product(s, range(KQ))
            k_product(s)
            pe.wait_ge(s_kpe, 1)
            head(0)
            head(1)
            with loop(pe, HEADS // 4 - 1, [(lo, 4), (bank, 8), (panel_c, 4), (part, 4), (q, 4), (sc, 16),
                                           (prob, 16), (turn, 16), (unturn, 16), (o, 2), (ol, 2)]):
                for u in range(4):
                    head(u)
            head(0)
            head(1, more=False)
            out_tiles(OH, OL, KD, lambda c: pe.wait_ge(s_ol, 1 + c + 1))
            norm("mla")

        def ret():
            n = 4 + 2 * EV

            def turn_v(j):
                pe.wait_ge(s_evac, bank.roll + (RING + bank.at - 1))
                take_turn()
                for t in range(TT):
                    ins = pe.transpose(TURN[:, t * P:(t + 1) * P], R[:, j, t * P:(t + 1) * P], IDENT[:, :])
                ins.then_inc(s_turn, turn.up())
            with loop(pe, RH, [(lo, n), (bank, n + EV), (panel_c, n), (turn, EV), (unturn, EV), (q, 2), (sd, TT), (sc, TT),
                               (o, EV), (sums, EV), (stat, 1), (mean, 1), (bmean, 1), (std, 1), (brstd, 1)]):
                first_tiles()
                tile(XH, XL, KD)
                tile(XH, XL, KD)
                for j in range(1, EV):
                    tile(XH, XL, KD)
                    turn_v(j - 1)
                pe.wait_ge(s_q, q.next(2))
                for kt in range(TT):
                    if kt == 2:
                        turn_v(EV - 1)
                    b = SUMB[kt % 2]
                    pe.wait_ge(s_sd, sd.next())
                    for c in range(2):
                        ins = pe.matmul(b[:, 0:SEQ - kt * P], KT[:, c, kt * P:(kt + 1) * P], QT[:, c, kt * P:SEQ],
                                        start=c == 0, stop=c == 1)
                    ins.then_inc(s_sc, sc.up())
                tile(XH, XL, KD)
                pe.wait_ge(s_unturn, unturn.now(1))
                pe.wait_ge(s_sd, sd.now(2))
                for j in range(EV):
                    b = take_bank()
                    for kt in range(TT):
                        ins = pe.matmul(b[:, kt * P:SEQ], V[:, kt, j * P:(j + 1) * P], SD[:, kt, kt * P:SEQ],
                                        start=kt == 0, stop=kt == TT - 1)
                    ins.then_inc(s_o, o.up())
                for _ in range(EV - 2):
                    tile(XH, XL, KD)
                token_sums(SUMS["ret"][0:2], EV).then_inc(s_stat, stat.up())
                tile(XH, XL, KD)
                spread_mean()
                spread_rstd()
            base = yr.at
            with loop(pe, 2, [(lo, 8), (bank, 4), (panel_c, 8)]):
                for pair in range(2):
                    b = [take_bank(), take_bank()]
                    for half in range(2):
                        for u in range(2):
                            s = take_panel()
                            for k in range(8):
                                c = 8 * half + k
                                if pair == 0 and u == 0:
                                    pe.wait_ge(s_y, base + c + 1)
                                last = product(b[u][:, :], s, k, P, RYH[:, c, :], RYL[:, c, :], c == 0, c == KR - 1)
                            last.then_inc(s_panel, panel_c.up())
            yr.at += KR
            norm("ret")

        for kind, j, l in layers:
            lru(j) if kind == "lru" else (mla if kind == "mla" else ret)()
            ffn()
        for m in range(KD):
            pe.wait_ge(s_xr, x_at[0] - 2 * KD + m + 1)
            b = take_bank()
            for t in range(TT):
                ins = pe.transpose(b[:, t * P:(t + 1) * P], R[:, m, t * P:(t + 1) * P], IDENT[:, :])
            ins.then_inc(s_turn, turn.up())

    @block.scalar
    def _(act):
        hi, panel_c, evac, ev = Count(s_hi), Count(s_panel), Count(s_evac, RING), Count(s_ev)
        raw = [Count(q) for q in s_raw + s_rawk]
        step, res, xh = Count(s_act), Count(s_res), Count(s_xh)
        turn, unturn = Count(s_turn), Count(s_unturn, 1)
        var, std, bmean, smean = Count(s_var), Count(s_std), Count(s_bmean), Count(s_smean)
        part = Count(s_part)
        hin, hout, gelu = Count(s_hin), Count(s_hout), Count(s_gelu)
        iu, ta, mul, sq, yr = Count(s_iu), Count(s_ta), Count(s_mul), Count(s_sq), Count(s_y)
        rot, trig, dec = Count(s_rot), Count(s_trig), Count(s_dec)
        q, mx, exp_c, o, oh = Count(s_q), Count(s_max), Count(s_exp), Count(s_o), Count(s_oh)
        sd = Count(s_sd, 2)
        act.sem_inc(s_unturn, 1)

        def split():
            if hi.at == NPAN:
                return
            s = hi.at % RING
            act.wait_ge(s_raw[s], raw[s].next(16))
            act.wait_ge(s_rawk[s], raw[RING + s].next(16))
            act.activation(WH[:, s], RAW[:, s], ACT.Copy).then_inc(s_hi, hi.up())

        def panels_per(n):
            return [(hi, n), (panel_c, n)] + [(c, 16 * n // RING) for c in raw]

        def used(*evacs):
            act.wait_ge(s_panel, panel_c.next())
            for e in evacs:
                e().then_inc(s_evac, evac.up())
            split()

        def to_stage():
            b, s = BANK[(evac.at - RING) % RING], ev.at % RING
            act.wait_ge(s_ev, ev.next())
            return act.activation(stage(s), b[:, :], ACT.Copy)

        def now(rows=slice(0, P)):
            return BANK[(evac.at - RING) % RING][rows, :]

        def par(c):
            return PAR[:, col(c)]

        for m in range(KD):
            act.wait_ge(s_evac, evac.next())
            act.activation(XH[:, m], R[:, m], ACT.Copy).then_inc(s_xh, xh.up())
            turn.up()
            if m % 2 == 1:
                split()

        def root():
            act.wait_ge(s_act, step.now())
            act.activation(WARM[:, :], ONES[:, 0:1], ACT.Sqrt).then_inc(s_act, step.up())
            act.wait_ge(s_var, var.next())
            act.activation(RSTD, VINV, ACT.Sqrt).then_inc(s_std, std.up())

        def norm(gain, shift, last=False):
            def result(m):
                act.wait_ge(s_turn, turn.next())
                act.activation(XT[:, :, m * P:(m + 1) * P], now().rearrange("p (t f) -> p t f", t=TT), ACT.Copy).then_inc(s_evac, evac.up())
                if (m + 1) % OUT_TILES == 0:
                    sl = slice((m + 1 - OUT_TILES) * P, (m + 1) * P)
                    act.wait_ge(s_evac, evac.now())
                    act.dma_start(out[0, :, sl].rearrange("(t p) d -> p t d", p=P), XT[:, :, sl]).then_inc(s_store, 16)
            root()
            act.wait_ge(s_bmean, bmean.next())
            act.activation(stage(0), SUMB[0][:, :], ACT.Copy).then_inc(s_smean, smean.up())
            for m in range(KD):
                if last:
                    result(m)
                else:
                    act.wait_ge(s_res, res.next())
                    act.activation(XH[:, m], stage(2 + m % 2), ACT.Identity, scale=par(gain + m), bias=par(shift + m)).then_inc(s_xh, xh.up())

        def lnorm(which, l, last=False):
            c = PC_LN + 2 * which * DEPTH * KD + l * KD
            norm(c, c + DEPTH * KD, last)

        def x_tiles(times, each, e):
            with loop(act, times, panels_per(each) + [(evac, each), (ev, each if e is to_stage else 0)]):
                for _ in range(each):
                    used(e)

        def out_tiles(blocks, tables=None, paired=False):
            n = (blocks + 7) // 8
            for m in range(KD):
                if paired:
                    if m % 2 == 0:
                        used()
                        used()
                    if m < KD - 1:
                        used(to_stage)
                    else:
                        used()
                        evac.up()
                    continue
                if m == 1 and tables:
                    angles(tables[0][:, :], OB[:, :])
                for _ in range(n - 1):
                    used()
                if m < KD - 1:
                    used(to_stage)
                else:
                    used()
                    evac.up()

        def place_params():
            for n, (rows, c0, _) in enumerate(ROW_GROUPS):
                act.wait_ge(s_turn, turn.next())
                act.activation(PAR[:, c0:c0 + rows], now()[:, 0:rows], ACT.Copy).then_inc(s_evac, evac.up())
            act.wait_ge(s_evac, evac.now())
            for j in range(2):
                lam = PC_LRU + j * LRU_COLS + 7 * KD
                act.activation(LAM[:, j, :], PAR[:, lam:lam + KD], ACT.Abs).then_inc(s_act, step.up())
            act.wait_ge(s_act, step.now())
            act.activation(LAM[:, :, :], LAM[:, :, :], ACT.Exp, scale=-1.0).then_inc(s_lam, 1)

        def lru(j):
            base, rate = PC_LRU + j * LRU_COLS, PC_RATE + j * 2 * KD
            if j == 0:
                for _ in range(3):
                    used(to_stage)
                place_params()
            for _ in range(3 if j == 0 else 0, KD):
                used(to_stage)
            for g in range(LRU_BLOCKS):
                for n, (gate, half) in enumerate(((A, s_part), (I, s_panel))):
                    act.wait_ge(half, (part, panel_c)[n].next())
                    for m in range(2):
                        act.activation(gate[:, 2 * g + m], now(), ACT.Sigmoid,
                                       bias=par(base + (5 + n) * KD + 2 * g + m)).then_inc(s_evac, evac.up())
                split()
            for c in range(KD):
                act.wait_ge(s_iu, iu.next())
                act.activation(I[:, c], A[:, c], ACT.Tanh, scale=par(rate + c))
                act.activation(A[:, c], A[:, c], ACT.Exp, scale=par(rate + KD + c)).then_inc(s_ta, ta.up())
            for c in range(2):
                used(lambda: act.activation(GATE[:, c], now(), ACT.Copy))
            for c in range(KD):
                act.wait_ge(s_mul, mul.next())
                act.activation(I[:, c], I[:, c], ACT.Sqrt).then_inc(s_sq, sq.up())
            for c in range(2, PLAIN_GATES):
                used(lambda: act.activation(GATE[:, c], now(), ACT.Copy))
            act.wait_ge(s_evac, evac.now())
            for c in range(PLAIN_GATES):
                act.activation(GATE[:, c], GATE[:, c], ACT.Gelu_apprx_tanh).then_inc(s_gelu, gelu.up())
            for c in range(PLAIN_GATES, KD):
                used(lambda: act.activation(GATE[:, c], now(), ACT.Gelu_apprx_tanh))
            yr.at += KD
            out_tiles(KD)

        def angles(cos, sin):
            act.wait_ge(s_rot, rot.next())
            act.activation(sin, sin, ACT.Sin).then_inc(s_trig, trig.up())
            act.activation(cos, cos, ACT.Sin).then_inc(s_trig, trig.up())

        def ffn(l, last, before):
            if before in ANGLES:
                cos, _, s_in = ANGLES[before]
                act.dma_start(cos[:, :].bitcast(I32), a["positions"].broadcast_to([P, SEQ])).then_inc(s_in, 16)
            with loop(act, NF // 2, panels_per(4) + [(evac, 4), (ev, 4), (gelu, 2)]):
                for _ in range(2):
                    used(to_stage)
                    used(to_stage)
                    act.wait_ge(s_ev, ev.now(RING - 1))
                    act.activation(AG[:, :], AG[:, :], ACT.Gelu_apprx_tanh).then_inc(s_gelu, gelu.up())
            out_tiles(NF, ANGLES.get(before))
            lnorm(1, l, last)

        def mla():
            for m in range(KQ, KD):
                used(lambda: act.activation(LAT[:, m], now(), ACT.Copy))
            used(lambda: act.activation(KB[NOPE:QKH, 0], now(slice(NOPE, QKH)), ACT.Copy))

            def hi_part(m):
                act.wait_ge(s_hin, hin.next())
                act.activation(CNH[:, m], LAT[:, m], ACT.Copy).then_inc(s_hout, hout.up())
            used(lambda: act.activation(LAT[:, 0], now(), ACT.Copy))
            root()
            for m in range(KQ, KD):
                hi_part(m)
            for m in range(1, KQ):
                used(lambda: act.activation(LAT[:, m], now(), ACT.Copy))

            def v_tile(t, half):
                act.activation(VM[:, t, half * SEQ:(half + 1) * SEQ], now(), ACT.Copy).then_inc(s_evac, evac.up())
            root()
            hi_part(0)
            hi_part(1)
            act.wait_ge(s_panel, panel_c.next())
            v_tile(0, 0)
            v_tile(1, 0)
            hi_part(2)
            v_tile(2, 0)
            v_tile(3, 0)
            split()
            hi_part(3)
            hi_part(4)
            hi_part(5)
            act.wait_ge(s_panel, panel_c.next())
            for t in range(TT):
                v_tile(t, 1)
            split()

            def k_product(u):
                act.wait_ge(s_panel, panel_c.next())
                act.activation(KB[0:NOPE, u % 2], BANK[1][0:NOPE, :], ACT.Copy).then_inc(s_evac, evac.up())
                split()

            def q_product(u):
                act.wait_ge(s_part, part.next())
                act.activation(QB[:, u % 2], BANK[0][0:QKH, :], ACT.Copy, scale=MLA_SCALE).then_inc(s_evac, evac.up())

            def head(u, pair, more=True):
                for qt in QT_ORDER:
                    kv = (qt + 1) * P
                    act.wait_ge(s_max, mx.next())
                    act.activation(PB[:, qt, 0:kv], HEADB[qt][:, 0:kv], ACT.Exp,
                                   bias=NM[:, qt:qt + 1], accum_out=RSUM[:, qt:qt + 1]).then_inc(s_exp, exp_c.up())
                if more:
                    q_product(u + 1)
                for qt in QT_ORDER:
                    act.wait_ge(s_turn, turn.next())
                    act.activation(PT[:, 0:qt + 1, qt * P:(qt + 1) * P],
                                   HEADB[qt][:, 0:(qt + 1) * P].rearrange("p (k q) -> p k q", q=P), ACT.Copy).then_inc(s_unturn, unturn.up())
                if more:
                    k_product(u + 1)
                if u % 2 == 1:
                    act.wait_ge(s_o, o.next())
                    act.activation(OH[:, pair].rearrange("p a b -> p (a b)"), OB[:, :], ACT.Copy).then_inc(s_oh, oh.up())
            q_product(0)
            k_product(0)
            head(0, col(0))
            head(1, col(0))
            with loop(act, HEADS // 4 - 1, panels_per(4) + [(evac, 8), (part, 4), (mx, 16), (exp_c, 16), (turn, 16), (unturn, 16),
                                                           (o, 2), (oh, 2)]) as i:
                for u in range(4):
                    head(u, col(i * 2 + (1 + u // 2)))
            head(0, col(0))
            head(1, col(HEADS // 2 - 1), more=False)
            out_tiles(KD)

        def ret():
            n = 4 + 2 * EV
            with loop(act, RH, panels_per(n) + [(evac, n + EV), (ev, 4), (turn, EV), (unturn, EV), (yr, EV), (o, EV), (dec, 16),
                                                (step, 1), (var, 1), (std, 1), (bmean, 1), (hin, EV), (hout, EV), (sd, TT)]) as i:
                act.wait_ge(s_sd, sd.now())
                act.dma_start(DEC[:, :], a["ret_decay"][col(i)].rearrange("a p q -> (a p) q")).then_inc(s_dec, dec.up(16))
                for _ in range(4):
                    used(to_stage)
                act.wait_ge(s_y, yr.now())

                def place(j):
                    act.wait_ge(s_turn, turn.next())
                    act.activation(V[:, :, j * P:(j + 1) * P], TURN[:, :].rearrange("p (t f) -> p t f", t=TT), ACT.Copy).then_inc(s_unturn, unturn.up())
                for j in range(EV):
                    used(lambda: act.activation(R[:, j], now(), ACT.Copy))
                    if j:
                        place(j - 1)
                place(EV - 1)
                used(lambda: act.activation(R[:, EV], now(), ACT.Silu))
                for j in range(EV):
                    act.wait_ge(s_o, o.next())
                    act.activation(R[:, j], now(), ACT.Copy).then_inc(s_evac, evac.up())
                for j in range(1, EV - 1):
                    used(lambda: act.activation(R[:, EV + j], now(), ACT.Silu))
                root()
                bmean.up()
                used(lambda: act.activation(R[:, 2 * EV - 1], now(), ACT.Silu))
                for j in range(EV):
                    act.wait_ge(s_hin, hin.next())
                    act.activation(RYH[:, col(i * EV + j)].rearrange("p a b -> p (a b)"), R[:, j], ACT.Copy).then_inc(s_hout, hout.up())
                sd.at += TT
                yr.at += EV
            out_tiles(KR, paired=True)

        for kind, j, l in layers:
            if kind == "lru":
                lru(j)
            else:
                (mla if kind == "mla" else ret)()
            lnorm(0, l)
            ffn(l, l == depth - 1, layers[l + 1][0] if l < depth - 1 else None)
        act.wait_ge(s_store, 16 * KD // OUT_TILES)

    @block.vector
    def _(dve):
        evac, ev, step = Count(s_evac, RING), Count(s_ev, RING), Count(s_dve)
        res, xr, xh, x, sums = Count(s_res), Count(s_xr), Count(s_xh), Count(s_x), Count(s_sum)
        stat, mean, bmean, brstd = Count(s_stat), Count(s_mean), Count(s_bmean), Count(s_brstd)
        var, hin, hout = Count(s_var), Count(s_hin), Count(s_hout)
        gelu, g_c, u_c, iu, ta = Count(s_gelu), Count(s_g), Count(s_u), Count(s_iu), Count(s_ta)
        mul, sq, yr, rot, trig = Count(s_mul), Count(s_sq), Count(s_y), Count(s_rot), Count(s_trig)
        cn, kpe, q, sc, mx, exp_c = Count(s_cn), Count(s_kpe), Count(s_q), Count(s_sc), Count(s_max), Count(s_exp)
        prob, oh, ol, sd, dec = Count(s_prob), Count(s_oh), Count(s_ol, 1), Count(s_sd, 2), Count(s_dec)
        smean, cen = Count(s_smean), Count(s_cen)
        sizes = [PANELS[section] for kind, _, _ in layers for section in (kind, "ffn")]
        ends = [sum(sizes[:n + 1]) for n in range(len(sizes))]
        staged = [0]
        dve.sem_inc(s_evac, RING)
        dve.sem_inc(s_ev, RING)
        dve.sem_inc(s_ol, 1)
        dve.sem_inc(s_sd, 2)

        def par(c):
            return PAR[:, col(c)]

        def next_stage():
            s = staged[0] % RING
            staged[0] += 1
            return s

        dve.memset(ST[:, :, 0:PAD], 0.0).then_inc(s_dve, step.up())
        dve.wait_ge(s_dve, step.now())
        def x_lo(m):
            dve.wait_ge(s_xh, xh.next())
            dve.tensor_tensor(XL[:, m], R[:, m], XH[:, m].bitcast(F32), ALU.subtract).then_inc(s_x, x.up())
            dve.wait_ge(s_x, x.now())
        for m in range(KD):
            dve.wait_ge(s_turn, m + 1)
            dve.tensor_copy(R[:, m], BANK[m % RING][:, :]).then_inc(s_evac, evac.up())
            dve.wait_ge(s_evac, evac.now())
            if m:
                x_lo(m - 1)
        x_lo(KD - 1)

        def square(kind, tile, done):
            dve.tensor_tensor(SUMS[kind][2], tile, tile, ALU.mult).then_inc(done.sem, done.up())
            dve.wait_ge(done.sem, done.now())

        def add_sums(kind, tile):
            s1, s2, t = SUMS[kind]
            dve.tensor_tensor(s1, s1, tile, ALU.add).then_inc(s_dve, step.up())
            dve.wait_ge(s_dve, step.now())
            square(kind, tile, step)
            dve.tensor_tensor(s2, s2, t, ALU.add).then_inc(s_sum, sums.up())
            dve.wait_ge(s_sum, sums.now())

        def clear_sums(kind):
            dve.memset(SUMS[kind][0], 0.0).then_inc(s_dve, step.up())
            dve.wait_ge(s_dve, step.now())
            dve.memset(SUMS[kind][1], 0.0).then_inc(s_dve, step.up())
            dve.wait_ge(s_dve, step.now())

        def inverse_std(n, parts=1):
            dve.wait_ge(s_stat, stat.next())
            if parts == 1:
                dve.tensor_scalar(MEANS, TURN[:, 0:2 * TT], 1.0 / n, None, ALU.mult).then_inc(s_mean, mean.up())
            else:
                dve.tensor_copy(MEANS, TURN[:, 0:2 * TT]).then_inc(s_dve, step.up())
                dve.wait_ge(s_dve, step.now())
                dve.wait_ge(s_stat, stat.next())
                dve.tensor_tensor(MEANS, MEANS, SUMB[0][:, 0:2 * TT], ALU.add).then_inc(s_mean, mean.up())
            dve.wait_ge(s_mean, mean.now())
            dve.tensor_tensor(TMP4, MEAN, MEAN, ALU.mult).then_inc(s_dve, step.up())
            dve.wait_ge(s_dve, step.now())
            dve.scalar_tensor_tensor(TMP4, SQUARE, LN_EPS, TMP4, ALU.add, ALU.subtract).then_inc(s_dve, step.up())
            dve.wait_ge(s_dve, step.now())
            dve.tensor_scalar(TMP4, TMP4, LN_EPS, None, ALU.max).then_inc(s_dve, step.up())
            dve.wait_ge(s_dve, step.now())
            dve.reciprocal(VINV, TMP4).then_inc(s_var, var.up())
            dve.wait_ge(s_var, var.now())

        def inverse_rms(n):
            dve.wait_ge(s_stat, stat.next())
            dve.tensor_scalar(TMP4, TURN[:, 0:TT], 1.0 / n, RMS_EPS, ALU.mult, ALU.add).then_inc(s_dve, step.up())
            dve.wait_ge(s_dve, step.now())
            dve.reciprocal(VINV, TMP4).then_inc(s_var, var.up())
            dve.wait_ge(s_var, var.now())
            dve.wait_ge(s_brstd, brstd.next())

        def residual(kind):
            clear_sums(kind)
            for m in range(KD):
                if m < KD - 1:
                    dve.wait_ge(s_evac, evac.next())
                    mix, done = stage(next_stage()), ev
                else:
                    dve.wait_ge(s_panel, ends.pop(0))
                    mix, done = BANK[(evac.at - RING) % RING][:, :], evac
                if kind in ("mla", "ret"):
                    dve.scalar_tensor_tensor(R[:, m], XH[:, m].bitcast(F32), ALPHA, mix, ALU.mult, ALU.add).then_inc(s_dve, step.up())
                    dve.wait_ge(s_dve, step.now())
                    dve.scalar_tensor_tensor(R[:, m], XL[:, m].bitcast(F32), ALPHA, R[:, m], ALU.mult, ALU.add).then_inc(done.sem, done.up())
                else:
                    dve.scalar_tensor_tensor(R[:, m], R[:, m], ALPHA, mix, ALU.mult, ALU.add).then_inc(done.sem, done.up())
                dve.wait_ge(done.sem, done.now())
                if m < KD - 1:
                    add_sums(kind, R[:, m])
                else:
                    dve.sem_inc(s_sum, 1)
                    sums.up()
                    square(kind, R[:, m], sums)

        def norm(which, l, last=False):
            gain = PC_LN + 2 * which * DEPTH * KD + l * KD
            shift = gain + DEPTH * KD
            inverse_std(D, parts=2)
            bmean.up()
            dve.wait_ge(s_smean, smean.next())
            dve.tensor_tensor(R[:, 0], R[:, 0], stage(0), ALU.subtract).then_inc(s_dve, step.up())
            dve.wait_ge(s_dve, step.now())
            dve.wait_ge(s_brstd, brstd.next())
            for m in range(KD):
                if m:
                    dve.wait_ge(s_cen, cen.next())
                dve.tensor_tensor(stage(2 + m % 2), R[:, m], SUMB[1][:, :], ALU.mult).then_inc(s_res, res.up())
                dve.wait_ge(s_res, res.now())
                if m > 1 and not last:
                    x_lo(m - 1)
                dve.tensor_scalar(R[:, m], stage(2 + m % 2), par(gain + m), par(shift + m), ALU.mult, ALU.add).then_inc(s_xr, xr.up())
                dve.wait_ge(s_xr, xr.now())
                if m == 0 and not last:
                    x_lo(0)
            if not last:
                x_lo(KD - 1)

        def conv(dst, s, taps, w, b):
            dve.tensor_scalar(dst, stage(s), par(w(0)), par(b), ALU.mult, ALU.add).then_inc(s_dve, step.up())
            dve.wait_ge(s_dve, step.now())
            for lag in range(1, taps):
                done = ev if lag == taps - 1 else step
                dve.scalar_tensor_tensor(dst, stage(s, lag), par(w(lag)), dst, ALU.mult, ALU.add).then_inc(done.sem, done.up())
                dve.wait_ge(done.sem, done.now())

        def decay_rates():
            dve.wait_ge(s_evac, evac.now(3 + len(ROW_GROUPS)))
            dve.wait_ge(s_lam, 1)
            dve.tensor_scalar(LAMT[:, 0], LAM[:, :, :], 2.0, None, ALU.add).then_inc(s_dve, step.up())
            dve.wait_ge(s_dve, step.now())
            dve.reciprocal(LAMT[:, 0], LAMT[:, 0]).then_inc(s_dve, step.up())
            dve.wait_ge(s_dve, step.now())
            dve.tensor_tensor(LAMT[:, 0], LAMT[:, 0], LAM[:, :, :], ALU.mult).then_inc(s_dve, step.up())
            dve.wait_ge(s_dve, step.now())
            dve.tensor_tensor(LAMT[:, 1], LAMT[:, 0], LAMT[:, 0], ALU.mult).then_inc(s_dve, step.up())
            dve.wait_ge(s_dve, step.now())
            dve.tensor_scalar(LAMT[:, 2], LAMT[:, 1], 1.0 / 19, None, ALU.mult).then_inc(s_dve, step.up())
            dve.wait_ge(s_dve, step.now())
            for k in (17, 15, 13, 11, 9, 7, 5, 3):
                dve.scalar_tensor_tensor(LAMT[:, 2], LAMT[:, 2], 1.0 / k, LAMT[:, 1], ALU.add, ALU.mult).then_inc(s_dve, step.up())
                dve.wait_ge(s_dve, step.now())
            dve.scalar_tensor_tensor(LAMT[:, 2], LAMT[:, 2], 1.0, LAMT[:, 0], ALU.add, ALU.mult).then_inc(s_dve, step.up())
            dve.wait_ge(s_dve, step.now())
            for j in range(2):
                lam, rate = PC_LRU + j * LRU_COLS + 7 * KD, PC_RATE + j * 2 * KD
                dve.tensor_scalar(LAMT[:, 0, j], PAR[:, lam:lam + KD], -1.0, 0.0, ALU.mult, ALU.max).then_inc(s_dve, step.up())
                dve.wait_ge(s_dve, step.now())
                dve.scalar_tensor_tensor(LAMT[:, 0, j], LAMT[:, 2, j], 2.0, LAMT[:, 0, j], ALU.mult, ALU.add).then_inc(s_dve, step.up())
                dve.wait_ge(s_dve, step.now())
                dve.tensor_scalar(PAR[:, rate:rate + KD], LAMT[:, 0, j], LRU_C, None, ALU.mult).then_inc(s_dve, step.up())
                dve.wait_ge(s_dve, step.now())
                dve.tensor_scalar(PAR[:, rate + KD:rate + 2 * KD], LAMT[:, 0, j], -LRU_C, None, ALU.mult).then_inc(s_dve, step.up())
                dve.wait_ge(s_dve, step.now())

        def lru(j):
            base = PC_LRU + j * LRU_COLS
            if j == 0:
                decay_rates()
            for m in range(KD):
                dve.wait_ge(s_evac, evac.next() + (len(ROW_GROUPS) if j == 0 else 0))
                conv(U[:, m], next_stage(), 4, lambda lag: base + (3 - lag) * KD + m, base + 4 * KD + m)
                dve.tensor_copy(UH[:, m], U[:, m]).then_inc(s_dve, step.up())
                dve.wait_ge(s_dve, step.now())
                dve.tensor_tensor(UL[:, m], U[:, m], UH[:, m].bitcast(F32), ALU.subtract).then_inc(s_u, u_c.up())
                dve.wait_ge(s_u, u_c.now())
            if j == 0:
                evac.at += len(ROW_GROUPS)
            for g in range(LRU_BLOCKS):
                dve.wait_ge(s_evac, evac.next(4))
                for c in (2 * g, 2 * g + 1):
                    dve.tensor_tensor(U[:, c], U[:, c], I[:, c], ALU.mult).then_inc(s_iu, iu.up())
                    dve.wait_ge(s_iu, iu.now())
            for c in range(KD):
                dve.wait_ge(s_ta, ta.next())
                dve.tensor_tensor(stage(3), A[:, c], A[:, c], ALU.mult).then_inc(s_dve, step.up())
                dve.wait_ge(s_dve, step.now())
                dve.scalar_tensor_tensor(I[:, c], stage(3), 1.0, I[:, c], ALU.add, ALU.mult).then_inc(s_mul, mul.up())
                dve.wait_ge(s_mul, mul.now())
            for c in range(KD):
                dve.wait_ge(s_sq, sq.next())
                dve.tensor_tensor(I[:, c], I[:, c], U[:, c], ALU.mult).then_inc(s_dve, step.up())
                dve.wait_ge(s_dve, step.now())
                dve.tensor_tensor_scan(U[:, c], A[:, c], I[:, c], 0.0, ALU.mult, ALU.add).then_inc(s_dve, step.up())
                dve.wait_ge(s_dve, step.now())
                evac.up()
                if c < PLAIN_GATES:
                    dve.wait_ge(s_gelu, gelu.next())
                else:
                    dve.wait_ge(s_evac, evac.now())
                dve.tensor_tensor(U[:, c], U[:, c], GATE[:, c], ALU.mult).then_inc(s_dve, step.up())
                dve.wait_ge(s_dve, step.now())
                dve.tensor_copy(YH[:, c], U[:, c]).then_inc(s_dve, step.up())
                dve.wait_ge(s_dve, step.now())
                dve.tensor_tensor(YL[:, c], U[:, c], YH[:, c].bitcast(F32), ALU.subtract).then_inc(s_y, yr.up())
                dve.wait_ge(s_y, yr.now())
            residual("lru")

        def ffn(l, last, before):
            base = PC_FFN + l * FFN_COLS
            with loop(dve, NF // 2, [(evac, 4), (ev, 4), (gelu, 2), (g_c, 2), (step, 12)]) as i:
                for u in range(2):
                    f = i * 2 + u
                    for half, dst in enumerate((AG, AU)):
                        dve.wait_ge(s_evac, evac.next())
                        conv(dst[:, :], next_stage(), 3, lambda lag: f + (base + (2 - lag) * 2 * NF + half * NF),
                             f + (base + 6 * NF + half * NF))
                    dve.wait_ge(s_gelu, gelu.next())
                    dve.tensor_tensor(AU[:, :], AU[:, :], AG[:, :], ALU.mult).then_inc(s_dve, step.up())
                    dve.wait_ge(s_dve, step.now())
                    gh, gl = (t[:, col(f)].rearrange("p a b -> p (a b)") for t in (GH, GL))
                    dve.tensor_copy(gh, AU[:, :]).then_inc(s_dve, step.up())
                    dve.wait_ge(s_dve, step.now())
                    dve.tensor_tensor(gl, AU[:, :], gh.bitcast(F32), ALU.subtract).then_inc(s_g, g_c.up())
                    dve.wait_ge(s_g, g_c.now())
            if before in ANGLES:
                cos, freq, s_in = ANGLES[before]
                angles(cos[:, :].bitcast(I32), s_in, freq, cos[:, :], OB[:, :], AT[:, :])
            residual("ffn")
            norm(1, l, last)

        def angles(pos, s_in, freq, cos, sin, tmp):
            dve.wait_ge(s_in, 16)
            dve.tensor_copy(cos, pos).then_inc(s_dve, step.up())
            dve.wait_ge(s_dve, step.now())
            dve.tensor_scalar(cos, cos, freq, None, ALU.mult).then_inc(s_dve, step.up())
            dve.wait_ge(s_dve, step.now())
            for dst, turn, done in ((sin, 0.0, step), (cos, 0.25, rot)):
                dve.tensor_scalar(tmp, cos, 1 / TWO_PI, turn, ALU.mult, ALU.add).then_inc(s_dve, step.up())
                dve.wait_ge(s_dve, step.now())
                dve.tensor_scalar(tmp, tmp, ROUND, None, ALU.add).then_inc(s_dve, step.up())
                dve.wait_ge(s_dve, step.now())
                dve.tensor_scalar(tmp, tmp, ROUND, None, ALU.subtract).then_inc(s_dve, step.up())
                dve.wait_ge(s_dve, step.now())
                dve.scalar_tensor_tensor(dst, tmp, -PI2_A, cos, ALU.mult, ALU.add).then_inc(s_dve, step.up())
                dve.wait_ge(s_dve, step.now())
                dve.scalar_tensor_tensor(dst, tmp, -PI2_B, dst, ALU.mult, ALU.add).then_inc(s_dve, step.up())
                dve.wait_ge(s_dve, step.now())
                dve.scalar_tensor_tensor(dst, tmp, -PI2_C, dst, ALU.mult, ALU.add).then_inc(s_dve, step.up())
                dve.wait_ge(s_dve, step.now())
                dve.tensor_scalar(dst, dst, turn * TWO_PI, PI_CLAMP, ALU.add, ALU.min).then_inc(s_dve, step.up())
                dve.wait_ge(s_dve, step.now())
                dve.tensor_scalar(dst, dst, -PI_CLAMP, None, ALU.max).then_inc(done.sem, done.up())
                dve.wait_ge(done.sem, done.now())
            dve.wait_ge(s_trig, trig.next(2))

        rows = slice(NOPE, QKH)
        swap = [(r + ROPE // 2) % ROPE for r in range(ROPE)]

        def mla_rope(t, done):
            dve.sem_inc(s_go, 1)
            dve.stream_shuffle(ROT[rows, :], t, swap).then_inc(s_dve, step.up())
            dve.wait_ge(s_dve, step.now())
            dve.tensor_tensor(ROT[rows, :], ROT[rows, :], MSIN[rows, :], ALU.mult).then_inc(s_dve, step.up())
            dve.wait_ge(s_dve, step.now())
            dve.tensor_tensor(t, t, MCOS[rows, :], ALU.mult).then_inc(s_dve, step.up())
            dve.wait_ge(s_dve, step.now())
            dve.tensor_tensor(t, t, ROT[rows, :], ALU.add).then_inc(done.sem, done.up())
            dve.wait_ge(done.sem, done.now())

        def mla():
            dve.memset(PT[:, 1], 0.0).then_inc(s_dve, step.up())
            dve.wait_ge(s_dve, step.now())
            dve.memset(PT[:, 2], 0.0).then_inc(s_dve, step.up())
            dve.wait_ge(s_dve, step.now())

            def add_square(m):
                dve.wait_ge(s_evac, evac.next())
                acc = PT[:, 2] if m < KQ else PT[:, 1]
                dve.tensor_tensor(PT[:, 0], LAT[:, m], LAT[:, m], ALU.mult).then_inc(s_dve, step.up())
                dve.wait_ge(s_dve, step.now())
                dve.tensor_tensor(acc, acc, PT[:, 0], ALU.add).then_inc(s_sum, sums.up())
                dve.wait_ge(s_sum, sums.now())

            def lo(m):
                dve.wait_ge(s_hout, hout.next())
                dve.tensor_tensor(CNL[:, m], LAT[:, m], CNH[:, m].bitcast(F32), ALU.subtract).then_inc(s_cn, cn.up())
                dve.wait_ge(s_cn, cn.now())

            def latents(tiles):
                for m in tiles:
                    dve.scalar_tensor_tensor(LAT[:, m], LAT[:, m], par(PC_MLA + m), SUMB[1][:, :], ALU.mult, ALU.mult).then_inc(s_hin, hin.up())
                    dve.wait_ge(s_hin, hin.now())
                    if m != tiles[0]:
                        lo(m - 1)
                lo(tiles[-1])
            for m in range(KQ, KD):
                add_square(m)
            inverse_rms(KV_LORA)
            latents(range(KQ, KD))
            dve.tensor_scalar(MSIN[:, :], OB[:, :], FREQ[:, 2:3], None, ALU.mult).then_inc(s_dve, step.up())
            dve.wait_ge(s_dve, step.now())
            dve.wait_ge(s_evac, evac.next())
            mla_rope(KB[rows, 0], step)
            dve.tensor_copy(KB[rows, 1], KB[rows, 0]).then_inc(s_kpe, kpe.up())
            dve.wait_ge(s_kpe, kpe.now())
            for m in range(KQ):
                add_square(m)
            inverse_rms(Q_LORA)
            latents(range(KQ))
            evac.at += 2 * TT

            def new_q(h, i=0):
                dve.wait_ge(s_evac, evac.next())
                mla_rope(QB[rows, h % 2], q)
                evac.at += 1
                dve.tensor_copy(VB[:, h % 2], VM[:, :, col(i * (4 * VH) + h * VH, VH)]).then_inc(s_dve, step.up())
                dve.wait_ge(s_dve, step.now())

            def o_lo(h, i=0):
                dve.wait_ge(s_oh, oh.next())
                hi_o, lo_o = (t[:, col(i * 2 + h // 2)].rearrange("p a b -> p (a b)") for t in (OH, OL))
                dve.tensor_tensor(lo_o, OB[:, :], hi_o.bitcast(F32), ALU.subtract).then_inc(s_ol, ol.up())
                dve.wait_ge(s_ol, ol.now())

            def head(h, i=0):
                for n in range(TT + 1):
                    if n < TT:
                        qt = QT_ORDER[n]
                        dve.wait_ge(s_sc, sc.next())
                        dve.tensor_reduce(NM[:, qt:qt + 1], HEADB[qt][:, 0:(qt + 1) * P], AX.X, ALU.max, negate=True).then_inc(s_max, mx.up())
                        dve.wait_ge(s_max, mx.now())
                    if n == 1 and h % 2 == 0 and h:
                        o_lo(h - 1, i)
                    if n:
                        qt = QT_ORDER[n - 1]
                        dve.wait_ge(s_exp, exp_c.next())
                        dve.reciprocal(RINV[:, qt:qt + 1], RSUM[:, qt:qt + 1]).then_inc(s_dve, step.up())
                        dve.wait_ge(s_dve, step.now())
                        p = PB[:, qt, 0:(qt + 1) * P]
                        dve.tensor_scalar(p, p, RINV[:, qt:qt + 1], None, ALU.mult).then_inc(s_prob, prob.up())
                        dve.wait_ge(s_prob, prob.now())
                if h < HEADS - 1:
                    new_q(h + 1, i)
            dve.wait_ge(s_evac, evac.now())
            new_q(0)
            head(0)
            head(1)
            with loop(dve, HEADS // 4 - 1, [(evac, 8), (q, 4), (sc, 16), (mx, 16), (exp_c, 16), (prob, 16), (oh, 2), (ol, 2),
                                            (step, 4 * (3 + 1 + 4))]) as i:
                for u in range(4):
                    head(2 + u, i)
            head(HEADS - 2)
            head(HEADS - 1)
            o_lo(HEADS - 1)
            residual("mla")

        def ret():
            n = 4 + 2 * EV
            with loop(dve, RH, [(evac, n + EV), (ev, 4), (q, 2), (dec, 16), (sc, TT), (sd, TT), (sums, EV), (stat, 1), (mean, 1),
                                (bmean, 1), (var, 1), (brstd, 1), (hin, EV), (hout, EV), (yr, EV),
                                (step, 2 * 3 + 2 + 2 * EV + 3 + 2 * EV)]) as i:
                for t in (QT, KT):
                    dve.wait_ge(s_evac, evac.next(2))
                    s1, s2 = next_stage(), next_stage()
                    dve.tensor_tensor(t[:, 0], stage(s1), RCOS[:, :], ALU.mult).then_inc(s_dve, step.up())
                    dve.wait_ge(s_dve, step.now())
                    dve.tensor_tensor(RTMP[:, :], stage(s2), RSIN[:, :], ALU.mult).then_inc(s_dve, step.up())
                    dve.wait_ge(s_dve, step.now())
                    dve.tensor_tensor(t[:, 0], t[:, 0], RTMP[:, :], ALU.subtract).then_inc(s_dve, step.up())
                    dve.wait_ge(s_dve, step.now())
                    dve.tensor_tensor(t[:, 1], stage(s1), RSIN[:, :], ALU.mult).then_inc(s_ev, ev.up())
                    dve.wait_ge(s_ev, ev.now())
                    dve.tensor_tensor(RTMP[:, :], stage(s2), RCOS[:, :], ALU.mult).then_inc(s_ev, ev.up())
                    dve.wait_ge(s_ev, ev.now())
                    dve.tensor_tensor(t[:, 1], t[:, 1], RTMP[:, :], ALU.add).then_inc(s_q, q.up())
                    dve.wait_ge(s_q, q.now())
                dve.wait_ge(s_dec, dec.next(16))
                for kt in range(TT):
                    dve.wait_ge(s_sc, sc.next())
                    w = SEQ - kt * P
                    dve.tensor_tensor(SD[:, kt, kt * P:SEQ], SUMB[kt % 2][:, 0:w], DEC[:, 0:w], ALU.mult).then_inc(s_sd, sd.up())
                    dve.wait_ge(s_sd, sd.now())
                evac.at += EV + 1
                clear_sums("ret")
                for j in range(EV):
                    dve.wait_ge(s_evac, evac.next())
                    add_sums("ret", R[:, j])
                inverse_std(RV)
                dve.wait_ge(s_bmean, bmean.next())
                dve.wait_ge(s_brstd, brstd.next())
                dve.wait_ge(s_evac, evac.next(EV - 1))

                def lo(j):
                    dve.wait_ge(s_hout, hout.next())
                    y_hi, y_lo = (t[:, col(i * EV + j)].rearrange("p a b -> p (a b)") for t in (RYH, RYL))
                    dve.tensor_tensor(y_lo, R[:, j], y_hi.bitcast(F32), ALU.subtract).then_inc(s_y, yr.up())
                    dve.wait_ge(s_y, yr.now())
                for j in range(EV):
                    dve.tensor_tensor(R[:, j], R[:, j], SUMB[0][:, :], ALU.subtract).then_inc(s_dve, step.up())
                    dve.wait_ge(s_dve, step.now())
                    dve.tensor_tensor(R[:, j], R[:, j], SUMB[1][:, :], ALU.mult).then_inc(s_dve, step.up())
                    dve.wait_ge(s_dve, step.now())
                    dve.scalar_tensor_tensor(R[:, j], R[:, j], par(i * EV + (PC_RET + j)), R[:, EV + j], ALU.mult, ALU.mult).then_inc(s_hin, hin.up())
                    dve.wait_ge(s_hin, hin.now())
                    if j:
                        lo(j - 1)
                lo(EV - 1)
            residual("ret")

        for kind, j, l in layers:
            if kind == "lru":
                lru(j)
            else:
                (mla if kind == "mla" else ret)()
            norm(0, l)
            ffn(l, l == depth - 1, layers[l + 1][0] if l < depth - 1 else None)


def constants():
    import numpy as np

    def freq(d):
        return (10000.0 ** (-np.arange(0, d, 2, dtype=np.float64) / d)).astype(np.float32)
    f = np.zeros((P, 4), np.float32)
    f[:, 0] = np.tile(freq(ROPE), 2 * P // ROPE)
    f[:, 1] = freq(RQK)
    f[:, 2] = np.tile(np.repeat([-1.0, 1.0], ROPE // 2), P // ROPE)
    k, q = np.arange(P)[:, None], np.arange(SEQ)[None, :]
    log_gamma = np.log1p(-np.exp2(-5.0 - np.arange(RH, dtype=np.float64)))
    decay = np.exp(log_gamma[:, None, None] * np.abs(q - k)) * (k // CHUNK <= q // CHUNK) * float(RQK) ** -0.5
    return {"rope_freq": f, "ret_decay": decay.astype(np.float32)}


def kernel(**inputs):
    import numpy as np
    import concourse.bacc as bacc
    from concourse.bass_utils import run_bass_kernel_spmd

    nc = bacc.Bacc("TRN2", target_bir_lowering=False, num_devices=1)
    arrays = {n: np.ascontiguousarray(v) for n, v in {**inputs, **constants()}.items()}
    aps = {n: nc.dram_tensor(n, v.shape, mybir.dt.from_np(v.dtype), kind="ExternalInput").ap() for n, v in arrays.items()}
    out = nc.dram_tensor("out", (1, SEQ, D), F32, kind="ExternalOutput").ap()
    build(nc, aps, out)
    r = run_bass_kernel_spmd(nc, [arrays], core_ids=[0])
    return r.results[0]["out"]
```
